# Optimizing a Trainium2 kernel written in Bass

```python
import numpy as np
import jax
import jax.numpy as jnp
from jax import lax

D_MODEL = 1024
BATCH = 1
SEQ = 256
DEPTH = 2

HEAD_DIM = 64
QBLOCK = 128
ROPE_THETA = 10000.0
PLE_DIM = 256
LN_EPS = 1e-5
RMS_EPS = 1e-6
NEG = -1e30
BIG = 1e30

A_HEADS = 8
IDX_HEADS = 8
IDX_DIM = 64
DSA_TOPK_MAX = 256

B_HEADS = 8
CMP_LEN = 32
CMP_STRIDE = 16
SEL_LEN = 32
SEL_BLOCKS_MAX = 8
WINDOW = 512

C_HEADS = 16
FORGET_BIAS_INIT = 3.0

N_EXPERTS = 64
TOP_K = 8
N_GROUPS = 8
TOPK_GROUPS = 4
D_EXPERT = 256
ROUTED_SCALE = 2.5
EXPERT_BLOCK = 256

N_EVEN = (DEPTH + 1) // 2
N_ODD = DEPTH // 2
ALPHA = (2.0 * DEPTH) ** 0.25
BETA = (8.0 * DEPTH) ** -0.25

MIX_A = A_HEADS * HEAD_DIM
MIX_B = B_HEADS * HEAD_DIM
MIX_EVEN = MIX_A + MIX_B
MIX_ODD = C_HEADS * HEAD_DIM
EVEN_SPLITS = (MIX_A, HEAD_DIM, HEAD_DIM, IDX_HEADS * IDX_DIM, IDX_DIM, IDX_HEADS, MIX_B, 6 * HEAD_DIM, 3 * B_HEADS)
EVEN_COLS = sum(EVEN_SPLITS)
ODD_SPLITS = (MIX_ODD, MIX_ODD, MIX_ODD, C_HEADS)
ODD_COLS = sum(ODD_SPLITS)

kernel_name = 'hybrid_dsa_nsa_fox_moe_trunk'

def split_cols(h, sizes):
    cuts = [int(c) for c in np.cumsum(sizes)[:-1]]
    return jnp.split(h, cuts, axis=-1)

def rope_tables(pos):
    inv = 1.0 / (ROPE_THETA ** (np.arange(0, HEAD_DIM, 2, dtype=np.float32) / HEAD_DIM))
    ang = pos.astype(jnp.float32)[:, None] * jnp.asarray(inv, dtype=jnp.float32)[None, :]
    return jnp.cos(ang), jnp.sin(ang)

def apply_rope(x, cos, sin):
    if x.ndim == 4:
        cos = cos[:, None, :]
        sin = sin[:, None, :]
    half = x.shape[-1] // 2
    xf = x.astype(jnp.float32)
    x1, x2 = xf[..., :half], xf[..., half:]
    return jnp.concatenate([x1 * cos - x2 * sin, x2 * cos + x1 * sin], axis=-1).astype(x.dtype)

def layer_norm(x, g, b):
    xf = x.astype(jnp.float32)
    mu = jnp.mean(xf, axis=-1, keepdims=True)
    var = jnp.mean(jnp.square(xf - mu), axis=-1, keepdims=True)
    return ((xf - mu) * lax.rsqrt(var + LN_EPS)).astype(x.dtype) * g + b

def rms_norm(x, g):
    xf = x.astype(jnp.float32)
    return (xf * lax.rsqrt(jnp.mean(jnp.square(xf), axis=-1, keepdims=True) + RMS_EPS)).astype(x.dtype) * g

def masked_softmax(s, valid):
    p = jax.nn.softmax(jnp.where(valid, s, NEG), axis=-1)
    return jnp.where(valid, p, 0.0)

def to_blocks(a):
    b, s = a.shape[:2]
    return jnp.swapaxes(a.reshape((b, s // QBLOCK, QBLOCK) + a.shape[2:]), 0, 1)

def from_blocks(a):
    nb, b = a.shape[:2]
    return jnp.swapaxes(a, 0, 1).reshape((b, nb * QBLOCK) + a.shape[3:])

def dsa_attention(q, k, v, q_idx, k_idx, w_idx, pos):
    bsz, s_len = q.shape[:2]
    k_sel = min(DSA_TOPK_MAX, s_len // 4)
    b_idx = jnp.arange(bsz)[:, None, None]
    idx_scale = (IDX_HEADS * IDX_DIM) ** -0.5
    scale = HEAD_DIM ** -0.5

    def block(args):
        qb, qib, wb, t = args
        logits = jnp.einsum('bqhd,bkd->bqhk', qib, k_idx, preferred_element_type=jnp.float32)
        score = jnp.einsum('bqhk,bqh->bqk', jax.nn.relu(logits), wb.astype(jnp.float32)) * idx_scale
        causal = pos[None, :] <= t[:, None]
        score = jnp.where(causal[None], score, NEG)
        _, sel = lax.top_k(score, k_sel)
        ks = k[b_idx, sel]
        vs = v[b_idx, sel]
        valid = (sel <= t[None, :, None])[:, :, None, :]
        s = jnp.einsum('bqhd,bqkd->bqhk', qb, ks, preferred_element_type=jnp.float32) * scale
        pr = masked_softmax(s, valid)
        return jnp.einsum('bqhk,bqkd->bqhd', pr.astype(vs.dtype), vs)

    out = lax.map(block, (to_blocks(q), to_blocks(q_idx), to_blocks(w_idx), pos.reshape(-1, QBLOCK)))
    return from_blocks(out)

def nsa_attention(q, k_cmp, v_cmp, k_slc, v_slc, k_win, v_win, gate_logits,
                  pos_k, w1_k, w2_k, pos_v, w1_v, w2_v, pos, cos, sin):
    bsz, s_len = q.shape[:2]
    n_cmp = (s_len - CMP_LEN) // CMP_STRIDE + 1
    c_start = np.arange(n_cmp) * CMP_STRIDE
    cidx = c_start[:, None] + np.arange(CMP_LEN)[None, :]
    c_last = c_start + CMP_LEN - 1

    def compress(kv, pe, w1, w2):
        blk = (kv[:, cidx] + pe).reshape(bsz, n_cmp, CMP_LEN * HEAD_DIM)
        return jax.nn.silu(blk @ w1) @ w2

    kc = apply_rope(compress(k_cmp, pos_k, w1_k, w2_k), cos[c_last], sin[c_last])
    vc = compress(v_cmp, pos_v, w1_v, w2_v)
    n_sb = s_len // SEL_LEN
    n_sel = min(SEL_BLOCKS_MAX, n_sb)
    s_start = np.arange(n_sb) * SEL_LEN
    ov = np.clip(np.minimum(c_start[:, None] + CMP_LEN, s_start[None, :] + SEL_LEN)
                 - np.maximum(c_start[:, None], s_start[None, :]), 0, None)
    overlap = jnp.asarray(ov / CMP_LEN, dtype=jnp.float32)
    kw_pad = jnp.pad(k_win, ((0, 0), (WINDOW, 0), (0, 0)))
    vw_pad = jnp.pad(v_win, ((0, 0), (WINDOW, 0), (0, 0)))
    b_idx = jnp.arange(bsz)[:, None, None]
    c_last_j = jnp.asarray(c_last)
    s_start_j = jnp.asarray(s_start)
    blk_ids = jnp.arange(n_sb)
    scale = HEAD_DIM ** -0.5

    def block(args):
        qb, gb, t = args
        s_c = jnp.einsum('bqhd,bcd->bqhc', qb, kc, preferred_element_type=jnp.float32) * scale
        valid_c = (c_last_j[None, :] <= t[:, None])[None, :, None, :]
        p_c = masked_softmax(s_c, valid_c)
        o_c = jnp.einsum('bqhc,bcd->bqhd', p_c.astype(vc.dtype), vc, preferred_element_type=jnp.float32)
        imp = jnp.einsum('bqhc,cj->bqj', p_c, overlap)
        cur = t // SEL_LEN
        forced = (blk_ids[None, :] == 0) | (blk_ids[None, :] == cur[:, None]) | (blk_ids[None, :] == cur[:, None] - 1)
        future = s_start_j[None, :] > t[:, None]
        imp = jnp.where(forced[None], BIG, jnp.where(future[None], NEG, imp))
        _, sb = lax.top_k(imp, n_sel)
        tok = (sb[..., None] * SEL_LEN + jnp.arange(SEL_LEN)).reshape(bsz, QBLOCK, n_sel * SEL_LEN)
        ks = k_slc[b_idx, tok]
        vs = v_slc[b_idx, tok]
        valid_s = (tok <= t[None, :, None])[:, :, None, :]
        s_s = jnp.einsum('bqhd,bqkd->bqhk', qb, ks, preferred_element_type=jnp.float32) * scale
        o_s = jnp.einsum('bqhk,bqkd->bqhd', masked_softmax(s_s, valid_s).astype(vs.dtype), vs,
                         preferred_element_type=jnp.float32)
        q0 = t[0]
        kw = lax.dynamic_slice_in_dim(kw_pad, q0, WINDOW + QBLOCK, axis=1)
        vw = lax.dynamic_slice_in_dim(vw_pad, q0, WINDOW + QBLOCK, axis=1)
        kpos = q0 - WINDOW + jnp.arange(WINDOW + QBLOCK)
        valid_w = ((kpos[None, :] <= t[:, None]) & (kpos[None, :] > t[:, None] - WINDOW)
                   & (kpos[None, :] >= 0))[None, :, None, :]
        s_w = jnp.einsum('bqhd,bkd->bqhk', qb, kw, preferred_element_type=jnp.float32) * scale
        o_w = jnp.einsum('bqhk,bkd->bqhd', masked_softmax(s_w, valid_w).astype(vw.dtype), vw,
                         preferred_element_type=jnp.float32)
        g = jax.nn.sigmoid(gb.astype(jnp.float32))
        o = g[..., 0:1] * o_c + g[..., 1:2] * o_s + g[..., 2:3] * o_w
        return o.astype(qb.dtype)

    out = lax.map(block, (to_blocks(q), to_blocks(gate_logits), pos.reshape(-1, QBLOCK)))
    return from_blocks(out)

def fox_attention(q, k, v, log_f, pos):
    dcum = jnp.cumsum(log_f, axis=1)
    d_keys = jnp.transpose(dcum, (0, 2, 1))
    scale = HEAD_DIM ** -0.5

    def block(args):
        qb, db, t = args
        s = jnp.einsum('bqhd,bkhd->bhqk', qb, k, preferred_element_type=jnp.float32) * scale
        s = s + jnp.transpose(db, (0, 2, 1))[..., None] - d_keys[:, :, None, :]
        valid = (pos[None, :] <= t[:, None])[None, None]
        p = masked_softmax(s, valid)
        return jnp.einsum('bhqk,bkhd->bqhd', p.astype(v.dtype), v)

    out = lax.map(block, (to_blocks(q), to_blocks(dcum), pos.reshape(-1, QBLOCK)))
    return from_blocks(out)

def even_mixer(x, w_in, b_gate, pos_k, w1_k, w2_k, pos_v, w1_v, w2_v, w_o, pos, cos, sin):
    bsz, s_len, _ = x.shape
    h = x @ w_in
    q_a, k_a, v_a, q_i, k_i, w_i, q_b, kv_b, g_b = split_cols(h, EVEN_SPLITS)
    q_a = apply_rope(q_a.reshape(bsz, s_len, A_HEADS, HEAD_DIM), cos, sin)
    k_a = apply_rope(k_a, cos, sin)
    q_i = apply_rope(q_i.reshape(bsz, s_len, IDX_HEADS, IDX_DIM), cos, sin)
    k_i = apply_rope(k_i, cos, sin)
    o_a = dsa_attention(q_a, k_a, v_a, q_i, k_i, w_i, pos)
    k_c, v_c, k_s, v_s, k_w, v_w = jnp.split(kv_b, 6, axis=-1)
    q_b = apply_rope(q_b.reshape(bsz, s_len, B_HEADS, HEAD_DIM), cos, sin)
    o_b = nsa_attention(q_b, k_c, v_c, apply_rope(k_s, cos, sin), v_s, apply_rope(k_w, cos, sin), v_w,
                        (g_b + b_gate).reshape(bsz, s_len, B_HEADS, 3),
                        pos_k, w1_k, w2_k, pos_v, w1_v, w2_v, pos, cos, sin)
    o = jnp.concatenate([o_a.reshape(bsz, s_len, MIX_A), o_b.reshape(bsz, s_len, MIX_B)], axis=-1)
    return o @ w_o

def odd_mixer(x, w_in, b_f, w_o, pos):
    bsz, s_len, _ = x.shape
    q, k, v, f = split_cols(x @ w_in, ODD_SPLITS)
    shp = (bsz, s_len, C_HEADS, HEAD_DIM)
    log_f = jax.nn.log_sigmoid((f + b_f).astype(jnp.float32))
    o = fox_attention(q.reshape(shp), k.reshape(shp), v.reshape(shp), log_f, pos)
    return o.reshape(bsz, s_len, MIX_ODD) @ w_o

def grouped_experts(xf, eidx, gates, w1, w3, w2):
    n_tok, d = xf.shape
    tk = n_tok * TOP_K
    n_blocks = (tk + N_EXPERTS * (EXPERT_BLOCK - 1)) // EXPERT_BLOCK + 1
    flat_e = eidx.reshape(tk)
    flat_tok = jnp.arange(tk, dtype=jnp.int32) // TOP_K
    flat_g = gates.reshape(tk)
    order = jnp.argsort(flat_e)
    se = flat_e[order]
    counts = jnp.bincount(flat_e, length=N_EXPERTS)
    padded = (counts + EXPERT_BLOCK - 1) // EXPERT_BLOCK * EXPERT_BLOCK
    start_sorted = jnp.cumsum(counts) - counts
    pad_end = jnp.cumsum(padded)
    start_pad = pad_end - padded
    dest = start_pad[se] + (jnp.arange(tk, dtype=jnp.int32) - start_sorted[se])
    n_slots = n_blocks * EXPERT_BLOCK
    slot_tok = jnp.full((n_slots,), n_tok, jnp.int32).at[dest].set(flat_tok[order])
    slot_gate = jnp.zeros((n_slots,), jnp.float32).at[dest].set(flat_g[order])
    blk_e = jnp.minimum(jnp.searchsorted(pad_end, jnp.arange(n_blocks, dtype=jnp.int32) * EXPERT_BLOCK,
                                         side='right'), N_EXPERTS - 1)
    xpad = jnp.concatenate([xf, jnp.zeros((1, d), xf.dtype)], axis=0)

    def step(out, args):
        tok, g, e = args
        xe = xpad[tok]
        h = jax.nn.silu(xe @ w1[e]) * (xe @ w3[e])
        y = (h @ w2[e]) * g[:, None].astype(xe.dtype)
        return out.at[tok].add(y), None

    out, _ = lax.scan(step, jnp.zeros((n_tok + 1, d), xf.dtype),
                      (slot_tok.reshape(n_blocks, EXPERT_BLOCK), slot_gate.reshape(n_blocks, EXPERT_BLOCK), blk_e))
    return out[:n_tok]

def moe_ffn(x, router_w, router_bias, w1, w3, w2, sw1, sw3, sw2):
    bsz, s_len, d = x.shape
    n_tok = bsz * s_len
    xf = x.reshape(n_tok, d)
    shared = (jax.nn.silu(xf @ sw1) * (xf @ sw3)) @ sw2
    s = jax.nn.sigmoid(jnp.matmul(xf, router_w, preferred_element_type=jnp.float32))
    sb = s + router_bias.astype(jnp.float32)
    gscore = lax.top_k(sb.reshape(n_tok, N_GROUPS, N_EXPERTS // N_GROUPS), 2)[0].sum(-1)
    _, gsel = lax.top_k(gscore, TOPK_GROUPS)
    gmask = jnp.any(gsel[..., None] == jnp.arange(N_GROUPS), axis=-2)
    emask = jnp.repeat(gmask, N_EXPERTS // N_GROUPS, axis=-1)
    _, eidx = lax.top_k(jnp.where(emask, sb, NEG), TOP_K)
    sel = jnp.take_along_axis(s, eidx, axis=-1)
    gates = sel / jnp.sum(sel, axis=-1, keepdims=True) * ROUTED_SCALE
    routed = grouped_experts(xf, eidx, gates, w1, w3, w2)
    return (shared + routed).reshape(bsz, s_len, d)

def setup_inputs(seed: int = 0) -> dict:
    key = jax.random.key(seed)
    ks = jax.random.split(key, 32)

    def nrm(k, shape, scale):
        return jax.random.normal(k, shape, jnp.float32) * scale

    d, f, e = D_MODEL, D_EXPERT, N_EXPERTS
    cl = CMP_LEN * HEAD_DIM
    return {
        'x': nrm(ks[0], (BATCH, SEQ, d), 1.0),
        'p': nrm(ks[1], (DEPTH, BATCH, SEQ, PLE_DIM), 1.0),
        'ev_w_in': nrm(ks[2], (N_EVEN, d, EVEN_COLS), d ** -0.5),
        'ev_b_gate': nrm(ks[3], (N_EVEN, 3 * B_HEADS), 0.1),
        'ev_cmp_pos_k': nrm(ks[4], (N_EVEN, CMP_LEN, HEAD_DIM), 0.1),
        'ev_cmp_w1_k': nrm(ks[5], (N_EVEN, cl, HEAD_DIM), cl ** -0.5),
        'ev_cmp_w2_k': nrm(ks[6], (N_EVEN, HEAD_DIM, HEAD_DIM), HEAD_DIM ** -0.5),
        'ev_cmp_pos_v': nrm(ks[7], (N_EVEN, CMP_LEN, HEAD_DIM), 0.1),
        'ev_cmp_w1_v': nrm(ks[8], (N_EVEN, cl, HEAD_DIM), cl ** -0.5),
        'ev_cmp_w2_v': nrm(ks[9], (N_EVEN, HEAD_DIM, HEAD_DIM), HEAD_DIM ** -0.5),
        'ev_w_o': nrm(ks[10], (N_EVEN, MIX_EVEN, d), BETA * MIX_EVEN ** -0.5),
        'od_w_in': nrm(ks[11], (N_ODD, d, ODD_COLS), d ** -0.5),
        'od_b_f': FORGET_BIAS_INIT + nrm(ks[12], (N_ODD, C_HEADS), 0.1),
        'od_w_o': nrm(ks[13], (N_ODD, MIX_ODD, d), BETA * MIX_ODD ** -0.5),
        'ln1_g': 1.0 + nrm(ks[14], (DEPTH, d), 0.05),
        'ln1_b': nrm(ks[15], (DEPTH, d), 0.02),
        'ln2_g': 1.0 + nrm(ks[16], (DEPTH, d), 0.05),
        'ln2_b': nrm(ks[17], (DEPTH, d), 0.02),
        'router_w': nrm(ks[18], (DEPTH, d, e), d ** -0.5),
        'router_bias': nrm(ks[19], (DEPTH, e), 0.01),
        'exp_w1': nrm(ks[20], (DEPTH, e, d, f), d ** -0.5),
        'exp_w3': nrm(ks[21], (DEPTH, e, d, f), d ** -0.5),
        'exp_w2': nrm(ks[22], (DEPTH, e, f, d), BETA * f ** -0.5),
        'sh_w1': nrm(ks[23], (DEPTH, d, f), d ** -0.5),
        'sh_w3': nrm(ks[24], (DEPTH, d, f), d ** -0.5),
        'sh_w2': nrm(ks[25], (DEPTH, f, d), BETA * f ** -0.5),
        'ple_w_gate': nrm(ks[26], (DEPTH, d, d), d ** -0.5),
        'ple_w_proj': nrm(ks[27], (DEPTH, PLE_DIM, d), PLE_DIM ** -0.5),
        'ple_norm_g': 1.0 + nrm(ks[28], (DEPTH, d), 0.05),
    }

def reference(x, p, ev_w_in, ev_b_gate, ev_cmp_pos_k, ev_cmp_w1_k, ev_cmp_w2_k,
              ev_cmp_pos_v, ev_cmp_w1_v, ev_cmp_w2_v, ev_w_o, od_w_in, od_b_f, od_w_o,
              ln1_g, ln1_b, ln2_g, ln2_b, router_w, router_bias, exp_w1, exp_w3, exp_w2,
              sh_w1, sh_w3, sh_w2, ple_w_gate, ple_w_proj, ple_norm_g):
    s_len = x.shape[1]
    pos = jnp.arange(s_len, dtype=jnp.int32)
    cos, sin = rope_tables(pos)
    for i in range(DEPTH):
        j = i // 2
        if i % 2 == 0:
            h = even_mixer(x, ev_w_in[j], ev_b_gate[j], ev_cmp_pos_k[j], ev_cmp_w1_k[j], ev_cmp_w2_k[j],
                           ev_cmp_pos_v[j], ev_cmp_w1_v[j], ev_cmp_w2_v[j], ev_w_o[j], pos, cos, sin)
        else:
            h = odd_mixer(x, od_w_in[j], od_b_f[j], od_w_o[j], pos)
        x = layer_norm(ALPHA * x + h, ln1_g[i], ln1_b[i])
        m = moe_ffn(x, router_w[i], router_bias[i], exp_w1[i], exp_w3[i], exp_w2[i],
                    sh_w1[i], sh_w3[i], sh_w2[i])
        x = layer_norm(ALPHA * x + m, ln2_g[i], ln2_b[i])
        e_i = rms_norm(p[i] @ ple_w_proj[i], ple_norm_g[i])
        x = x + jax.nn.sigmoid(x @ ple_w_gate[i]) * e_i
    return x


_drawn_inputs = setup_inputs


def setup_inputs(seed=0):
    import zlib

    import numpy as np

    out = dict(_drawn_inputs(seed))
    spreads = {}
    factors = {'ev_b_gate': 3.934, 'ev_cmp_pos_k': 15.02, 'od_b_f': 36.384}
    for name, (base, spread) in spreads.items():
        noise = np.random.default_rng([zlib.crc32(name.encode()), seed]).standard_normal(out[name].shape)
        drawn = base * np.exp(spread * noise) if base else spread * noise
        out[name] = jnp.asarray(drawn.astype(out[name].dtype))
    for name, factor in factors.items():
        out[name] = (out[name] * factor).astype(out[name].dtype)
    return out
```

```python
from contextlib import ExitStack

import numpy as np
import concourse.bass as bass
from concourse import mybir

ALU = mybir.AluOpType
ACT = mybir.ActivationFunctionType
F32 = mybir.dt.float32
AX_X = mybir.AxisListType.X

P = 128
D = 1024
DC = D // P
SEQ = 256
NT = SEQ // P
DEPTH = 2
HD = 64
PLE = 256
LN_EPS = 1e-5
RMS_EPS = 1e-6
NEG = -1e30
TAKEN = -3e38
ALPHA = (2.0 * DEPTH) ** 0.25
SCALE = HD ** -0.5

HEADS = 8
FOX_HEADS = 16
IDX_SCALE = (8 * 64) ** -0.5
TOPK_KEYS = 64
CMP_LEN = 32
CMP_STRIDE = 16
N_CMP = (SEQ - CMP_LEN) // CMP_STRIDE + 1
CMP_PAD = 16

NE = 64
TOP_E = 8
N_GROUPS = 8
TOP_GROUPS = 4
FE = 256
ROUTED_SCALE = 2.5

QA, KA, VA, QI, KI, WI, QB, KC, VC, KS, VS, KW, VW, GB = (
    0, 512, 576, 640, 1152, 1216, 1224, 1736, 1800, 1864, 1928, 1992, 2056, 2120)
EVEN_COLS = 2144
ODD_COLS = 3 * D + FOX_HEADS

RING = 4
SLOT = 6144
PIECE = 512
UNROLL = 4

C_ID = 0
C_CAUSAL = C_ID + P
C_TRI = C_CAUSAL + SEQ
C_COS = C_TRI + 2 * SEQ
C_SIN = C_COS + NT * 32
C_CCOS = C_SIN + NT * 32
C_CSIN = C_CCOS + 32
C_CBIAS = C_CSIN + 32
C_CVALID = C_CBIAS + NT * CMP_PAD
C_REP = C_CVALID + NT * CMP_PAD
C_BD = C_REP + P
C_DELTA = C_BD + HEADS
C_END = C_DELTA + FOX_HEADS // 2


def slot_head(s):
    return 2 * (s % 4) + s // 4


def constant_table():
    t = np.zeros((P, C_END), np.float32)
    r = np.arange(P)
    t[:, C_ID:C_ID + P] = np.eye(P)
    t[:, C_CAUSAL + P:C_CAUSAL + SEQ] = np.where(r[None, :] > r[:, None], NEG, 0.0)
    for c in range(NT):
        tok, pos = c * P + r, np.arange(SEQ)
        t[:, C_TRI + c * SEQ:C_TRI + (c + 1) * SEQ] = tok[:, None] <= pos[None, :]
    inv = 1.0 / (10000.0 ** (np.arange(0, HD, 2, dtype=np.float32) / HD))
    ang = np.arange(SEQ, dtype=np.float32)[:, None] * inv.astype(np.float32)[None, :]
    cos, sin = np.cos(ang), np.sin(ang)
    last = np.arange(N_CMP) * CMP_STRIDE + CMP_LEN - 1
    for c in range(NT):
        t[:, C_COS + 32 * c:C_COS + 32 * c + 32] = cos[c * P:(c + 1) * P]
        t[:, C_SIN + 32 * c:C_SIN + 32 * c + 32] = sin[c * P:(c + 1) * P]
        ok = np.zeros((P, CMP_PAD), bool)
        ok[:, :N_CMP] = last[None, :] <= (c * P + r)[:, None]
        t[:, C_CBIAS + CMP_PAD * c:C_CBIAS + CMP_PAD * (c + 1)] = np.where(ok, 0.0, NEG)
        t[:, C_CVALID + CMP_PAD * c:C_CVALID + CMP_PAD * (c + 1)] = ok
    t[:N_CMP, C_CCOS:C_CCOS + 32] = cos[last]
    t[:N_CMP, C_CSIN:C_CSIN + 32] = sin[last]
    for c in range(CMP_PAD):
        t[c, C_REP + c:C_REP + P:CMP_PAD] = 1.0
    for s in range(HEADS):
        t[s * CMP_PAD:(s + 1) * CMP_PAD, C_BD + slot_head(s)] = 1.0
    for h in range(FOX_HEADS):
        t[64 * (h % 2) + h, C_DELTA + h // 2] = 1.0
        t[64 * (h % 2) + 32 + h, C_DELTA + h // 2] = -1.0
    return t


def build_trunk(nc, a, out):
    with ExitStack() as ctx:
        def sb(name, *shape):
            return ctx.enter_context(nc.sbuf_tensor(name, [P, *shape], F32))

        sems = {}

        def sem(name):
            if name not in sems:
                sems[name] = ctx.enter_context(nc.semaphore(name))
            return sems[name]

        ps = ctx.enter_context(nc.psum_tensor("ps", [P, 8, 512], F32))

        ring = sb("ring", RING, SLOT)
        const = sb("const", C_END)
        x_tok = sb("x_tok", NT, D)
        xT = sb("xT", DC, SEQ)
        proj = sb("proj", NT, EVEN_COLS)
        qkT = sb("qkT", 17, SEQ)
        roped = sb("roped", NT, 2048)
        pT = sb("pT", 2, 1024)
        o_tok = sb("o_tok", NT, D)
        gb_row = sb("gb_row", 2, D)
        router_w = sb("router_w", DC, NE)
        router_b = sb("router_b", NE)
        p_tok = sb("p_tok", NT, PLE)
        bgate = sb("bgate", 24)
        fox_b = sb("fox_b", FOX_HEADS)
        small = sb("small", 1024)
        stats = sb("stats", NT, 2, 6)
        selbias = sb("selbias", NT, SEQ)
        gates = sb("gates", NT, 1 + NE)

        scores = roped[:, :, :].rearrange("p t n -> p (t n)").rearrange("p (u n) -> p u n", u=4)
        cmp_w1 = o_tok[:, :, :].rearrange("p t n -> p (t n)").rearrange("p (l f) -> p l f", l=CMP_LEN)
        h_silu = roped[:, 0, 0:1024].rearrange("p (b n) -> p b n", b=2)
        h_gated = roped[:, 1, 0:1024].rearrange("p (b n) -> p b n", b=2)
        y_acc = o_tok

        cmp_blk = selbias[:, :, :].rearrange("p t n -> p (t n)")[:, 0:CMP_LEN * N_CMP].rearrange("p (l c) -> p l c", l=CMP_LEN)
        cmp_s = small[:, 512:768].rearrange("p (t n) -> p t n", t=NT)
        small_pT = small[:, 768:1024].rearrange("p (t n) -> p t n", t=NT)
        v_bd = pT[:, 0, 0:512]
        v_fox = proj[:, :, :].rearrange("p t n -> p (t n)")[:, 0:NT * D].rearrange("p (t n) -> p t n", t=NT)
        logf = small[:, 64:64 + NT * FOX_HEADS].rearrange("p (t n) -> p t n", t=NT)
        aug_k = small[:, 256:512]
        proj_flat = proj[:, :, :].rearrange("p t n -> p (t n)")
        aug_q = proj_flat[:, NT * D:NT * D + 8 * SEQ].rearrange("p (h n) -> p h n", h=8)
        aug_d = small[:, 512:768]
        ple_pT = pT[:, 0, 0:512].rearrange("p (c n) -> p c n", c=2)

        relu_buf = pT[:, 1, 0:512].rearrange("p (b n) -> p b n", b=2)
        rows = sb("rows", 512)
        neg_max = rows[:, 0:8].rearrange("p (u s) -> p u s", u=2)
        denom = rows[:, 8:24].rearrange("p (u s) -> p u s", u=2)
        coef = rows[:, 24:32]
        coef_h = rows[:, 32:40]
        mean_var = rows[:, 40:42]
        rstd = rows[:, 42:43]
        ple_ss = rows[:, 43:45]
        best8 = rows[:, 48:56]
        gscore = rows[:, 56:64]
        gmask0 = rows[:, 64:72]
        gmax = rows[:, 72:136].rearrange("p (g e) -> p g e", g=8)
        gate_sig = rows[:, 136:184]
        cmp_m = rows[:, 184:200]
        fox_t = rows[:, 200:232]
        fox_zb = rows[:, 232:264]
        sb_ = rows[:, 264:328]
        sig = rows[:, 328:456].rearrange("p (t n) -> p t n", t=NT)
        peT = rows[:, 456:488]
        var_eps = rows[:, 488:489]
        newton = rows[:, 489:490]
        kvT = small[:, 512:768]
        tmp_o = sb("tmp_o", 512)[:, :]
        o_tok_tmp = tmp_o

        ident = const[:, C_ID:C_ID + P]
        block = ctx.enter_context(nc.Block())

        items = []

        def static_item(parts, release):
            items.append((parts, release))

        def piece(w, c0, c1):
            n = c1 - c0
            return ((0, DC * n), (DC, n), w.rearrange("(p c) n -> p c n", c=DC)[:, :, c0:c1])

        proj_pieces = {
            0: [(c, min(c + PIECE, EVEN_COLS)) for c in range(0, EVEN_COLS, PIECE)],
            1: [(3 * D, ODD_COLS)] + [(c, c + PIECE) for c in range(0, 3 * D, PIECE)],
        }
        first_item = {}
        shared_item = {}
        for L in range(DEPTH):
            w_in = a["ev_w_in"][0] if L % 2 == 0 else a["od_w_in"][0]
            w_o = a["ev_w_o"][0] if L % 2 == 0 else a["od_w_o"][0]
            first_item[L] = len(items)
            for n, (c0, c1) in enumerate(proj_pieces[L % 2]):
                static_item([piece(w_in, c0, c1)], ("proj_mm", L, n))
            for n in range(2):
                static_item([piece(w_o, n * PIECE, (n + 1) * PIECE)], ("wo_mm", L, n))
            shared_item[L] = len(items)
            items.append(("shared", ("moe_down", L, 0)))
            for e in range(NE):
                items.append(("expert", ("moe_down", L, e + 1)))
            static_item([((0, 2 * D), (2, D), a["ple_w_proj"][L].rearrange("(p c) n -> p c n", c=2))], ("ple_mm", L, 0))
            for n in range(2):
                static_item([piece(a["ple_w_gate"][L], n * PIECE, (n + 1) * PIECE)], ("ple_mm", L, 1 + n))

        def release_value(rel):
            what, L, n = rel
            if what == "proj_mm":
                return sem(f"proj_mm{L}"), NT * (n + 1)
            if what == "wo_mm":
                return sem(f"wo_mm{L}"), NT * (n + 1)
            if what == "moe_down":
                return sem("moe_down"), L * (NE + 1) + n + 1
            return sem(f"ple_mm{L}"), NT * (n + 1)

        loaded = []
        total = [0] * RING
        for k, (parts, _) in enumerate(items):
            total[k % RING] += 16 * (3 if parts in ("shared", "expert") else len(parts))
            loaded.append(total[k % RING])
        w_loaded = [sem(f"w_loaded{s}") for s in range(RING)]

        def slot_view(k, n, c):
            return ring[:, k % RING, 0:c * n].rearrange("p (c n) -> p c n", c=c)

        def wait_item(eng, k):
            eng.wait_ge(w_loaded[k % RING], loaded[k])

        UP_N = DC * FE
        DOWN0 = 2 * UP_N

        def ffn_views(slot):
            w1 = ring[:, slot, 0:UP_N].rearrange("p (c f) -> p c f", c=DC)
            w3 = ring[:, slot, UP_N:2 * UP_N].rearrange("p (c f) -> p c f", c=DC)
            w2 = ring[:, slot, DOWN0:DOWN0 + 2 * D].rearrange("p (c n) -> p c n", c=2)
            return w1, w3, w2

        @block.sync
        def _(sp):
            def ffn_load(slot, w1, w3, w2):
                up = "(p c) f -> p (c f)"
                sp.dma_start(ring[:, slot, 0:UP_N], w1.rearrange(up, c=DC)).then_inc(w_loaded[slot], 16)
                sp.dma_start(ring[:, slot, UP_N:2 * UP_N], w3.rearrange(up, c=DC)).then_inc(w_loaded[slot], 16)
                sp.dma_start(ring[:, slot, DOWN0:DOWN0 + 2 * D], w2.rearrange(up, c=2)).then_inc(w_loaded[slot], 16)

            sp.dma_start(x_tok[:, :, :], a["x"][0].rearrange("(t p) n -> p t n", p=P)).then_inc(sem("x_loaded"), 16)
            sp.dma_start(const[:, :], a["const"]).then_inc(sem("const_loaded"), 16)
            for L in range(DEPTH):
                k = first_item[L]
                e0 = shared_item[L] + 1
                end = e0 + NE + 3
                while k < end:
                    if k == e0 + UNROLL:
                        with sp.Fori(1, NE // UNROLL) as i:
                            for u in range(UNROLL):
                                sp.wait_ge(sem("moe_down"), i * UNROLL + (L * (NE + 1) + 2 + u - RING))
                                e = i * UNROLL + u
                                ffn_load((e0 + u) % RING, a["exp_w1"][L, e], a["exp_w3"][L, e], a["exp_w2"][L, e])
                        k = e0 + NE
                        continue
                    if k >= RING:
                        sp.wait_ge(*release_value(items[k - RING][1]))
                    parts = items[k][0]
                    if parts == "shared":
                        ffn_load(k % RING, a["sh_w1"][L], a["sh_w3"][L], a["sh_w2"][L])
                    elif parts == "expert":
                        e = k - e0
                        ffn_load(k % RING, a["exp_w1"][L, e], a["exp_w3"][L, e], a["exp_w2"][L, e])
                    else:
                        for (lo, hi), (c, n), src in parts:
                            sp.dma_start(slot_view(k, n, c), src).then_inc(w_loaded[k % RING], 16)
                    k += 1
            for t in range(NT):
                sp.wait_ge(sem(f"ple_out{DEPTH - 1}"), t + 1)
                sp.dma_start(out[0, t * P:(t + 1) * P, :], x_tok[:, t, :]).then_inc(sem("out_stored"), 16)
            sp.wait_ge(sem("out_stored"), 16 * NT)

        @block.gpsimd
        def _(pool):
            pool.memset(small[:, 0:1024], 0.0).then_inc(sem("small_zero"), 1)
            pool.dma_start(bgate[:, :], a["ev_b_gate"][0].partition_broadcast(P)).then_inc(sem("bias_loaded"), 16)
            pool.dma_start(fox_b[:, :], a["od_b_f"][0].partition_broadcast(P)).then_inc(sem("bias_loaded"), 16)
            pe_t = qkT[:, 16, 0:2 * HD]
            pool.dma_start(pe_t[0:CMP_LEN, 0:HD], a["ev_cmp_pos_k"][0]).then_inc(sem("cmp_loaded"), 16)
            pool.dma_start(pe_t[0:CMP_LEN, HD:2 * HD], a["ev_cmp_pos_v"][0]).then_inc(sem("cmp_loaded"), 16)
            pool.dma_start(cmp_w1[0:HD], a["ev_cmp_w1_k"][0].rearrange("(l d) f -> d l f", d=HD)).then_inc(sem("cmp_loaded"), 16)
            pool.dma_start(cmp_w1[HD:P], a["ev_cmp_w1_v"][0].rearrange("(l d) f -> d l f", d=HD)).then_inc(sem("cmp_loaded"), 16)
            pool.wait_ge(sem("small_zero"), 1)
            pool.dma_start(small[0:HD, 0:HD], a["ev_cmp_w2_k"][0]).then_inc(sem("cmp_loaded"), 16)
            pool.dma_start(small[0:HD, HD:2 * HD], a["ev_cmp_w2_v"][0]).then_inc(sem("cmp_loaded"), 16)
            for L in range(DEPTH):
                if L:
                    pool.wait_ge(sem(f"router_mm{L - 1}"), NT)
                    pool.wait_ge(sem(f"router_dve{L - 1}"), NT)
                    pool.wait_ge(sem(f"pT_tp{L - 1}"), NT)
                pool.dma_start(router_w[:, :, :], a["router_w"][L].rearrange("(p c) n -> p c n", c=DC)).then_inc(sem("layer_loaded"), 16)
                pool.dma_start(router_b[:, :], a["router_bias"][L].partition_broadcast(P)).then_inc(sem("layer_loaded"), 16)
                pool.dma_start(p_tok[:, :, :], a["p"][L, 0].rearrange("(t p) n -> p t n", p=P)).then_inc(sem("layer_loaded"), 16)
                for n, (g, b) in enumerate((("ln1_g", "ln1_b"), ("ln2_g", "ln2_b"), ("ple_norm_g", None))):
                    if 3 * L + n:
                        pool.wait_ge(sem("gb_used"), NT * (3 * L + n))
                    pool.dma_start(gb_row[:, 0, :], a[g][L].partition_broadcast(P)).then_inc(sem("gb_loaded"), 16)
                    pool.dma_start(gb_row[:, 1, :], a[b or g][L].partition_broadcast(P)).then_inc(sem("gb_loaded"), 16)

        UNITS = {0: [("sel", t, g) for t in range(NT) for g in range(2)]
                 + [("win", t, g) for t in range(NT) for g in range(2)]
                 + [("dsa", t, g) for t in range(NT) for g in range(2)],
                 1: [("fox", t, g) for t in range(NT) for g in range(4)]}
        BRANCH = {"sel": (20, 28, VS), "win": (20, 30, VW), "dsa": (0, 8, VA)}

        def n_keys(t):
            return (t + 1) * P

        def unit_slots(g):
            return [4 * g + 2 * j + parity for parity in range(2) for j in range(2)]

        @block.tensor
        def _(pe):
            def transpose_x(j, src, ready):
                for t in range(NT):
                    ready(t)
                    for c in range(DC):
                        ins = pe.transpose(ps[:, 2 * t + c // 4, (c % 4) * P:(c % 4 + 1) * P],
                                           src[:, t, c::DC], ident)
                    ins.then_inc(sem("xT_tp"), 1)

            def wait_xT(j):
                pe.wait_ge(sem("xT_act"), NT * (j + 1))
                pe.wait_ge(sem("xT_dve"), NT * (j + 1))

            def attention(L):
                units = UNITS[L % 2]
                for u in range(len(units) + 2):
                    if u < len(units):
                        what, t, g = units[u]
                        K = n_keys(t)
                        if u >= 2:
                            pe.wait_ge(sem(f"sc_biased{L}"), u - 1)
                        for s, h in enumerate(unit_slots(g)):
                            o = ps[:, 2 * (u % 2) + s // 2, (s % 2) * K:(s % 2 + 1) * K]
                            r = slice(HD * (h % 2), HD * (h % 2) + HD)
                            if what == "fox":
                                ra = slice(HD * (h % 2), HD * (h % 2) + 48)
                                ins = pe.matmul(o, qkT[r, h // 2, t * P:(t + 1) * P], qkT[r, 8 + h // 2, 0:K],
                                                start=True, stop=False)
                                ins = pe.matmul(o, aug_q[ra, h // 2, t * P:(t + 1) * P], aug_k[ra, 0:K],
                                                start=False, stop=True)
                            else:
                                q0, k0, _ = BRANCH[what]
                                ins = pe.matmul(o, qkT[r, (q0 + h) // 2, t * P:(t + 1) * P],
                                                qkT[r, k0 // 2, 0:K], start=True, stop=True)
                        ins.then_inc(sem(f"sc_mm{L}"), 1)
                    if 1 <= u <= len(units):
                        v = u - 1
                        what, t, g = units[v]
                        pe.wait_ge(sem(f"sc_exp{L}"), v + 1)
                        if v:
                            pe.wait_ge(sem(f"pT_copied{L}"), v)
                        for s in range(4):
                            for c in range(t + 1):
                                b = s * (t + 1) + c
                                ins = pe.transpose(ps[:, 4 + b // 4, (b % 4) * P:(b % 4 + 1) * P],
                                                   scores[:, v % 2, s * n_keys(t) + c * P:s * n_keys(t) + (c + 1) * P],
                                                   ident)
                        ins.then_inc(sem(f"pT_tp{L}u"), 1)
                    if u >= 2:
                        v = u - 2
                        what, t, g = units[v]
                        pe.wait_ge(sem(f"pT_copied{L}"), v + 1)
                        grp = v // 2
                        if v % 2 == 0 and grp >= 2:
                            pe.wait_ge(sem(f"pv_out{L}"), grp - 1)
                        for s, h in enumerate(unit_slots(g)):
                            hh = h % 8
                            for c in range(t + 1):
                                vals = (v_fox[:, c, h * HD:(h + 1) * HD] if what == "fox"
                                        else proj[:, c, BRANCH[what][2]:BRANCH[what][2] + HD])
                                ins = pe.matmul(ps[:, 6 + grp % 2, hh * HD:(hh + 1) * HD],
                                                pT[:, v % 2, (s * (t + 1) + c) * P:(s * (t + 1) + c + 1) * P],
                                                vals, start=(c == 0), stop=(c == t))
                        ins.then_inc(sem(f"pv_mm{L}"), 1)

            pe.wait_ge(sem("const_loaded"), 16)
            for L in range(DEPTH):
                if L == 0:
                    def ready(t):
                        pe.wait_ge(sem("x_loaded"), 16)
                else:
                    def ready(t, L=L):
                        pe.wait_ge(sem(f"ple_out{L - 1}"), t + 1)
                transpose_x(3 * L, x_tok, ready)
                wait_xT(3 * L)
                n = 0
                if L % 2 == 0:
                    for j, (c0, c1) in enumerate(proj_pieces[0]):
                        k = first_item[L] + j
                        wait_item(pe, k)
                        w = slot_view(k, c1 - c0, DC)
                        for t in range(NT):
                            if j >= 2:
                                pe.wait_ge(sem(f"proj_t{t}_{L}"), j - 1)
                            for c in range(DC):
                                ins = pe.matmul(ps[:, 4 + (2 * j + t) % 4, 0:c1 - c0], xT[:, c, t * P:(t + 1) * P],
                                                w[:, c, :], start=(c == 0), stop=(c == DC - 1))
                            ins.then_inc(sem(f"proj_mm{L}"), 1)
                    for m in range(4):
                        pe.wait_ge(sem(f"roped{L}"), (1, 3, 4, 5)[m])
                        pe.wait_ge(sem(f"dup{L}"), (0, 2, 2, 4)[m]) if m else None
                        if m >= 2:
                            pe.wait_ge(sem(f"qkT_copied{L}"), m - 1)
                        for b in range(4):
                            for t in range(NT):
                                ins = pe.transpose(ps[:, 2 * (m % 2) + b // 2, (b % 2) * SEQ + t * P:(b % 2) * SEQ + (t + 1) * P],
                                                   roped[:, t, (4 * m + b) * P:(4 * m + b + 1) * P], ident)
                        ins.then_inc(sem(f"qkT_tp{L}"), 1)
                    pe.wait_ge(sem(f"proj_t0_{L}"), 5)
                    pe.wait_ge(sem(f"proj_t1_{L}"), 5)
                    for t in range(NT):
                        pe.transpose(ps[:, 4, t * P:(t + 1) * P], proj[:, t, KC:KC + P], ident)
                    pe.wait_ge(sem("cmp_loaded"), 96)
                    pe.transpose(ps[:, 5, 0:CMP_LEN], qkT[0:CMP_LEN, 16, 0:P], ident[0:CMP_LEN, 0:CMP_LEN])\
                        .then_inc(sem("cmp_tp"), 1)
                    pe.wait_ge(sem("cmp_blk"), 1)
                    for half in range(2):
                        r = slice(HD * half, HD * half + HD)
                        for l in range(CMP_LEN):
                            ins = pe.matmul(ps[0:HD, 6 + half, 0:N_CMP], cmp_w1[r, l, :],
                                            cmp_blk[r, l, :], start=(l == 0), stop=(l == CMP_LEN - 1))
                    ins.then_inc(sem("cmp_h"), 1)
                    pe.wait_ge(sem("cmp_hs"), 1)
                    for half in range(2):
                        ins = pe.matmul(ps[0:N_CMP, 4, half * HD:(half + 1) * HD],
                                        small[0:HD, 128 + 16 * half:128 + 16 * half + N_CMP],
                                        small[0:HD, half * HD:(half + 1) * HD], start=True, stop=True)
                    ins.then_inc(sem("cmp_kv"), 1)
                    pe.wait_ge(sem("cmp_roped"), 1)
                    pe.transpose(ps[:, 5, 0:CMP_PAD], small[0:CMP_PAD, 256:384], ident[0:CMP_PAD, 0:CMP_PAD])
                    pe.matmul(ps[:, 6, 0:HD], const[0:CMP_PAD, C_REP:C_REP + P], small[0:CMP_PAD, 384:448],
                              start=True, stop=True).then_inc(sem("cmp_rep"), 1)
                    pe.wait_ge(sem("cmp_kT"), 1)
                    pe.wait_ge(sem(f"qkT_copied{L}"), 4)
                    for t in range(NT):
                        for h in range(HEADS):
                            r = slice(HD * (h % 2), HD * (h % 2) + HD)
                            c0 = t * 64 + (h // 2) * CMP_PAD
                            ins = pe.matmul(ps[:, 4 + h % 2, c0:c0 + CMP_PAD], qkT[r, (20 + h) // 2, t * P:(t + 1) * P],
                                            small[r, 448:448 + CMP_PAD], start=True, stop=True)
                    ins.then_inc(sem("cmp_sc"), 1)
                    pe.wait_ge(sem("cmp_p"), NT)
                    for t in range(NT):
                        ins = pe.transpose(ps[:, 4, t * P:(t + 1) * P], cmp_s[:, t, :], ident)
                    ins.then_inc(sem("cmp_pT"), 1)
                    pe.wait_ge(sem("cmp_pT_copied"), 1)
                    for t in range(NT):
                        ins = pe.matmul(ps[:, 6 + t, :], small_pT[:, t, :], v_bd, start=True, stop=True)
                    ins.then_inc(sem("cmp_o"), 1)
                    for n in range(NT * HEADS):
                        t, h = n // HEADS, n % HEADS
                        r = slice(HD * (h % 2), HD * (h % 2) + HD)
                        if n >= 4:
                            pe.wait_ge(sem("idx_relu"), n - 3)
                        pe.matmul(ps[:, n % 4, 0:n_keys(t)], qkT[r, (10 + h) // 2, t * P:(t + 1) * P],
                                  qkT[r, 9, 0:n_keys(t)], start=True, stop=True).then_inc(sem("idx_mm"), 1)
                    pe.wait_ge(sem("idx_relu"), NT * HEADS)
                    pe.wait_ge(sem("cmp_out"), NT)
                else:
                    k = first_item[L]
                    wait_item(pe, k)
                    w = slot_view(k, FOX_HEADS, DC)
                    for t in range(NT):
                        for c in range(DC):
                            ins = pe.matmul(ps[:, 6, t * FOX_HEADS:(t + 1) * FOX_HEADS], xT[:, c, t * P:(t + 1) * P],
                                            w[:, c, :], start=(c == 0), stop=(c == DC - 1))
                        ins.then_inc(sem(f"proj_mm{L}"), 1)
                    for j in range(4):
                        k = first_item[L] + 1 + j
                        wait_item(pe, k)
                        w = slot_view(k, PIECE, DC)
                        for half in range(2):
                            if j >= 2:
                                pe.wait_ge(sem(f"proj_t{half}_{L}"), j - 1)
                            for b in range(2):
                                for c in range(DC):
                                    ins = pe.matmul(ps[:, (2 * j + half) % 4, b * SEQ:(b + 1) * SEQ],
                                                    w[:, c, (2 * half + b) * P:(2 * half + b + 1) * P], xT[:, c, :],
                                                    start=(c == 0), stop=(c == DC - 1))
                            ins.then_inc(sem(f"proj_mm{L}"), 1)
                    pe.wait_ge(sem("logf"), 1)
                    for c in range(NT):
                        ins = pe.matmul(ps[0:FOX_HEADS, 7, 0:SEQ], logf[:, c, :],
                                        const[:, C_TRI + c * SEQ:C_TRI + (c + 1) * SEQ], start=(c == 0), stop=(c == NT - 1))
                    ins.then_inc(sem("dcum"), 1)
                    for j in range(2):
                        k = first_item[L] + 5 + j
                        wait_item(pe, k)
                        w = slot_view(k, PIECE, DC)
                        for t in range(NT):
                            pe.wait_ge(sem(f"proj_t{t}_{L}"), j + 3)
                            for c in range(DC):
                                ins = pe.matmul(ps[:, (2 * j + t) % 4, :], xT[:, c, t * P:(t + 1) * P],
                                                w[:, c, :], start=(c == 0), stop=(c == DC - 1))
                            ins.then_inc(sem(f"proj_mm{L}"), 1)
                    pe.wait_ge(sem(f"proj_t0_{L}"), 6)
                    pe.wait_ge(sem(f"proj_t1_{L}"), 6)
                    pe.wait_ge(sem("aug"), 1)
                attention(L)

                def o_ready(t, L=L):
                    pe.wait_ge(sem(f"o_ready{L}"), t + 1)
                    if L % 2 == 0:
                        pe.wait_ge(sem(f"proj_t0_{L}"), 5)
                transpose_x(3 * L, o_tok, o_ready)
                pe.wait_ge(sem("oT_act"), NT * (L + 1))
                pe.wait_ge(sem("oT_dve"), NT * (L + 1))
                for n in range(2):
                    k = shared_item[L] - 2 + n
                    wait_item(pe, k)
                    w = slot_view(k, PIECE, DC)
                    for t in range(NT):
                        for c in range(DC):
                            ins = pe.matmul(ps[:, 4 + 2 * t + n, :], xT[:, c, t * P:(t + 1) * P], w[:, c, :],
                                            start=(c == 0), stop=(c == DC - 1))
                        ins.then_inc(sem(f"wo_mm{L}"), 1)

                transpose_x(3 * L + 1, x_tok, lambda t: pe.wait_ge(sem(f"ln1_out{L}"), t + 1))
                wait_xT(3 * L + 1)
                pe.wait_ge(sem("layer_loaded"), 48 * (L + 1))
                for t in range(NT):
                    for c in range(DC):
                        ins = pe.matmul(ps[:, 4 + t, 0:NE], xT[:, c, t * P:(t + 1) * P], router_w[:, c, :],
                                        start=(c == 0), stop=(c == DC - 1))
                    ins.then_inc(sem(f"router_mm{L}"), 1)
                pe.wait_ge(sem(f"router_dve{L}"), NT)

                base = L * (NE + 1)

                def up(n, par, slot):
                    w1, w3, _ = ffn_views(slot)
                    for b, w in enumerate((w1, w3)):
                        for f in range(2):
                            for c in range(DC):
                                ins = pe.matmul(ps[:, 4 + 2 * par + b, f * SEQ:(f + 1) * SEQ], w[:, c, f::2],
                                                xT[:, c, :], start=(c == 0), stop=(c == DC - 1))
                    ins.then_inc(sem("moe_up"), 1)

                def down(n, par, slot):
                    _, _, w2 = ffn_views(slot)
                    pe.wait_ge(sem("moe_h"), n + 1)
                    if base or not isinstance(n, int) or n >= 1:
                        pe.wait_ge(sem("moe_added"), n)
                    for t in range(NT):
                        for half in range(2):
                            for f in range(2):
                                ins = pe.matmul(ps[:, 2 * t + half, :], h_gated[:, par, f * SEQ + t * P:f * SEQ + (t + 1) * P],
                                                w2[:, f, half * PIECE:(half + 1) * PIECE], start=(f == 0), stop=(f == 1))
                    ins.then_inc(sem("moe_down"), 1)

                ks = shared_item[L]
                wait_item(pe, ks)
                up(base, 0, ks % RING)
                with pe.Fori(0, NE // UNROLL) as i:
                    for u in range(UNROLL):
                        slot = (ks + 1 + u) % RING
                        pe.wait_ge(w_loaded[slot], i * 48 + loaded[ks + 1 + u])
                        if u % 2 == 0 and base == 0:
                            pe.wait_ge(sem("moe_h"), i * UNROLL + (base + u))
                        else:
                            pe.wait_ge(sem("moe_h"), i * UNROLL + (base + u))
                        up(None, (u + 1) % 2, slot)
                        down(i * UNROLL + (base + u), u % 2, (ks + u) % RING)
                down(base + NE, NE % 2, (ks + NE) % RING)

                kp = ks + 1 + NE
                for t in range(NT):
                    for c in range(2):
                        ins = pe.transpose(ps[:, 4, c * SEQ + t * P:c * SEQ + (t + 1) * P], p_tok[:, t, c::2], ident)
                    ins.then_inc(sem(f"pT_tp{L}"), 1)
                pe.wait_ge(sem(f"pT_done{L}"), 1)
                wait_item(pe, kp)
                w = slot_view(kp, D, 2)
                for t in range(NT):
                    for half in range(2):
                        for c in range(2):
                            ins = pe.matmul(ps[:, 4 + 2 * t + half, :], ple_pT[:, c, t * P:(t + 1) * P],
                                            w[:, c, half * PIECE:(half + 1) * PIECE], start=(c == 0), stop=(c == 1))
                    ins.then_inc(sem(f"ple_mm{L}"), 1)
                transpose_x(3 * L + 2, x_tok, lambda t: pe.wait_ge(sem(f"ln2_out{L}"), t + 1))
                wait_xT(3 * L + 2)
                for n in range(2):
                    wait_item(pe, kp + 1 + n)
                    w = slot_view(kp + 1 + n, PIECE, DC)
                    for t in range(NT):
                        for c in range(DC):
                            ins = pe.matmul(ps[:, 2 * t + n, :], xT[:, c, t * P:(t + 1) * P], w[:, c, :],
                                            start=(c == 0), stop=(c == DC - 1))
                        ins.then_inc(sem(f"ple_mm{L}"), 1)
                pe.wait_ge(sem(f"ple_out{L}"), NT)

        @block.scalar
        def _(act):
            def copy_T(name, count):
                for t in range(NT):
                    act.wait_ge(sem("xT_tp"), count + t + 1)
                    act.activation(xT[:, 0:4, t * P:(t + 1) * P],
                                   ps[:, 2 * t, :].rearrange("p (c n) -> p c n", c=4),
                                   ACT.Copy).then_inc(sem(name), 1)

            def attention(L):
                units = UNITS[L % 2]
                for u in range(len(units) + 1):
                    if u < len(units):
                        what, t, g = units[u]
                        K = n_keys(t)
                        act.wait_ge(sem(f"sc_max{L}"), u + 1)
                        for s, h in enumerate(unit_slots(g)):
                            ins = act.activation(scores[:, u % 2, s * K:(s + 1) * K], scores[:, u % 2, s * K:(s + 1) * K],
                                                 ACT.Exp, bias=neg_max[:, u % 2, s:s + 1],
                                                 accum_out=denom[:, (u // 2) % 2, 4 * (u % 2) + s:4 * (u % 2) + s + 1])
                        ins.then_inc(sem(f"sc_exp{L}"), 1)
                    if u >= 1:
                        v = u - 1
                        t = units[v][1]
                        act.wait_ge(sem(f"pT_tp{L}u"), v + 1)
                        if v >= 2:
                            act.wait_ge(sem(f"pv_mm{L}"), v - 1)
                        n = 4 * (t + 1) * P
                        act.activation(pT[:, v % 2, 0:n], ps[:, 4:6, :].rearrange("p b n -> p (b n)")[:, 0:n],
                                       ACT.Copy).then_inc(sem(f"pT_copied{L}"), 1)

            rs_count = [0]

            def rsqrt_guess():
                rs_count[0] += 1
                act.wait_ge(sem("var_ready"), rs_count[0])
                act.activation(rstd, var_eps, ACT.Ln).then_inc(sem("var_ln"), 1)
                act.wait_ge(sem("var_ln"), rs_count[0])
                act.activation(rstd, rstd, ACT.Exp, scale=-0.5).then_inc(sem("rstd_guess"), 1)

            tp = 0
            for L in range(DEPTH):
                copy_T("xT_act", tp)
                tp += NT
                if L % 2 == 0:
                    for j, (c0, c1) in enumerate(proj_pieces[0]):
                        act.wait_ge(sem(f"proj_mm{L}"), 2 * j + 1)
                        act.activation(proj[:, 0, c0:c1], ps[:, 4 + 2 * j % 4, 0:c1 - c0], ACT.Copy)\
                           .then_inc(sem(f"proj_t0_{L}"), 1)
                    dups = ((1, 8, 9), (2, 18, 19), (4, 28, 29), (5, 30, 31))
                    for need, s, d in dups[0:2]:
                        act.wait_ge(sem(f"roped{L}"), (need + 1 if need == 1 else 3))
                        act.activation(roped[:, :, d * HD:(d + 1) * HD], roped[:, :, s * HD:(s + 1) * HD], ACT.Copy)\
                           .then_inc(sem(f"dup{L}"), 1)
                    for m in range(4):
                        if m == 3:
                            for need, s, d in dups[2:4]:
                                act.wait_ge(sem(f"roped{L}"), 5)
                                act.activation(roped[:, :, d * HD:(d + 1) * HD], roped[:, :, s * HD:(s + 1) * HD], ACT.Copy)\
                                   .then_inc(sem(f"dup{L}"), 1)
                        act.wait_ge(sem(f"qkT_tp{L}"), m + 1)
                        act.activation(qkT[:, 4 * m:4 * m + 4, :],
                                       ps[:, 2 * (m % 2):2 * (m % 2) + 2, :].rearrange("p b (c n) -> p (b c) n", c=2),
                                       ACT.Copy).then_inc(sem(f"qkT_copied{L}"), 1)
                    act.wait_ge(sem("cmp_h"), 1)
                    act.activation(small[0:HD, 160:160 + N_CMP], ps[0:HD, 6, 0:N_CMP], ACT.Exp, scale=-1.0)
                    act.activation(small[0:HD, 176:176 + N_CMP], ps[0:HD, 7, 0:N_CMP], ACT.Exp, scale=-1.0)\
                       .then_inc(sem("cmp_exp"), 1)
                    act.wait_ge(sem("gate_z"), 1)
                    act.activation(gate_sig, gate_sig, ACT.Exp, scale=-1.0).then_inc(sem("gate_e"), 1)
                    act.wait_ge(sem("cmp_sub"), 1)
                    act.activation(cmp_s, cmp_s, ACT.Exp).then_inc(sem("cmp_e"), 1)
                    act.wait_ge(sem("cmp_pT"), 1)
                    act.activation(small_pT, ps[:, 4, 0:SEQ], ACT.Copy).then_inc(sem("cmp_pT_copied"), 1)
                    for n in range(NT * HEADS):
                        t = n // HEADS
                        act.wait_ge(sem("idx_mm"), n + 1)
                        if n >= 2:
                            act.wait_ge(sem("idx_acc"), n - 1)
                        act.activation(relu_buf[:, n % 2, 0:n_keys(t)], ps[:, n % 4, 0:n_keys(t)], ACT.Relu)\
                           .then_inc(sem("idx_relu"), 1)
                else:
                    act.wait_ge(sem("fox_z"), 1)
                    act.activation(fox_t, fox_zb, ACT.Abs).then_inc(sem("fox_abs"), 1)
                    act.wait_ge(sem("fox_abs"), 1)
                    act.activation(fox_t, fox_t, ACT.Exp, scale=-1.0).then_inc(sem("fox_e"), 1)
                    act.wait_ge(sem("fox_e"), 1)
                    act.activation(fox_t, fox_t, ACT.Ln, bias=1.0).then_inc(sem("fox_ln"), 1)
                    for j in range(4):
                        act.wait_ge(sem(f"proj_mm{L}"), NT + 2 * j + 1)
                        act.activation(qkT[:, 4 * j:4 * j + 2, :], ps[:, 2 * j % 4, :], ACT.Copy)\
                           .then_inc(sem(f"proj_t0_{L}"), 1)
                    for j in range(2):
                        act.wait_ge(sem(f"proj_mm{L}"), NT + 8 + 2 * j + 1)
                        act.activation(v_fox[:, 0, j * PIECE:(j + 1) * PIECE], ps[:, 2 * j, :], ACT.Copy)\
                           .then_inc(sem(f"proj_t0_{L}"), 1)
                attention(L)
                copy_T("oT_act", tp)
                tp += NT
                rsqrt_guess()
                rsqrt_guess()
                copy_T("xT_act", tp)
                tp += NT
                for t in range(NT):
                    act.wait_ge(sem(f"router_mm{L}"), t + 1)
                    act.activation(sig[:, t, :], ps[:, 4 + t, 0:NE], ACT.Exp, scale=-1.0).then_inc(sem("router_e"), 1)

                base = L * (NE + 1)

                def silu(n, par, first=False):
                    act.wait_ge(sem("moe_up"), n + 1)
                    if not first:
                        act.wait_ge(sem("moe_h"), n - 1)
                    act.activation(h_silu[:, par, :], ps[:, 4 + 2 * par, :], ACT.Silu).then_inc(sem("moe_silu"), 1)

                silu(base, 0, first=True)
                silu(base + 1, 1, first=(base == 0))
                with act.Fori(0, NE // UNROLL - 1) as i:
                    for u in range(UNROLL):
                        silu(i * UNROLL + (base + 2 + u), u % 2)
                for u in range(UNROLL - 1):
                    silu(base + NE - 2 + u, u % 2)

                act.wait_ge(sem(f"pT_tp{L}"), NT)
                act.activation(ple_pT, ps[:, 4, :], ACT.Copy).then_inc(sem(f"pT_done{L}"), 1)
                rsqrt_guess()
                rsqrt_guess()
                for t in range(NT):
                    act.wait_ge(sem(f"ple_mm{L}"), t + 1)
                    act.activation(roped[:, t, 0:D], ps[:, 4 + 2 * t:6 + 2 * t, :], ACT.Square,
                                   accum_out=ple_ss[:, t:t + 1]).then_inc(sem(f"ple_sq{L}"), 1)
                copy_T("xT_act", tp)
                tp += NT
                rsqrt_guess()
                rsqrt_guess()
                for t in range(NT):
                    act.wait_ge(sem(f"ple_mm{L}"), NT * 2 + t + 1)
                    act.wait_ge(sem(f"ple_sq{L}"), NT)
                    act.activation(roped[:, t, 0:D], ps[:, 2 * t:2 * t + 2, :], ACT.Sigmoid)\
                       .then_inc(sem(f"ple_sig{L}"), 1)

        @block.vector
        def _(dve):
            step = [0]
            rs_count = [0]
            chain = sem("dve_step")

            def seq(ins):
                step[0] += 1
                ins.then_inc(chain, 1)
                dve.wait_ge(chain, step[0])

            def copy_T(name, count):
                for t in range(NT):
                    dve.wait_ge(sem("xT_tp"), count + t + 1)
                    dve.tensor_copy(xT[:, 4:8, t * P:(t + 1) * P],
                                    ps[:, 2 * t + 1, :].rearrange("p (c n) -> p c n", c=4))\
                       .then_inc(sem(name), 1)

            def rope(t, src, n, dst, cs, sn, rows_=P, tmp=None):
                c = cs.unsqueeze(1).unsqueeze(1)
                s = sn.unsqueeze(1)
                tmp = tmp if tmp is not None else o_tok_tmp[0:rows_, 0:n * 32].rearrange("p (n k) -> p n k", n=n)
                seq(dve.tensor_tensor(dst, src, c.to_broadcast([rows_, n, 2, 32]), ALU.mult))
                seq(dve.tensor_tensor(tmp, src[:, :, 1, :], s.to_broadcast([rows_, n, 32]), ALU.mult))
                seq(dve.tensor_tensor(dst[:, :, 0, :], dst[:, :, 0, :], tmp, ALU.subtract))
                seq(dve.tensor_tensor(tmp, src[:, :, 0, :], s.to_broadcast([rows_, n, 32]), ALU.mult))
                return dve.tensor_tensor(dst[:, :, 1, :], dst[:, :, 1, :], tmp, ALU.add)

            def attention(L):
                units = UNITS[L % 2]
                for u in range(len(units) + 2):
                    if u < len(units):
                        what, t, g = units[u]
                        K = n_keys(t)
                        dve.wait_ge(sem(f"sc_mm{L}"), u + 1)
                        if u >= 2:
                            dve.wait_ge(sem(f"pT_tp{L}u"), u - 1)
                        bias = selbias[:, t, 0:K] if what == "dsa" else const[:, C_CAUSAL + SEQ - K:C_CAUSAL + SEQ]
                        s_out = scores[:, u % 2, 0:4 * K].rearrange("p (s k) -> p s k", s=4)
                        for b in range(2):
                            ins = dve.scalar_tensor_tensor(
                                s_out[:, 2 * b:2 * b + 2, :], ps[:, 2 * (u % 2) + b, 0:2 * K].rearrange("p (s k) -> p s k", s=2),
                                SCALE, bias.unsqueeze(1).to_broadcast([P, 2, K]), ALU.mult, ALU.add)
                        ins.then_inc(sem(f"sc_biased{L}"), 1)
                        dve.wait_ge(sem(f"sc_biased{L}"), u + 1)
                        if u >= 2:
                            dve.wait_ge(sem(f"sc_exp{L}"), u - 1)
                        dve.tensor_reduce(neg_max[:, u % 2, 0:4], s_out, AX_X, ALU.max, negate=True)\
                           .then_inc(sem(f"sc_max{L}"), 1)
                    if u >= 2 and u % 2 == 1:
                        v = u - 2
                        what, t, g = units[v]
                        grp = v // 2
                        dve.wait_ge(sem(f"pv_mm{L}"), v + 1)
                        seq(dve.reciprocal(coef, denom[:, grp % 2, :]))
                        by_head = coef.rearrange("p (g b j) -> p g j b", g=2, b=2)
                        if what in ("sel", "win"):
                            br = 1 if what == "sel" else 2
                            gate = gate_sig.rearrange("p (t h b) -> p t h b", t=NT, b=3)[:, t, :, br]
                            seq(dve.tensor_tensor(coef_h.rearrange("p (g j b) -> p g j b", g=2, b=2), by_head,
                                                  gate.rearrange("p (g j b) -> p g j b", g=2, b=2), ALU.mult))
                        else:
                            seq(dve.tensor_copy(coef_h.rearrange("p (g j b) -> p g j b", g=2, b=2), by_head))
                        o_ps = ps[:, 6 + grp % 2, :].rearrange("p (h d) -> p h d", h=8)
                        cb = coef_h.unsqueeze(2).to_broadcast([P, 8, HD])
                        if what in ("sel", "win"):
                            o = o_tok[:, t, 512:1024]
                            seq_ins = dve.tensor_tensor(tmp_o.rearrange("p (h d) -> p h d", h=8), o_ps, cb, ALU.mult)
                            seq_ins.then_inc(sem(f"pv_out{L}"), 1)
                            dve.wait_ge(sem(f"pv_out{L}"), grp + 1)
                            seq(dve.tensor_tensor(o, o, tmp_o, ALU.add))
                        else:
                            c0 = 0 if what == "dsa" else 512 * (g // 2)
                            dve.tensor_tensor(o_tok[:, t, c0:c0 + 512].rearrange("p (h d) -> p h d", h=8), o_ps, cb, ALU.mult)\
                               .then_inc(sem(f"pv_out{L}"), 1)
                            last = (what == "dsa") or g >= 2
                            if last:
                                dve.wait_ge(sem(f"pv_out{L}"), grp + 1)
                                dve.engine_nop().then_inc(sem(f"o_ready{L}"), 1)

            def rsqrt(v, scale, eps):
                rs_count[0] += 1
                dve.tensor_scalar(var_eps, v, scale, eps, ALU.mult, ALU.add).then_inc(sem("var_ready"), 1)
                dve.wait_ge(sem("rstd_guess"), rs_count[0])
                seq(dve.tensor_scalar(newton, rstd, rstd, var_eps, ALU.mult, ALU.mult))
                seq(dve.tensor_scalar(newton, newton, -0.5, 1.5, ALU.mult, ALU.add))
                seq(dve.tensor_tensor(rstd, rstd, newton, ALU.mult))

            def layer_norm(L, which, other):
                j = 3 * L + which - 1
                for t in range(NT):
                    for half in range(2):
                        xs = x_tok[:, t, half * PIECE:(half + 1) * PIECE]
                        if which == 1:
                            dve.wait_ge(sem(f"wo_mm{L}"), NT * half + t + 1)
                        seq(dve.scalar_tensor_tensor(xs, xs, ALPHA, other(t, half), ALU.mult, ALU.add))
                        seq(dve.bn_stats(stats[:, t, half, :], xs))
                    seq(dve.bn_aggr(mean_var, stats[:, t, :, :]))
                    rsqrt(mean_var[:, 1:2], 1.0, LN_EPS)
                    seq(dve.tensor_scalar(x_tok[:, t, :], x_tok[:, t, :], mean_var[:, 0:1], rstd, ALU.subtract, ALU.mult))
                    dve.wait_ge(sem("gb_loaded"), 32 * (j + 1))
                    seq(dve.tensor_tensor(x_tok[:, t, :], x_tok[:, t, :], gb_row[:, 0, :], ALU.mult))
                    seq(dve.tensor_tensor(x_tok[:, t, :], x_tok[:, t, :], gb_row[:, 1, :], ALU.add))
                    dve.engine_nop().then_inc(sem(f"ln{which}_out{L}"), 1)
                    dve.engine_nop().then_inc(sem("gb_used"), 1)

            tp = 0
            dve.wait_ge(sem("const_loaded"), 16)
            for L in range(DEPTH):
                copy_T("xT_dve", tp)
                tp += NT
                if L % 2 == 0:
                    for j, (c0, c1) in enumerate(proj_pieces[0]):
                        dve.wait_ge(sem(f"proj_mm{L}"), 2 * j + 2)
                        dve.tensor_copy(proj[:, 1, c0:c1], ps[:, 4 + (2 * j + 1) % 4, 0:c1 - c0])\
                           .then_inc(sem(f"proj_t1_{L}"), 1)
                    dve.wait_ge(sem(f"proj_t0_{L}"), 5)
                    dve.wait_ge(sem(f"proj_t1_{L}"), 5)
                    for groups in (((QA, 8, 0),), ((KA, 1, 8),), ((QI, 9, 10),), ((QB, 8, 20),), ((KS, 1, 28), (KW, 1, 30))):
                        for src, n, dst in groups:
                            for t in range(NT):
                                ins = rope(t, proj[:, t, src:src + n * HD].rearrange("p (n h k) -> p n h k", n=n, h=2), n,
                                           roped[:, t, dst * HD:(dst + n) * HD].rearrange("p (n h k) -> p n h k", n=n, h=2),
                                           const[:, C_COS + 32 * t:C_COS + 32 * t + 32],
                                           const[:, C_SIN + 32 * t:C_SIN + 32 * t + 32])
                                if t == NT - 1 and (src, n, dst) == groups[-1]:
                                    ins.then_inc(sem(f"roped{L}"), 1)
                                else:
                                    seq(ins)
                        dve.wait_ge(sem(f"roped{L}"), 1) if groups[0][0] == QA else None
                    dve.wait_ge(sem(f"roped{L}"), 5)
                    dve.wait_ge(sem("cmp_tp"), 1)
                    seq(dve.tensor_copy(kvT, ps[:, 4, 0:SEQ]))
                    seq(dve.tensor_copy(peT, ps[:, 5, 0:CMP_LEN]))
                    for c in range(N_CMP):
                        ins = dve.tensor_tensor(cmp_blk[:, :, c], kvT[:, c * CMP_STRIDE:c * CMP_STRIDE + CMP_LEN], peT, ALU.add)
                    ins.then_inc(sem("cmp_blk"), 1)
                    dve.wait_ge(sem("cmp_exp"), 1)
                    seq(dve.tensor_scalar(small[0:HD, 160:192], small[0:HD, 160:192], 1.0, None, ALU.add))
                    seq(dve.reciprocal(small[0:HD, 160:192], small[0:HD, 160:192]))
                    dve.tensor_tensor(small[0:HD, 128:128 + N_CMP], ps[0:HD, 6, 0:N_CMP], small[0:HD, 160:160 + N_CMP], ALU.mult)
                    dve.tensor_tensor(small[0:HD, 144:144 + N_CMP], ps[0:HD, 7, 0:N_CMP], small[0:HD, 176:176 + N_CMP], ALU.mult)\
                       .then_inc(sem("cmp_hs"), 1)
                    dve.wait_ge(sem("cmp_kv"), 1)
                    seq(dve.tensor_copy(small[0:N_CMP, 384:448], ps[0:N_CMP, 4, HD:P]))
                    seq(rope(0, ps[0:N_CMP, 4, 0:HD].rearrange("p (n h k) -> p n h k", n=1, h=2), 1,
                             small[0:N_CMP, 256:320].rearrange("p (n h k) -> p n h k", n=1, h=2),
                             const[0:N_CMP, C_CCOS:C_CCOS + 32], const[0:N_CMP, C_CSIN:C_CSIN + 32], rows_=N_CMP,
                             tmp=small[0:N_CMP, 192:224].rearrange("p (n k) -> p n k", n=1)))
                    dve.tensor_copy(small[0:N_CMP, 320:384], small[0:N_CMP, 256:320]).then_inc(sem("cmp_roped"), 1)
                    dve.wait_ge(sem("bias_loaded"), 32)
                    dve.tensor_tensor(gate_sig.rearrange("p (t n) -> p t n", t=NT), proj[:, :, GB:GB + 24],
                                      bgate[:, :].unsqueeze(1).to_broadcast([P, NT, 24]), ALU.add).then_inc(sem("gate_z"), 1)
                    dve.wait_ge(sem("cmp_rep"), 1)
                    dve.tensor_copy(small[:, 448:448 + CMP_PAD], ps[:, 5, 0:CMP_PAD]).then_inc(sem("cmp_kT"), 1)
                    for h in range(HEADS):
                        ins = dve.tensor_scalar(v_bd[:, h * HD:(h + 1) * HD], ps[:, 6, 0:HD],
                                                const[:, C_BD + h:C_BD + h + 1], None, ALU.mult)
                    ins.then_inc(sem("v_bd_dve"), 1)
                    dve.wait_ge(sem("cmp_sc"), 1)
                    for b in range(2):
                        for t in range(NT):
                            sc = cmp_s[:, t, b * 64:(b + 1) * 64].rearrange("p (s c) -> p s c", s=4)
                            ins = dve.scalar_tensor_tensor(
                                sc, ps[:, 4 + b, t * 64:(t + 1) * 64].rearrange("p (s c) -> p s c", s=4), SCALE,
                                const[:, C_CBIAS + t * CMP_PAD:C_CBIAS + (t + 1) * CMP_PAD].unsqueeze(1).to_broadcast([P, 4, CMP_PAD]),
                                ALU.mult, ALU.add)
                    seq(ins)
                    sall = cmp_s.rearrange("p t (s c) -> p (t s) c", s=8)
                    seq(dve.tensor_reduce(cmp_m, sall, AX_X, ALU.max, negate=True))
                    dve.tensor_tensor(sall, sall, cmp_m.unsqueeze(2).to_broadcast([P, 16, CMP_PAD]), ALU.add)\
                       .then_inc(sem("cmp_sub"), 1)
                    dve.wait_ge(sem("cmp_e"), 1)
                    seq(dve.tensor_reduce(cmp_m, sall, AX_X, ALU.add))
                    for t in range(NT):
                        sc = cmp_s[:, t, :].rearrange("p (s c) -> p s c", s=8)
                        dve.tensor_tensor(sc, sc, const[:, C_CVALID + t * CMP_PAD:C_CVALID + (t + 1) * CMP_PAD]
                                          .unsqueeze(1).to_broadcast([P, 8, CMP_PAD]), ALU.mult).then_inc(sem("cmp_p"), 1)
                    dve.wait_ge(sem("gate_e"), 1)
                    seq(dve.tensor_scalar(gate_sig, gate_sig, 1.0, None, ALU.add))
                    seq(dve.reciprocal(gate_sig, gate_sig))
                    seq(dve.reciprocal(cmp_m, cmp_m))
                    for t in range(NT):
                        gate = gate_sig.rearrange("p (t h b) -> p t h b", t=NT, b=3)[:, t, :, 0]
                        seq(dve.tensor_tensor(coef_h.rearrange("p (j b) -> p j b", b=2),
                                              cmp_m[:, 8 * t:8 * t + 8].rearrange("p (b j) -> p j b", b=2),
                                              gate.rearrange("p (j b) -> p j b", b=2), ALU.mult))
                        dve.wait_ge(sem("cmp_o"), 1)
                        dve.tensor_tensor(o_tok[:, t, 512:1024].rearrange("p (h d) -> p h d", h=8),
                                          ps[:, 6 + t, :].rearrange("p (h d) -> p h d", h=8),
                                          coef_h.unsqueeze(2).to_broadcast([P, 8, HD]), ALU.mult).then_inc(sem("cmp_out"), 1)
                        dve.wait_ge(sem("cmp_out"), t + 1)
                    for n in range(NT * HEADS):
                        t, h = n // HEADS, n % HEADS
                        K = n_keys(t)
                        dve.wait_ge(sem("idx_relu"), n + 1)
                        w = proj[:, t, WI + h:WI + h + 1]
                        if h == 0:
                            ins = dve.tensor_scalar(selbias[:, t, 0:K], relu_buf[:, n % 2, 0:K], w, None, ALU.mult)
                        else:
                            ins = dve.scalar_tensor_tensor(selbias[:, t, 0:K], relu_buf[:, n % 2, 0:K], w,
                                                           selbias[:, t, 0:K], ALU.mult, ALU.add)
                        ins.then_inc(sem("idx_acc"), 1)
                        dve.wait_ge(sem("idx_acc"), n + 1)
                    for t in range(NT):
                        K = n_keys(t)
                        s = selbias[:, t, 0:K]
                        causal = const[:, C_CAUSAL + SEQ - K:C_CAUSAL + SEQ]
                        seq(dve.scalar_tensor_tensor(s, s, IDX_SCALE, causal, ALU.mult, ALU.add))
                        for _ in range(TOPK_KEYS // 8):
                            seq(dve.max(best8, s))
                            seq(dve.match_replace(s, best8, s, TAKEN))
                        seq(dve.tensor_scalar(s, s, TAKEN, 1.0, ALU.is_equal, ALU.subtract))
                        seq(dve.scalar_tensor_tensor(s, s, -NEG, causal, ALU.mult, ALU.add))
                else:
                    for t in range(NT):
                        dve.wait_ge(sem(f"proj_mm{L}"), t + 1)
                    z = fox_zb
                    dve.tensor_tensor(z.rearrange("p (t n) -> p t n", t=NT), ps[:, 6, 0:NT * FOX_HEADS].rearrange("p (t n) -> p t n", t=NT),
                                          fox_b[:, :].unsqueeze(1).to_broadcast([P, NT, FOX_HEADS]), ALU.add)\
                       .then_inc(sem("fox_z"), 1)
                    dve.wait_ge(sem("fox_abs"), 1)
                    seq(dve.tensor_scalar(z, z, 0.0, None, ALU.min))
                    dve.wait_ge(sem("fox_ln"), 1)
                    dve.tensor_tensor(logf.rearrange("p t n -> p (t n)"), z, fox_t, ALU.subtract).then_inc(sem("logf"), 1)
                    for j in range(4):
                        dve.wait_ge(sem(f"proj_mm{L}"), NT + 2 * j + 2)
                        dve.tensor_copy(qkT[:, 4 * j + 2:4 * j + 4, :], ps[:, (2 * j + 1) % 4, :].rearrange("p (b n) -> p b n", b=2))\
                           .then_inc(sem(f"proj_t1_{L}"), 1)
                    dve.memset(aug_d, 1.0)
                    seq(dve.memset(aug_k, 1.0))
                    dve.wait_ge(sem("dcum"), 1)
                    for r0, dst in ((0, aug_d), (64, aug_d), (32, aug_k), (96, aug_k)):
                        ins = dve.tensor_scalar(dst[r0:r0 + FOX_HEADS], ps[0:FOX_HEADS, 7, 0:SEQ], 1.0 / SCALE, None, ALU.mult)
                    seq(ins)
                    dve.tensor_tensor(aug_q, aug_d.unsqueeze(1).to_broadcast([P, 8, SEQ]),
                                      const[:, C_DELTA:C_DELTA + 8].unsqueeze(2).to_broadcast([P, 8, SEQ]), ALU.mult)\
                       .then_inc(sem("aug"), 1)
                    for j in range(2):
                        dve.wait_ge(sem(f"proj_mm{L}"), NT + 8 + 2 * j + 2)
                        dve.tensor_copy(v_fox[:, 1, j * PIECE:(j + 1) * PIECE], ps[:, 2 * j + 1, :])\
                           .then_inc(sem(f"proj_t1_{L}"), 1)
                attention(L)
                copy_T("oT_dve", tp)
                tp += NT
                layer_norm(L, 1, lambda t, half: ps[:, 4 + 2 * t + half, :])
                copy_T("xT_dve", tp)
                tp += NT

                dve.wait_ge(sem("layer_loaded"), 48 * (L + 1))
                for t in range(NT):
                    s = sig[:, t, :]
                    dve.wait_ge(sem("router_e"), NT * L + t + 1)
                    seq(dve.tensor_scalar(s, s, 1.0, None, ALU.add))
                    seq(dve.reciprocal(s, s))
                    seq(dve.tensor_tensor(sb_, s, router_b[:, :], ALU.add))
                    for g in range(N_GROUPS):
                        ins = dve.max(gmax[:, g, :], sb_[:, g * 8:(g + 1) * 8])
                    seq(ins)
                    seq(dve.tensor_tensor(gscore, gmax[:, :, 0], gmax[:, :, 1], ALU.add))
                    seq(dve.max(best8, gscore))
                    seq(dve.memset(best8[:, TOP_GROUPS:8], -TAKEN))
                    seq(dve.match_replace(gscore, best8, gscore, TAKEN))
                    seq(dve.tensor_scalar(gscore, gscore, TAKEN, 1.0, ALU.is_equal, ALU.subtract))
                    gm = gscore.unsqueeze(2).to_broadcast([P, 8, 8])
                    seq(dve.tensor_scalar(gmask0, gscore, 1.0, None, ALU.add))
                    g0 = gmask0.unsqueeze(2).to_broadcast([P, 8, 8])
                    sb3 = sb_.rearrange("p (g e) -> p g e", g=8)
                    seq(dve.tensor_tensor(sb3, sb3, g0, ALU.mult))
                    seq(dve.scalar_tensor_tensor(sb3, gm, -NEG, sb3, ALU.mult, ALU.add))
                    seq(dve.max(best8, sb_))
                    seq(dve.match_replace(sb_, best8, sb_, TAKEN))
                    seq(dve.tensor_scalar(sb_, sb_, TAKEN, None, ALU.is_equal))
                    g1 = gates[:, t, 1:1 + NE]
                    seq(dve.tensor_tensor(g1, s, sb_, ALU.mult))
                    seq(dve.tensor_reduce(rstd, g1, AX_X, ALU.add))
                    seq(dve.reciprocal(rstd, rstd))
                    seq(dve.tensor_scalar(g1, g1, rstd, ROUTED_SCALE, ALU.mult, ALU.mult))
                    seq(dve.memset(gates[:, t, 0:1], 1.0))
                    dve.memset(y_acc[:, t, :], 0.0).then_inc(sem(f"router_dve{L}"), 1)
                dve.wait_ge(sem(f"router_dve{L}"), NT)

                base = L * (NE + 1)

                def gate_h(n, par, first=False):
                    dve.wait_ge(sem("moe_silu"), n + 1)
                    if not first:
                        dve.wait_ge(sem("moe_down"), n - 1)
                    dve.tensor_tensor(h_gated[:, par, :], h_silu[:, par, :], ps[:, 5 + 2 * par, :], ALU.mult)\
                       .then_inc(sem("moe_h"), 1)

                def add_y(n, col):
                    dve.wait_ge(sem("moe_down"), n + 1)
                    if not isinstance(n, int) or n >= 1:
                        dve.wait_ge(sem("moe_added"), n)
                    for t in range(NT):
                        ins = dve.scalar_tensor_tensor(y_acc[:, t, :], ps[:, 2 * t:2 * t + 2, :].rearrange("p b n -> p (b n)"), gates[:, t, col],
                                                       y_acc[:, t, :], ALU.mult, ALU.add)
                    ins.then_inc(sem("moe_added"), 1)

                gate_h(base, 0, first=True)
                gate_h(base + 1, 1, first=(base == 0))
                with dve.Fori(0, NE // UNROLL - 1) as i:
                    for u in range(UNROLL):
                        add_y(i * UNROLL + (base + u), bass.ds(i * UNROLL + u, 1))
                        gate_h(i * UNROLL + (base + 2 + u), u % 2)
                for u in range(UNROLL - 1):
                    n = NE - UNROLL + u
                    add_y(base + n, slice(n, n + 1))
                    gate_h(base + n + 2, u % 2)
                for n in (NE - 1, NE):
                    add_y(base + n, slice(n, n + 1))
                dve.wait_ge(sem("moe_added"), base + NE + 1)
                layer_norm(L, 2, lambda t, half: y_acc[:, t, half * PIECE:(half + 1) * PIECE])
                copy_T("xT_dve", tp)
                tp += NT

                for t in range(NT):
                    dve.wait_ge(sem(f"ple_sq{L}"), t + 1)
                    rsqrt(ple_ss[:, t:t + 1], 1.0 / D, RMS_EPS)
                    dve.wait_ge(sem("gb_loaded"), 32 * (3 * L + 3))
                    seq(dve.scalar_tensor_tensor(y_acc[:, t, :], ps[:, 4 + 2 * t:6 + 2 * t, :].rearrange("p b n -> p (b n)"),
                                                 rstd, gb_row[:, 0, :], ALU.mult, ALU.mult))
                    dve.engine_nop().then_inc(sem("gb_used"), 1)
                for t in range(NT):
                    dve.wait_ge(sem(f"ple_sig{L}"), t + 1)
                    seq(dve.tensor_tensor(y_acc[:, t, :], y_acc[:, t, :], roped[:, t, 0:D], ALU.mult))
                    seq(dve.tensor_tensor(x_tok[:, t, :], x_tok[:, t, :], y_acc[:, t, :], ALU.add))
                    dve.engine_nop().then_inc(sem(f"ple_out{L}"), 1)


_INS = ['x', 'p', 'ev_w_in', 'ev_b_gate', 'ev_cmp_pos_k', 'ev_cmp_w1_k', 'ev_cmp_w2_k', 'ev_cmp_pos_v',
        'ev_cmp_w1_v', 'ev_cmp_w2_v', 'ev_w_o', 'od_w_in', 'od_b_f', 'od_w_o', 'ln1_g', 'ln1_b', 'ln2_g', 'ln2_b',
        'router_w', 'router_bias', 'exp_w1', 'exp_w3', 'exp_w2', 'sh_w1', 'sh_w3', 'sh_w2', 'ple_w_gate',
        'ple_w_proj', 'ple_norm_g']


def kernel(**inputs):
    import numpy as _np
    import concourse.bacc as _bacc
    from concourse import mybir as _mybir
    from concourse.bass_utils import run_bass_kernel_spmd as _run

    nc = _bacc.Bacc("TRN2", target_bir_lowering=False, num_devices=1)
    arrays, aps = {}, {}
    for name in _INS + ["const"]:
        v = constant_table() if name == "const" else _np.ascontiguousarray(inputs[name])
        arrays[f"in_{name}_dram"] = v
        aps[name] = nc.dram_tensor(f"in_{name}_dram", v.shape, _mybir.dt.from_np(v.dtype), kind="ExternalInput").ap()
    out = nc.dram_tensor("out_0_dram", (1, SEQ, D), _mybir.dt.float32, kind="ExternalOutput").ap()
    build_trunk(nc, aps, out)
    r = _run(nc, [arrays], core_ids=[0])
    return r.results[0]["out_0_dram"]
```

```python
from contextlib import ExitStack

import numpy as np
import concourse.bass as bass
from concourse import mybir

ALU = mybir.AluOpType
ACT = mybir.ActivationFunctionType
F32 = mybir.dt.float32
AX_X = mybir.AxisListType.X

P = 128
D = 1024
DC = D // P
SEQ = 256
NT = SEQ // P
DEPTH = 2
HD = 64
PLE = 256
LN_EPS = 1e-5
RMS_EPS = 1e-6
NEG = -1e30
TAKEN = -3e38
ALPHA = (2.0 * DEPTH) ** 0.25
SCALE = HD ** -0.5

HEADS = 8
FOX_HEADS = 16
IDX_SCALE = (8 * 64) ** -0.5
TOPK_KEYS = 64
CMP_LEN = 32
CMP_STRIDE = 16
N_CMP = (SEQ - CMP_LEN) // CMP_STRIDE + 1
CMP_PAD = 16

NE = 64
TOP_E = 8
N_GROUPS = 8
TOP_GROUPS = 4
FE = 256
ROUTED_SCALE = 2.5

QA, KA, VA, QI, KI, WI, QB, KC, VC, KS, VS, KW, VW, GB = (
    0, 512, 576, 640, 1152, 1216, 1224, 1736, 1800, 1864, 1928, 1992, 2056, 2120)
EVEN_COLS = 2144
ODD_COLS = 3 * D + FOX_HEADS

SLOTS = 64
PAIRS = NE // 2
RING = 4
SLOT = 6144
PIECE = 512
UNROLL = 4

C_ID = 0
C_CAUSAL = C_ID + P
C_TRI = C_CAUSAL + SEQ
C_COS = C_TRI + 2 * SEQ
C_SIN = C_COS + NT * 32
C_CCOS = C_SIN + NT * 32
C_CSIN = C_CCOS + 32
C_CBIAS = C_CSIN + 32
C_CVALID = C_CBIAS + NT * CMP_PAD
C_REP = C_CVALID + NT * CMP_PAD
C_BD = C_REP + P
C_DELTA = C_BD + HEADS
C_IOTA = C_DELTA + FOX_HEADS // 2
C_END = C_IOTA + SLOTS


def slot_head(s):
    return 2 * (s % 4) + s // 4


def constant_table():
    t = np.zeros((P, C_END), np.float32)
    r = np.arange(P)
    t[:, C_ID:C_ID + P] = np.eye(P)
    t[:, C_CAUSAL + P:C_CAUSAL + SEQ] = np.where(r[None, :] > r[:, None], NEG, 0.0)
    for c in range(NT):
        tok, pos = c * P + r, np.arange(SEQ)
        t[:, C_TRI + c * SEQ:C_TRI + (c + 1) * SEQ] = tok[:, None] <= pos[None, :]
    inv = 1.0 / (10000.0 ** (np.arange(0, HD, 2, dtype=np.float32) / HD))
    ang = np.arange(SEQ, dtype=np.float32)[:, None] * inv.astype(np.float32)[None, :]
    cos, sin = np.cos(ang), np.sin(ang)
    last = np.arange(N_CMP) * CMP_STRIDE + CMP_LEN - 1
    for c in range(NT):
        t[:, C_COS + 32 * c:C_COS + 32 * c + 32] = cos[c * P:(c + 1) * P]
        t[:, C_SIN + 32 * c:C_SIN + 32 * c + 32] = sin[c * P:(c + 1) * P]
        ok = np.zeros((P, CMP_PAD), bool)
        ok[:, :N_CMP] = last[None, :] <= (c * P + r)[:, None]
        t[:, C_CBIAS + CMP_PAD * c:C_CBIAS + CMP_PAD * (c + 1)] = np.where(ok, 0.0, NEG)
        t[:, C_CVALID + CMP_PAD * c:C_CVALID + CMP_PAD * (c + 1)] = ok
    t[:N_CMP, C_CCOS:C_CCOS + 32] = cos[last]
    t[:N_CMP, C_CSIN:C_CSIN + 32] = sin[last]
    for c in range(CMP_PAD):
        t[c, C_REP + c:C_REP + P:CMP_PAD] = 1.0
    for s in range(HEADS):
        t[s * CMP_PAD:(s + 1) * CMP_PAD, C_BD + slot_head(s)] = 1.0
    for h in range(FOX_HEADS):
        t[64 * (h % 2) + h, C_DELTA + h // 2] = 1.0
        t[64 * (h % 2) + 32 + h, C_DELTA + h // 2] = -1.0
    t[:, C_IOTA:C_IOTA + SLOTS] = np.arange(SLOTS)
    return t


def build_trunk(nc, a, out):
    with ExitStack() as ctx:
        def sb(name, *shape):
            return ctx.enter_context(nc.sbuf_tensor(name, [P, *shape], F32))

        sems = {}

        def sem(name):
            if name not in sems:
                sems[name] = ctx.enter_context(nc.semaphore(name))
            return sems[name]

        ps = ctx.enter_context(nc.psum_tensor("ps", [P, 8, 512], F32))

        ring = sb("ring", RING, SLOT)
        const = sb("const", C_END)
        x_tok = sb("x_tok", NT, D)
        xT = sb("xT", DC, SEQ)
        proj = sb("proj", NT, EVEN_COLS)
        qkT = sb("qkT", 17, SEQ)
        roped = sb("roped", NT, 2048)
        pT = sb("pT", 2, 1024)
        o_tok = sb("o_tok", NT, D)
        gb_row = sb("gb_row", 2, D)
        router_w = sb("router_w", DC, NE)
        router_b = sb("router_b", NE)
        p_tok = sb("p_tok", NT, PLE)
        bgate = sb("bgate", 24)
        fox_b = sb("fox_b", FOX_HEADS)
        small = sb("small", 1024)
        stats = sb("stats", NT, 2, 6)
        selbias = sb("selbias", NT, SEQ)
        gates = sb("gates", NT, NE)

        rows = sb("rows", 512)
        over_int = ctx.enter_context(nc.sbuf_tensor("over_int", [P, 1], mybir.dt.int32))[:, :]

        scores = roped[:, :, :].rearrange("p t n -> p (t n)").rearrange("p (u n) -> p u n", u=4)
        cmp_w1 = o_tok[:, :, :].rearrange("p t n -> p (t n)").rearrange("p (l f) -> p l f", l=CMP_LEN)
        h_silu_all = roped[:, 0, 0:512]
        h_all = roped[:, 0, 512:1024]
        y_acc = o_tok

        cmp_blk = selbias[:, :, :].rearrange("p t n -> p (t n)")[:, 0:CMP_LEN * N_CMP].rearrange("p (l c) -> p l c", l=CMP_LEN)
        cmp_s = small[:, 512:768].rearrange("p (t n) -> p t n", t=NT)
        small_pT = small[:, 768:1024].rearrange("p (t n) -> p t n", t=NT)
        v_bd = pT[:, 0, 0:512]
        v_fox = proj[:, :, :].rearrange("p t n -> p (t n)")[:, 0:NT * D].rearrange("p (t n) -> p t n", t=NT)
        logf = small[:, 64:64 + NT * FOX_HEADS].rearrange("p (t n) -> p t n", t=NT)
        aug_k = small[:, 256:512]
        proj_flat = proj[:, :, :].rearrange("p t n -> p (t n)")
        aug_q = proj_flat[:, NT * D:NT * D + 8 * SEQ].rearrange("p (h n) -> p h n", h=8)
        aug_d = small[:, 512:768]
        y_pair = proj_flat[:, 0:1024]
        xe = proj_flat[:, 1024:3072].rearrange("p (b c n) -> p b c n", b=2, c=DC)
        sel = proj_flat[:, 3072:3584].rearrange("p (b t n) -> p b t n", b=2, t=NT)
        hT = proj_flat[:, 3584:3840].rearrange("p (f n) -> p f n", f=2)
        selT = roped[:, 0, 1024:1536].rearrange("p (b n) -> p b n", b=2)
        h_silu = roped[:, 0, 1536:1792]
        h_exp = roped[:, 0, 1792:2048]
        slot_gate = rows[:, 492:494]
        chosen = roped[:, 1, 0:128].rearrange("p (t n) -> p t n", t=NT)
        place = roped[:, 1, 128:256].rearrange("p (t n) -> p t n", t=NT)
        gates_over = roped[:, 1, 256:384].rearrange("p (t n) -> p t n", t=NT)
        over_row = rows[:, 490:491]
        over_all = rows[:, 491:492]
        ple_pT = pT[:, 0, 0:512].rearrange("p (c n) -> p c n", c=2)

        relu_buf = pT[:, 1, 0:512].rearrange("p (b n) -> p b n", b=2)
        neg_max = rows[:, 0:8].rearrange("p (u s) -> p u s", u=2)
        denom = rows[:, 8:24].rearrange("p (u s) -> p u s", u=2)
        coef = rows[:, 24:32]
        coef_h = rows[:, 32:40]
        mean_var = rows[:, 40:42]
        rstd = rows[:, 42:43]
        ple_ss = rows[:, 43:45]
        best8 = rows[:, 48:56]
        gscore = rows[:, 56:64]
        gmask0 = rows[:, 64:72]
        gmax = rows[:, 72:136].rearrange("p (g e) -> p g e", g=8)
        gate_sig = rows[:, 136:184]
        cmp_m = rows[:, 184:200]
        fox_t = rows[:, 200:232]
        fox_zb = rows[:, 232:264]
        sb_ = rows[:, 264:328]
        sig = rows[:, 328:456].rearrange("p (t n) -> p t n", t=NT)
        peT = rows[:, 456:488]
        var_eps = rows[:, 488:489]
        newton = rows[:, 489:490]
        kvT = small[:, 512:768]
        tmp_o = sb("tmp_o", 512)[:, :]
        o_tok_tmp = tmp_o

        ident = const[:, C_ID:C_ID + P]
        block = ctx.enter_context(nc.Block())

        items = []

        def static_item(parts, release):
            items.append((parts, release))

        def piece(w, c0, c1):
            n = c1 - c0
            return ((0, DC * n), (DC, n), w.rearrange("(p c) n -> p c n", c=DC)[:, :, c0:c1])

        proj_pieces = {
            0: [(c, min(c + PIECE, EVEN_COLS)) for c in range(0, EVEN_COLS, PIECE)],
            1: [(3 * D, ODD_COLS)] + [(c, c + PIECE) for c in range(0, 3 * D, PIECE)],
        }
        first_item = {}
        shared_item = {}
        for L in range(DEPTH):
            w_in = a["ev_w_in"][0] if L % 2 == 0 else a["od_w_in"][0]
            w_o = a["ev_w_o"][0] if L % 2 == 0 else a["od_w_o"][0]
            first_item[L] = len(items)
            for n, (c0, c1) in enumerate(proj_pieces[L % 2]):
                static_item([piece(w_in, c0, c1)], ("proj_mm", L, n))
            for n in range(2):
                static_item([piece(w_o, n * PIECE, (n + 1) * PIECE)], ("wo_mm", L, n))
            shared_item[L] = len(items)
            items.append(("shared", ("shared_down", L, 0)))
            for e in range(NE):
                items.append(("expert", ("exp_down", L, e)))
            static_item([((0, 2 * D), (2, D), a["ple_w_proj"][L].rearrange("(p c) n -> p c n", c=2))], ("ple_mm", L, 0))
            for n in range(2):
                static_item([piece(a["ple_w_gate"][L], n * PIECE, (n + 1) * PIECE)], ("ple_mm", L, 1 + n))

        def release_value(rel):
            what, L, n = rel
            if what == "proj_mm":
                return sem(f"proj_mm{L}"), NT * (n + 1)
            if what == "wo_mm":
                return sem(f"wo_mm{L}"), NT * (n + 1)
            if what == "shared_down":
                return sem("shared_down"), L + 1
            if what == "exp_down":
                return sem("exp_down"), L * PAIRS + n // 2 + 1
            return sem(f"ple_mm{L}"), NT * (n + 1)

        loaded = []
        total = [0] * RING
        for k, (parts, _) in enumerate(items):
            total[k % RING] += 16 * (3 if parts in ("shared", "expert") else len(parts))
            loaded.append(total[k % RING])
        w_loaded = [sem(f"w_loaded{s}") for s in range(RING)]

        def slot_view(k, n, c):
            return ring[:, k % RING, 0:c * n].rearrange("p (c n) -> p c n", c=c)

        def wait_item(eng, k):
            eng.wait_ge(w_loaded[k % RING], loaded[k])

        UP_N = DC * FE
        DOWN0 = 2 * UP_N

        def ffn_views(slot):
            w1 = ring[:, slot, 0:UP_N].rearrange("p (c f) -> p c f", c=DC)
            w3 = ring[:, slot, UP_N:2 * UP_N].rearrange("p (c f) -> p c f", c=DC)
            w2 = ring[:, slot, DOWN0:DOWN0 + 2 * D].rearrange("p (c n) -> p c n", c=2)
            return w1, w3, w2

        @block.sync
        def _(sp):
            rows_of = "(p c) f -> p (c f)"

            def up_load(slot, w1, w3):
                sp.dma_start(ring[:, slot, 0:UP_N], w1.rearrange(rows_of, c=DC)).then_inc(w_loaded[slot], 16)
                sp.dma_start(ring[:, slot, UP_N:2 * UP_N], w3.rearrange(rows_of, c=DC)).then_inc(w_loaded[slot], 16)

            def down_load(slot, w2):
                sp.dma_start(ring[:, slot, DOWN0:DOWN0 + 2 * D], w2.rearrange(rows_of, c=2)).then_inc(w_loaded[slot], 16)

            def ffn_load(slot, w1, w3, w2):
                up_load(slot, w1, w3)
                down_load(slot, w2)

            def over_load(L, e):
                up = rows_of
                done = sem(f"over_loaded{L}")
                sp.dma_start(ring[:, 0, 0:UP_N], a["exp_w1"][L, e].rearrange(up, c=DC)).then_inc(done, 16)
                sp.dma_start(ring[:, 0, UP_N:2 * UP_N], a["exp_w3"][L, e].rearrange(up, c=DC)).then_inc(done, 16)
                sp.dma_start(ring[:, 0, DOWN0:DOWN0 + 2 * D], a["exp_w2"][L, e].rearrange(up, c=2)).then_inc(done, 16)

            sp.dma_start(x_tok[:, :, :], a["x"][0].rearrange("(t p) n -> p t n", p=P)).then_inc(sem("x_loaded"), 16)
            sp.dma_start(const[:, :], a["const"]).then_inc(sem("const_loaded"), 16)
            for L in range(DEPTH):
                k = first_item[L]
                e0 = shared_item[L] + 1
                end = e0 + NE + 3
                while k < end:
                    if k == e0 + UNROLL:
                        with sp.Fori(1, NE // UNROLL) as i:
                            for u in range(0, UNROLL, 2):
                                sp.wait_ge(sem("exp_up"), i * 2 + (L * PAIRS + u // 2 - 1))
                                for v in (u, u + 1):
                                    up_load((e0 + v) % RING, a["exp_w1"][L, i * UNROLL + v], a["exp_w3"][L, i * UNROLL + v])
                                sp.wait_ge(sem("exp_down"), i * 2 + (L * PAIRS + u // 2 - 1))
                                for v in (u, u + 1):
                                    down_load((e0 + v) % RING, a["exp_w2"][L, i * UNROLL + v])
                        k = e0 + NE
                        sp.wait_ge(sem("over_flag"), L + 1)
                        flag = sp.value_load(over_int[0:1, 0:1], min_val=0, max_val=1)
                        with sp.If(flag > 0):
                            sp.wait_ge(sem("exp_down"), (L + 1) * PAIRS)
                            over_load(L, 0)
                            with sp.Fori(1, NE) as e:
                                sp.wait_ge(sem(f"over_added{L}"), e)
                                over_load(L, e)
                            sp.wait_ge(sem(f"over_added{L}"), NE)
                        continue
                    if k >= RING:
                        sp.wait_ge(*release_value(items[k - RING][1]))
                    parts = items[k][0]
                    if parts == "shared":
                        ffn_load(k % RING, a["sh_w1"][L], a["sh_w3"][L], a["sh_w2"][L])
                    elif parts == "expert":
                        e = k - e0
                        ffn_load(k % RING, a["exp_w1"][L, e], a["exp_w3"][L, e], a["exp_w2"][L, e])
                    else:
                        for (lo, hi), (c, n), src in parts:
                            sp.dma_start(slot_view(k, n, c), src).then_inc(w_loaded[k % RING], 16)
                    k += 1
            for t in range(NT):
                sp.wait_ge(sem(f"ple_out{DEPTH - 1}"), t + 1)
                sp.dma_start(out[0, t * P:(t + 1) * P, :], x_tok[:, t, :]).then_inc(sem("out_stored"), 16)
            sp.wait_ge(sem("out_stored"), 16 * NT)

        @block.gpsimd
        def _(pool):
            pool.memset(small[:, 0:1024], 0.0).then_inc(sem("small_zero"), 1)
            pool.dma_start(bgate[:, :], a["ev_b_gate"][0].partition_broadcast(P)).then_inc(sem("bias_loaded"), 16)
            pool.dma_start(fox_b[:, :], a["od_b_f"][0].partition_broadcast(P)).then_inc(sem("bias_loaded"), 16)
            pe_t = qkT[:, 16, 0:2 * HD]
            pool.dma_start(pe_t[0:CMP_LEN, 0:HD], a["ev_cmp_pos_k"][0]).then_inc(sem("cmp_loaded"), 16)
            pool.dma_start(pe_t[0:CMP_LEN, HD:2 * HD], a["ev_cmp_pos_v"][0]).then_inc(sem("cmp_loaded"), 16)
            pool.dma_start(cmp_w1[0:HD], a["ev_cmp_w1_k"][0].rearrange("(l d) f -> d l f", d=HD)).then_inc(sem("cmp_loaded"), 16)
            pool.dma_start(cmp_w1[HD:P], a["ev_cmp_w1_v"][0].rearrange("(l d) f -> d l f", d=HD)).then_inc(sem("cmp_loaded"), 16)
            pool.wait_ge(sem("small_zero"), 1)
            pool.dma_start(small[0:HD, 0:HD], a["ev_cmp_w2_k"][0]).then_inc(sem("cmp_loaded"), 16)
            pool.dma_start(small[0:HD, HD:2 * HD], a["ev_cmp_w2_v"][0]).then_inc(sem("cmp_loaded"), 16)
            for L in range(DEPTH):
                if L:
                    pool.wait_ge(sem(f"router_mm{L - 1}"), NT)
                    pool.wait_ge(sem(f"router_dve{L - 1}"), NT)
                    pool.wait_ge(sem(f"pT_tp{L - 1}"), NT)
                pool.dma_start(router_w[:, :, :], a["router_w"][L].rearrange("(p c) n -> p c n", c=DC)).then_inc(sem("layer_loaded"), 16)
                pool.dma_start(router_b[:, :], a["router_bias"][L].partition_broadcast(P)).then_inc(sem("layer_loaded"), 16)
                pool.dma_start(p_tok[:, :, :], a["p"][L, 0].rearrange("(t p) n -> p t n", p=P)).then_inc(sem("layer_loaded"), 16)
                for n, (g, b) in enumerate((("ln1_g", "ln1_b"), ("ln2_g", "ln2_b"), ("ple_norm_g", None))):
                    if n == 1:
                        pool.wait_ge(sem("place_max"), L + 1)
                        pool.partition_all_reduce(over_all, over_row, P, bass.bass_isa.ReduceOp.max).then_inc(sem("place_all"), 1)
                    if 3 * L + n:
                        pool.wait_ge(sem("gb_used"), NT * (3 * L + n))
                    pool.dma_start(gb_row[:, 0, :], a[g][L].partition_broadcast(P)).then_inc(sem("gb_loaded"), 16)
                    pool.dma_start(gb_row[:, 1, :], a[b or g][L].partition_broadcast(P)).then_inc(sem("gb_loaded"), 16)

        UNITS = {0: [("sel", t, g) for t in range(NT) for g in range(2)]
                 + [("win", t, g) for t in range(NT) for g in range(2)]
                 + [("dsa", t, g) for t in range(NT) for g in range(2)],
                 1: [("fox", t, g) for t in range(NT) for g in range(4)]}
        BRANCH = {"sel": (20, 28, VS), "win": (20, 30, VW), "dsa": (0, 8, VA)}

        def n_keys(t):
            return (t + 1) * P

        def unit_slots(g):
            return [4 * g + 2 * j + parity for parity in range(2) for j in range(2)]

        @block.tensor
        def _(pe):
            def transpose_x(j, src, ready):
                for t in range(NT):
                    ready(t)
                    for c in range(DC):
                        ins = pe.transpose(ps[:, 2 * t + c // 4, (c % 4) * P:(c % 4 + 1) * P],
                                           src[:, t, c::DC], ident)
                    ins.then_inc(sem("xT_tp"), 1)

            def wait_xT(j):
                pe.wait_ge(sem("xT_act"), NT * (j + 1))
                pe.wait_ge(sem("xT_dve"), NT * (j + 1))

            def attention(L):
                units = UNITS[L % 2]
                for u in range(len(units) + 2):
                    if u < len(units):
                        what, t, g = units[u]
                        K = n_keys(t)
                        if u >= 2:
                            pe.wait_ge(sem(f"sc_biased{L}"), u - 1)
                        for s, h in enumerate(unit_slots(g)):
                            o = ps[:, 2 * (u % 2) + s // 2, (s % 2) * K:(s % 2 + 1) * K]
                            r = slice(HD * (h % 2), HD * (h % 2) + HD)
                            if what == "fox":
                                ra = slice(HD * (h % 2), HD * (h % 2) + 48)
                                ins = pe.matmul(o, qkT[r, h // 2, t * P:(t + 1) * P], qkT[r, 8 + h // 2, 0:K],
                                                start=True, stop=False)
                                ins = pe.matmul(o, aug_q[ra, h // 2, t * P:(t + 1) * P], aug_k[ra, 0:K],
                                                start=False, stop=True)
                            else:
                                q0, k0, _ = BRANCH[what]
                                ins = pe.matmul(o, qkT[r, (q0 + h) // 2, t * P:(t + 1) * P],
                                                qkT[r, k0 // 2, 0:K], start=True, stop=True)
                        ins.then_inc(sem(f"sc_mm{L}"), 1)
                    if 1 <= u <= len(units):
                        v = u - 1
                        what, t, g = units[v]
                        pe.wait_ge(sem(f"sc_exp{L}"), v + 1)
                        if v:
                            pe.wait_ge(sem(f"pT_copied{L}"), v)
                        for s in range(4):
                            for c in range(t + 1):
                                b = s * (t + 1) + c
                                ins = pe.transpose(ps[:, 4 + b // 4, (b % 4) * P:(b % 4 + 1) * P],
                                                   scores[:, v % 2, s * n_keys(t) + c * P:s * n_keys(t) + (c + 1) * P],
                                                   ident)
                        ins.then_inc(sem(f"pT_tp{L}u"), 1)
                    if u >= 2:
                        v = u - 2
                        what, t, g = units[v]
                        pe.wait_ge(sem(f"pT_copied{L}"), v + 1)
                        grp = v // 2
                        if v % 2 == 0 and grp >= 2:
                            pe.wait_ge(sem(f"pv_out{L}"), grp - 1)
                        for s, h in enumerate(unit_slots(g)):
                            hh = h % 8
                            for c in range(t + 1):
                                vals = (v_fox[:, c, h * HD:(h + 1) * HD] if what == "fox"
                                        else proj[:, c, BRANCH[what][2]:BRANCH[what][2] + HD])
                                ins = pe.matmul(ps[:, 6 + grp % 2, hh * HD:(hh + 1) * HD],
                                                pT[:, v % 2, (s * (t + 1) + c) * P:(s * (t + 1) + c + 1) * P],
                                                vals, start=(c == 0), stop=(c == t))
                        ins.then_inc(sem(f"pv_mm{L}"), 1)

            pe.wait_ge(sem("const_loaded"), 16)
            for L in range(DEPTH):
                if L == 0:
                    def ready(t):
                        pe.wait_ge(sem("x_loaded"), 16)
                else:
                    def ready(t, L=L):
                        pe.wait_ge(sem(f"ple_out{L - 1}"), t + 1)
                transpose_x(3 * L, x_tok, ready)
                wait_xT(3 * L)
                n = 0
                if L % 2 == 0:
                    for j, (c0, c1) in enumerate(proj_pieces[0]):
                        k = first_item[L] + j
                        wait_item(pe, k)
                        w = slot_view(k, c1 - c0, DC)
                        for t in range(NT):
                            if j >= 2:
                                pe.wait_ge(sem(f"proj_t{t}_{L}"), j - 1)
                            for c in range(DC):
                                ins = pe.matmul(ps[:, 4 + (2 * j + t) % 4, 0:c1 - c0], xT[:, c, t * P:(t + 1) * P],
                                                w[:, c, :], start=(c == 0), stop=(c == DC - 1))
                            ins.then_inc(sem(f"proj_mm{L}"), 1)
                    for m in range(4):
                        pe.wait_ge(sem(f"roped{L}"), (1, 3, 4, 5)[m])
                        pe.wait_ge(sem(f"dup{L}"), (0, 2, 2, 4)[m]) if m else None
                        if m >= 2:
                            pe.wait_ge(sem(f"qkT_copied{L}"), m - 1)
                        for b in range(4):
                            for t in range(NT):
                                ins = pe.transpose(ps[:, 2 * (m % 2) + b // 2, (b % 2) * SEQ + t * P:(b % 2) * SEQ + (t + 1) * P],
                                                   roped[:, t, (4 * m + b) * P:(4 * m + b + 1) * P], ident)
                        ins.then_inc(sem(f"qkT_tp{L}"), 1)
                    pe.wait_ge(sem(f"proj_t0_{L}"), 5)
                    pe.wait_ge(sem(f"proj_t1_{L}"), 5)
                    for t in range(NT):
                        pe.transpose(ps[:, 4, t * P:(t + 1) * P], proj[:, t, KC:KC + P], ident)
                    pe.wait_ge(sem("cmp_loaded"), 96)
                    pe.transpose(ps[:, 5, 0:CMP_LEN], qkT[0:CMP_LEN, 16, 0:P], ident[0:CMP_LEN, 0:CMP_LEN])\
                        .then_inc(sem("cmp_tp"), 1)
                    pe.wait_ge(sem("cmp_blk"), 1)
                    for half in range(2):
                        r = slice(HD * half, HD * half + HD)
                        for l in range(CMP_LEN):
                            ins = pe.matmul(ps[0:HD, 6 + half, 0:N_CMP], cmp_w1[r, l, :],
                                            cmp_blk[r, l, :], start=(l == 0), stop=(l == CMP_LEN - 1))
                    ins.then_inc(sem("cmp_h"), 1)
                    pe.wait_ge(sem("cmp_hs"), 1)
                    for half in range(2):
                        ins = pe.matmul(ps[0:N_CMP, 4, half * HD:(half + 1) * HD],
                                        small[0:HD, 128 + 16 * half:128 + 16 * half + N_CMP],
                                        small[0:HD, half * HD:(half + 1) * HD], start=True, stop=True)
                    ins.then_inc(sem("cmp_kv"), 1)
                    pe.wait_ge(sem("cmp_roped"), 1)
                    pe.transpose(ps[:, 5, 0:CMP_PAD], small[0:CMP_PAD, 256:384], ident[0:CMP_PAD, 0:CMP_PAD])
                    pe.matmul(ps[:, 6, 0:HD], const[0:CMP_PAD, C_REP:C_REP + P], small[0:CMP_PAD, 384:448],
                              start=True, stop=True).then_inc(sem("cmp_rep"), 1)
                    pe.wait_ge(sem("cmp_kT"), 1)
                    pe.wait_ge(sem(f"qkT_copied{L}"), 4)
                    for t in range(NT):
                        for h in range(HEADS):
                            r = slice(HD * (h % 2), HD * (h % 2) + HD)
                            c0 = t * 64 + (h // 2) * CMP_PAD
                            ins = pe.matmul(ps[:, 4 + h % 2, c0:c0 + CMP_PAD], qkT[r, (20 + h) // 2, t * P:(t + 1) * P],
                                            small[r, 448:448 + CMP_PAD], start=True, stop=True)
                    ins.then_inc(sem("cmp_sc"), 1)
                    pe.wait_ge(sem("cmp_p"), NT)
                    for t in range(NT):
                        ins = pe.transpose(ps[:, 4, t * P:(t + 1) * P], cmp_s[:, t, :], ident)
                    ins.then_inc(sem("cmp_pT"), 1)
                    pe.wait_ge(sem("cmp_pT_copied"), 1)
                    for t in range(NT):
                        ins = pe.matmul(ps[:, 6 + t, :], small_pT[:, t, :], v_bd, start=True, stop=True)
                    ins.then_inc(sem("cmp_o"), 1)
                    for n in range(NT * HEADS):
                        t, h = n // HEADS, n % HEADS
                        r = slice(HD * (h % 2), HD * (h % 2) + HD)
                        if n >= 4:
                            pe.wait_ge(sem("idx_relu"), n - 3)
                        pe.matmul(ps[:, n % 4, 0:n_keys(t)], qkT[r, (10 + h) // 2, t * P:(t + 1) * P],
                                  qkT[r, 9, 0:n_keys(t)], start=True, stop=True).then_inc(sem("idx_mm"), 1)
                    pe.wait_ge(sem("idx_relu"), NT * HEADS)
                    pe.wait_ge(sem("cmp_out"), NT)
                else:
                    k = first_item[L]
                    wait_item(pe, k)
                    w = slot_view(k, FOX_HEADS, DC)
                    for t in range(NT):
                        for c in range(DC):
                            ins = pe.matmul(ps[:, 6, t * FOX_HEADS:(t + 1) * FOX_HEADS], xT[:, c, t * P:(t + 1) * P],
                                            w[:, c, :], start=(c == 0), stop=(c == DC - 1))
                        ins.then_inc(sem(f"proj_mm{L}"), 1)
                    for j in range(4):
                        k = first_item[L] + 1 + j
                        wait_item(pe, k)
                        w = slot_view(k, PIECE, DC)
                        for half in range(2):
                            if j >= 2:
                                pe.wait_ge(sem(f"proj_t{half}_{L}"), j - 1)
                            for b in range(2):
                                for c in range(DC):
                                    ins = pe.matmul(ps[:, (2 * j + half) % 4, b * SEQ:(b + 1) * SEQ],
                                                    w[:, c, (2 * half + b) * P:(2 * half + b + 1) * P], xT[:, c, :],
                                                    start=(c == 0), stop=(c == DC - 1))
                            ins.then_inc(sem(f"proj_mm{L}"), 1)
                    pe.wait_ge(sem("logf"), 1)
                    for c in range(NT):
                        ins = pe.matmul(ps[0:FOX_HEADS, 7, 0:SEQ], logf[:, c, :],
                                        const[:, C_TRI + c * SEQ:C_TRI + (c + 1) * SEQ], start=(c == 0), stop=(c == NT - 1))
                    ins.then_inc(sem("dcum"), 1)
                    for j in range(2):
                        k = first_item[L] + 5 + j
                        wait_item(pe, k)
                        w = slot_view(k, PIECE, DC)
                        for t in range(NT):
                            pe.wait_ge(sem(f"proj_t{t}_{L}"), j + 3)
                            for c in range(DC):
                                ins = pe.matmul(ps[:, (2 * j + t) % 4, :], xT[:, c, t * P:(t + 1) * P],
                                                w[:, c, :], start=(c == 0), stop=(c == DC - 1))
                            ins.then_inc(sem(f"proj_mm{L}"), 1)
                    pe.wait_ge(sem(f"proj_t0_{L}"), 6)
                    pe.wait_ge(sem(f"proj_t1_{L}"), 6)
                    pe.wait_ge(sem("aug"), 1)
                attention(L)

                def o_ready(t, L=L):
                    pe.wait_ge(sem(f"o_ready{L}"), t + 1)
                    if L % 2 == 0:
                        pe.wait_ge(sem(f"proj_t0_{L}"), 5)
                transpose_x(3 * L, o_tok, o_ready)
                pe.wait_ge(sem("oT_act"), NT * (L + 1))
                pe.wait_ge(sem("oT_dve"), NT * (L + 1))
                for n in range(2):
                    k = shared_item[L] - 2 + n
                    wait_item(pe, k)
                    w = slot_view(k, PIECE, DC)
                    for t in range(NT):
                        for c in range(DC):
                            ins = pe.matmul(ps[:, 4 + 2 * t + n, :], xT[:, c, t * P:(t + 1) * P], w[:, c, :],
                                            start=(c == 0), stop=(c == DC - 1))
                        ins.then_inc(sem(f"wo_mm{L}"), 1)

                transpose_x(3 * L + 1, x_tok, lambda t: pe.wait_ge(sem(f"ln1_out{L}"), t + 1))
                wait_xT(3 * L + 1)
                pe.wait_ge(sem("layer_loaded"), 48 * (L + 1))
                for t in range(NT):
                    for c in range(DC):
                        ins = pe.matmul(ps[:, 4 + t, 0:NE], xT[:, c, t * P:(t + 1) * P], router_w[:, c, :],
                                        start=(c == 0), stop=(c == DC - 1))
                    ins.then_inc(sem(f"router_mm{L}"), 1)
                pe.wait_ge(sem(f"router_dve{L}"), NT)

                ks = shared_item[L]

                def up_all(slot):
                    w1, w3, _ = ffn_views(slot)
                    for b, w in enumerate((w1, w3)):
                        for f in range(2):
                            for c in range(DC):
                                ins = pe.matmul(ps[:, 4 + b, f * SEQ:(f + 1) * SEQ], w[:, c, f::2],
                                                xT[:, c, :], start=(c == 0), stop=(c == DC - 1))
                    return ins

                def down_all(slot):
                    _, _, w2 = ffn_views(slot)
                    for t in range(NT):
                        for half in range(2):
                            for f in range(2):
                                ins = pe.matmul(ps[:, 2 * t + half, :], h_all[:, f * SEQ + t * P:f * SEQ + (t + 1) * P],
                                                w2[:, f, half * PIECE:(half + 1) * PIECE], start=(f == 0), stop=(f == 1))
                    return ins

                wait_item(pe, ks)
                pe.wait_ge(sem("router_e"), NT * (L + 1))
                up_all(ks % RING).then_inc(sem("shared_up"), 1)
                pe.wait_ge(sem(f"router_dve{L}"), NT)
                for t in range(NT):
                    for c in range(t + 1):
                        ins = pe.matmul(ps[:, 6 + t, 0:NE], const[:, C_TRI + c * SEQ + t * P:C_TRI + c * SEQ + (t + 1) * P],
                                        chosen[:, c, :], start=(c == 0), stop=(c == t))
                ins.then_inc(sem("place_mm"), 1)
                pe.wait_ge(sem("shared_h"), L + 1)
                down_all(ks % RING).then_inc(sem("shared_down"), 1)

                M0 = L * PAIRS

                def gather(m, par):
                    pe.wait_ge(sem("sel_built"), m + (M0 + 1))
                    if M0 or not isinstance(m, int) or m > 0:
                        pe.wait_ge(sem("xe_copied"), m + M0)
                    for c in range(DC):
                        for t in range(NT):
                            ins = pe.matmul(ps[:, c // 4, (c % 4) * P:(c % 4 + 1) * P], x_tok[:, t, c::DC],
                                            sel[:, par, t, :], start=(t == 0), stop=(t == NT - 1))
                    ins.then_inc(sem("gathered"), 1)

                def sel_transpose(m, par, first=False):
                    pe.wait_ge(sem("sel_built"), m + (M0 + 1))
                    if not first:
                        pe.wait_ge(sem("hT_copied"), m + M0)
                    for t in range(NT):
                        pe.transpose(ps[:, 3, t * P:(t + 1) * P], sel[:, par, t, :], ident)
                    for t in range(NT):
                        cols = slice(2 * m, 2 * m + 2) if isinstance(m, int) else bass.ds(2 * m, 2)
                        ins = pe.matmul(ps[:, 3, SEQ:SEQ + 2], sel[:, par, t, :], gates[:, t, cols],
                                        start=(t == 0), stop=(t == NT - 1))
                    ins.then_inc(sem("selT_tp"), 1)

                def exp_up(m, par, first):
                    pe.wait_ge(sem("xe_copied"), m + (M0 + 1))
                    if not first:
                        pe.wait_ge(sem("exp_h"), m + M0)
                    views = [ffn_views((ks + 1 + 2 * par + b) % RING) for b in range(2)]
                    for w in range(2):
                        for c in range(DC):
                            for b in range(2):
                                ins = pe.matmul(ps[b * SLOTS:(b + 1) * SLOTS, 2, w * FE:(w + 1) * FE],
                                                xe[:, par, c, b * SLOTS:(b + 1) * SLOTS], views[b][w][:, c, :],
                                                start=(c == 0), stop=(c == DC - 1))
                    ins.then_inc(sem("exp_up"), 1)

                def h_transpose(m):
                    pe.wait_ge(sem("exp_h"), m + (M0 + 1))
                    pe.wait_ge(sem("selT_copied"), m + (M0 + 1))
                    for f in range(2):
                        ins = pe.transpose(ps[:, 3, f * P:(f + 1) * P], h_exp[:, f::2], ident)
                    ins.then_inc(sem("hT_tp"), 1)

                def exp_down(m, par, first):
                    pe.wait_ge(sem("hT_copied"), m + (M0 + 1))
                    if not first:
                        pe.wait_ge(sem("yp_copied"), m + M0)
                    views = [ffn_views((ks + 1 + 2 * par + b) % RING)[2] for b in range(2)]
                    for half in range(2):
                        for f in range(2):
                            for b in range(2):
                                ins = pe.matmul(ps[b * SLOTS:(b + 1) * SLOTS, 4 + half, :],
                                                hT[:, f, b * SLOTS:(b + 1) * SLOTS],
                                                views[b][:, f, half * PIECE:(half + 1) * PIECE], start=(f == 0), stop=(f == 1))
                    ins.then_inc(sem("exp_down"), 1)

                def scatter(m, t, par, first):
                    if t == 0:
                        pe.wait_ge(sem("yp_copied"), m + (M0 + 1))
                    if not (first and t == 0):
                        pe.wait_ge(sem("y_added"), 2 * m + (2 * M0 + t))
                    for half in range(2):
                        ins = pe.matmul(ps[:, 6 + half, :], selT[:, par, t * P:(t + 1) * P],
                                        y_pair[:, half * PIECE:(half + 1) * PIECE], start=True, stop=True)
                    ins.then_inc(sem("scattered"), 1)

                def pe_step(m, u, gather_next=True, scatter_last=True, first=False):
                    for b in range(2):
                        k = ks + 1 + 2 * u + b
                        if isinstance(m, int):
                            pe.wait_ge(w_loaded[k % RING], 48 * (m // 2) + loaded[k])
                        else:
                            pe.wait_ge(w_loaded[k % RING], 24 * (m - u) + loaded[k])
                    exp_up(m, u, first and M0 == 0)
                    if gather_next:
                        gather(m + 1, 1 - u)
                    h_transpose(m)
                    if scatter_last:
                        scatter(m - 1, 0, 1 - u, M0 == 0 and isinstance(m, int) and m == 1)
                    exp_down(m, u, first and M0 == 0)
                    if gather_next:
                        sel_transpose(m + 1, 1 - u)
                    if scatter_last:
                        scatter(m - 1, 1, 1 - u, False)

                pe.wait_ge(sem("shared_added"), L + 1)
                gather(0, 0)
                sel_transpose(0, 0, first=True)
                pe_step(0, 0, scatter_last=False, first=True)
                pe_step(1, 1)
                with pe.Fori(1, PAIRS // 2 - 1) as i:
                    for u in range(2):
                        pe_step(2 * i + u, u)
                pe_step(PAIRS - 2, 0)
                pe_step(PAIRS - 1, 1, gather_next=False)
                scatter(PAIRS - 1, 0, 1, False)
                scatter(PAIRS - 1, 1, 1, False)

                pe.wait_ge(sem("y_added"), 2 * (M0 + PAIRS))
                pe.wait_ge(sem("over_flag"), L + 1)
                flag = pe.value_load(over_int[0:1, 0:1], min_val=0, max_val=1)
                with pe.If(flag > 0):
                    with pe.Fori(0, NE) as e:
                        pe.wait_ge(sem(f"over_loaded{L}"), 48 * e + 48)
                        up_all(0).then_inc(sem(f"over_up{L}"), 1)
                        pe.wait_ge(sem(f"over_h{L}"), e + 1)
                        down_all(0).then_inc(sem(f"over_down{L}"), 1)
                    pe.wait_ge(sem(f"over_added{L}"), NE)

                kp = ks + 1 + NE
                for t in range(NT):
                    for c in range(2):
                        ins = pe.transpose(ps[:, 4, c * SEQ + t * P:c * SEQ + (t + 1) * P], p_tok[:, t, c::2], ident)
                    ins.then_inc(sem(f"pT_tp{L}"), 1)
                pe.wait_ge(sem(f"pT_done{L}"), 1)
                wait_item(pe, kp)
                w = slot_view(kp, D, 2)
                for t in range(NT):
                    for half in range(2):
                        for c in range(2):
                            ins = pe.matmul(ps[:, 4 + 2 * t + half, :], ple_pT[:, c, t * P:(t + 1) * P],
                                            w[:, c, half * PIECE:(half + 1) * PIECE], start=(c == 0), stop=(c == 1))
                    ins.then_inc(sem(f"ple_mm{L}"), 1)
                transpose_x(3 * L + 2, x_tok, lambda t: pe.wait_ge(sem(f"ln2_out{L}"), t + 1))
                wait_xT(3 * L + 2)
                for n in range(2):
                    wait_item(pe, kp + 1 + n)
                    w = slot_view(kp + 1 + n, PIECE, DC)
                    for t in range(NT):
                        for c in range(DC):
                            ins = pe.matmul(ps[:, 2 * t + n, :], xT[:, c, t * P:(t + 1) * P], w[:, c, :],
                                            start=(c == 0), stop=(c == DC - 1))
                        ins.then_inc(sem(f"ple_mm{L}"), 1)
                pe.wait_ge(sem(f"ple_out{L}"), NT)

        @block.scalar
        def _(act):
            def copy_T(name, count):
                for t in range(NT):
                    act.wait_ge(sem("xT_tp"), count + t + 1)
                    act.activation(xT[:, 0:4, t * P:(t + 1) * P],
                                   ps[:, 2 * t, :].rearrange("p (c n) -> p c n", c=4),
                                   ACT.Copy).then_inc(sem(name), 1)

            def attention(L):
                units = UNITS[L % 2]
                for u in range(len(units) + 1):
                    if u < len(units):
                        what, t, g = units[u]
                        K = n_keys(t)
                        act.wait_ge(sem(f"sc_max{L}"), u + 1)
                        for s, h in enumerate(unit_slots(g)):
                            ins = act.activation(scores[:, u % 2, s * K:(s + 1) * K], scores[:, u % 2, s * K:(s + 1) * K],
                                                 ACT.Exp, bias=neg_max[:, u % 2, s:s + 1],
                                                 accum_out=denom[:, (u // 2) % 2, 4 * (u % 2) + s:4 * (u % 2) + s + 1])
                        ins.then_inc(sem(f"sc_exp{L}"), 1)
                    if u >= 1:
                        v = u - 1
                        t = units[v][1]
                        act.wait_ge(sem(f"pT_tp{L}u"), v + 1)
                        if v >= 2:
                            act.wait_ge(sem(f"pv_mm{L}"), v - 1)
                        n = 4 * (t + 1) * P
                        act.activation(pT[:, v % 2, 0:n], ps[:, 4:6, :].rearrange("p b n -> p (b n)")[:, 0:n],
                                       ACT.Copy).then_inc(sem(f"pT_copied{L}"), 1)

            rs_count = [0]

            def rsqrt_guess():
                rs_count[0] += 1
                act.wait_ge(sem("var_ready"), rs_count[0])
                act.activation(rstd, var_eps, ACT.Ln).then_inc(sem("var_ln"), 1)
                act.wait_ge(sem("var_ln"), rs_count[0])
                act.activation(rstd, rstd, ACT.Exp, scale=-0.5).then_inc(sem("rstd_guess"), 1)

            tp = 0
            for L in range(DEPTH):
                copy_T("xT_act", tp)
                tp += NT
                if L % 2 == 0:
                    for j, (c0, c1) in enumerate(proj_pieces[0]):
                        act.wait_ge(sem(f"proj_mm{L}"), 2 * j + 1)
                        act.activation(proj[:, 0, c0:c1], ps[:, 4 + 2 * j % 4, 0:c1 - c0], ACT.Copy)\
                           .then_inc(sem(f"proj_t0_{L}"), 1)
                    dups = ((1, 8, 9), (2, 18, 19), (4, 28, 29), (5, 30, 31))
                    for need, s, d in dups[0:2]:
                        act.wait_ge(sem(f"roped{L}"), (need + 1 if need == 1 else 3))
                        act.activation(roped[:, :, d * HD:(d + 1) * HD], roped[:, :, s * HD:(s + 1) * HD], ACT.Copy)\
                           .then_inc(sem(f"dup{L}"), 1)
                    for m in range(4):
                        if m == 3:
                            for need, s, d in dups[2:4]:
                                act.wait_ge(sem(f"roped{L}"), 5)
                                act.activation(roped[:, :, d * HD:(d + 1) * HD], roped[:, :, s * HD:(s + 1) * HD], ACT.Copy)\
                                   .then_inc(sem(f"dup{L}"), 1)
                        act.wait_ge(sem(f"qkT_tp{L}"), m + 1)
                        act.activation(qkT[:, 4 * m:4 * m + 4, :],
                                       ps[:, 2 * (m % 2):2 * (m % 2) + 2, :].rearrange("p b (c n) -> p (b c) n", c=2),
                                       ACT.Copy).then_inc(sem(f"qkT_copied{L}"), 1)
                    act.wait_ge(sem("cmp_h"), 1)
                    act.activation(small[0:HD, 160:160 + N_CMP], ps[0:HD, 6, 0:N_CMP], ACT.Exp, scale=-1.0)
                    act.activation(small[0:HD, 176:176 + N_CMP], ps[0:HD, 7, 0:N_CMP], ACT.Exp, scale=-1.0)\
                       .then_inc(sem("cmp_exp"), 1)
                    act.wait_ge(sem("gate_z"), 1)
                    act.activation(gate_sig, gate_sig, ACT.Exp, scale=-1.0).then_inc(sem("gate_e"), 1)
                    act.wait_ge(sem("cmp_sub"), 1)
                    act.activation(cmp_s, cmp_s, ACT.Exp).then_inc(sem("cmp_e"), 1)
                    act.wait_ge(sem("cmp_pT"), 1)
                    act.activation(small_pT, ps[:, 4, 0:SEQ], ACT.Copy).then_inc(sem("cmp_pT_copied"), 1)
                    for n in range(NT * HEADS):
                        t = n // HEADS
                        act.wait_ge(sem("idx_mm"), n + 1)
                        if n >= 2:
                            act.wait_ge(sem("idx_acc"), n - 1)
                        act.activation(relu_buf[:, n % 2, 0:n_keys(t)], ps[:, n % 4, 0:n_keys(t)], ACT.Relu)\
                           .then_inc(sem("idx_relu"), 1)
                else:
                    act.wait_ge(sem("fox_z"), 1)
                    act.activation(fox_t, fox_zb, ACT.Abs).then_inc(sem("fox_abs"), 1)
                    act.wait_ge(sem("fox_abs"), 1)
                    act.activation(fox_t, fox_t, ACT.Exp, scale=-1.0).then_inc(sem("fox_e"), 1)
                    act.wait_ge(sem("fox_e"), 1)
                    act.activation(fox_t, fox_t, ACT.Ln, bias=1.0).then_inc(sem("fox_ln"), 1)
                    for j in range(4):
                        act.wait_ge(sem(f"proj_mm{L}"), NT + 2 * j + 1)
                        act.activation(qkT[:, 4 * j:4 * j + 2, :], ps[:, 2 * j % 4, :], ACT.Copy)\
                           .then_inc(sem(f"proj_t0_{L}"), 1)
                    for j in range(2):
                        act.wait_ge(sem(f"proj_mm{L}"), NT + 8 + 2 * j + 1)
                        act.activation(v_fox[:, 0, j * PIECE:(j + 1) * PIECE], ps[:, 2 * j, :], ACT.Copy)\
                           .then_inc(sem(f"proj_t0_{L}"), 1)
                attention(L)
                copy_T("oT_act", tp)
                tp += NT
                rsqrt_guess()
                rsqrt_guess()
                copy_T("xT_act", tp)
                tp += NT
                for t in range(NT):
                    act.wait_ge(sem(f"router_mm{L}"), t + 1)
                    act.activation(sig[:, t, :], ps[:, 4 + t, 0:NE], ACT.Exp, scale=-1.0).then_inc(sem("router_e"), 1)

                act.wait_ge(sem("shared_up"), L + 1)
                act.activation(h_silu_all, ps[:, 4, :], ACT.Silu).then_inc(sem("shared_silu"), 1)

                M0 = L * PAIRS

                def later(m, n):
                    return M0 > 0 or not isinstance(m, int) or m >= n

                def xe_copy(m, par):
                    act.wait_ge(sem("gathered"), m + (M0 + 1))
                    if later(m, 2):
                        act.wait_ge(sem("exp_up"), m + (M0 - 1))
                    act.activation(xe[:, par, :, :], ps[:, 0:2, :].rearrange("p b (c n) -> p (b c) n", c=4), ACT.Copy)\
                       .then_inc(sem("xe_copied"), 1)

                def silu(m):
                    act.wait_ge(sem("exp_up"), m + (M0 + 1))
                    if later(m, 1):
                        act.wait_ge(sem("exp_h"), m + M0)
                    act.activation(h_silu, ps[:, 2, 0:FE], ACT.Silu).then_inc(sem("exp_silu"), 1)

                def hT_copy(m):
                    act.wait_ge(sem("hT_tp"), m + (M0 + 1))
                    if later(m, 1):
                        act.wait_ge(sem("exp_down"), m + M0)
                    act.activation(hT, ps[:, 3, 0:2 * P].rearrange("p (f n) -> p f n", f=2), ACT.Copy).then_inc(sem("hT_copied"), 1)

                def selT_copy(m, par):
                    act.wait_ge(sem("selT_tp"), m + (M0 + 1))
                    if later(m, 2):
                        act.wait_ge(sem("scattered"), 2 * m + (2 * M0 - 2))
                    if later(m, 2):
                        act.wait_ge(sem("exp_h"), m + (M0 - 1))
                    act.activation(selT[:, par, :], ps[:, 3, 0:SEQ], ACT.Copy)
                    for b in range(2):
                        ins = act.activation(slot_gate[b * SLOTS:(b + 1) * SLOTS, par:par + 1],
                                             ps[b * SLOTS:(b + 1) * SLOTS, 3, SEQ + b:SEQ + b + 1], ACT.Copy)
                    ins.then_inc(sem("selT_copied"), 1)

                def yp_copy(m):
                    act.wait_ge(sem("exp_down"), m + (M0 + 1))
                    if later(m, 1):
                        act.wait_ge(sem("scattered"), 2 * m + 2 * M0)
                    act.activation(y_pair, ps[:, 4:6, :], ACT.Copy).then_inc(sem("yp_copied"), 1)

                def act_step(m, u, more=True):
                    silu(m)
                    if more:
                        xe_copy(m + 1, 1 - u)
                    hT_copy(m)
                    yp_copy(m)
                    if more:
                        selT_copy(m + 1, 1 - u)

                xe_copy(0, 0)
                selT_copy(0, 0)
                act_step(0, 0)
                act_step(1, 1)
                with act.Fori(1, PAIRS // 2 - 1) as i:
                    for u in range(2):
                        act_step(2 * i + u, u)
                act_step(PAIRS - 2, 0)
                act_step(PAIRS - 1, 1, more=False)

                act.wait_ge(sem("over_flag"), L + 1)
                flag = act.value_load(over_int[0:1, 0:1], min_val=0, max_val=1)
                with act.If(flag > 0):
                    with act.Fori(0, NE) as e:
                        act.wait_ge(sem(f"over_up{L}"), e + 1)
                        act.activation(h_silu_all, ps[:, 4, :], ACT.Silu).then_inc(sem(f"over_silu{L}"), 1)

                act.wait_ge(sem(f"pT_tp{L}"), NT)
                act.activation(ple_pT, ps[:, 4, :], ACT.Copy).then_inc(sem(f"pT_done{L}"), 1)
                rsqrt_guess()
                rsqrt_guess()
                for t in range(NT):
                    act.wait_ge(sem(f"ple_mm{L}"), t + 1)
                    act.activation(roped[:, t, 0:D], ps[:, 4 + 2 * t:6 + 2 * t, :], ACT.Square,
                                   accum_out=ple_ss[:, t:t + 1]).then_inc(sem(f"ple_sq{L}"), 1)
                copy_T("xT_act", tp)
                tp += NT
                rsqrt_guess()
                rsqrt_guess()
                for t in range(NT):
                    act.wait_ge(sem(f"ple_mm{L}"), NT * 2 + t + 1)
                    act.wait_ge(sem(f"ple_sq{L}"), NT)
                    act.activation(roped[:, t, 0:D], ps[:, 2 * t:2 * t + 2, :], ACT.Sigmoid)\
                       .then_inc(sem(f"ple_sig{L}"), 1)

        @block.vector
        def _(dve):
            step = [0]
            rs_count = [0]
            chain = sem("dve_step")

            def seq(ins):
                step[0] += 1
                ins.then_inc(chain, 1)
                dve.wait_ge(chain, step[0])

            def copy_T(name, count):
                for t in range(NT):
                    dve.wait_ge(sem("xT_tp"), count + t + 1)
                    dve.tensor_copy(xT[:, 4:8, t * P:(t + 1) * P],
                                    ps[:, 2 * t + 1, :].rearrange("p (c n) -> p c n", c=4))\
                       .then_inc(sem(name), 1)

            def rope(t, src, n, dst, cs, sn, rows_=P, tmp=None):
                c = cs.unsqueeze(1).unsqueeze(1)
                s = sn.unsqueeze(1)
                tmp = tmp if tmp is not None else o_tok_tmp[0:rows_, 0:n * 32].rearrange("p (n k) -> p n k", n=n)
                seq(dve.tensor_tensor(dst, src, c.to_broadcast([rows_, n, 2, 32]), ALU.mult))
                seq(dve.tensor_tensor(tmp, src[:, :, 1, :], s.to_broadcast([rows_, n, 32]), ALU.mult))
                seq(dve.tensor_tensor(dst[:, :, 0, :], dst[:, :, 0, :], tmp, ALU.subtract))
                seq(dve.tensor_tensor(tmp, src[:, :, 0, :], s.to_broadcast([rows_, n, 32]), ALU.mult))
                return dve.tensor_tensor(dst[:, :, 1, :], dst[:, :, 1, :], tmp, ALU.add)

            def attention(L):
                units = UNITS[L % 2]
                for u in range(len(units) + 2):
                    if u < len(units):
                        what, t, g = units[u]
                        K = n_keys(t)
                        dve.wait_ge(sem(f"sc_mm{L}"), u + 1)
                        if u >= 2:
                            dve.wait_ge(sem(f"pT_tp{L}u"), u - 1)
                        bias = selbias[:, t, 0:K] if what == "dsa" else const[:, C_CAUSAL + SEQ - K:C_CAUSAL + SEQ]
                        s_out = scores[:, u % 2, 0:4 * K].rearrange("p (s k) -> p s k", s=4)
                        for b in range(2):
                            ins = dve.scalar_tensor_tensor(
                                s_out[:, 2 * b:2 * b + 2, :], ps[:, 2 * (u % 2) + b, 0:2 * K].rearrange("p (s k) -> p s k", s=2),
                                SCALE, bias.unsqueeze(1).to_broadcast([P, 2, K]), ALU.mult, ALU.add)
                        ins.then_inc(sem(f"sc_biased{L}"), 1)
                        dve.wait_ge(sem(f"sc_biased{L}"), u + 1)
                        if u >= 2:
                            dve.wait_ge(sem(f"sc_exp{L}"), u - 1)
                        dve.tensor_reduce(neg_max[:, u % 2, 0:4], s_out, AX_X, ALU.max, negate=True)\
                           .then_inc(sem(f"sc_max{L}"), 1)
                    if u >= 2 and u % 2 == 1:
                        v = u - 2
                        what, t, g = units[v]
                        grp = v // 2
                        dve.wait_ge(sem(f"pv_mm{L}"), v + 1)
                        seq(dve.reciprocal(coef, denom[:, grp % 2, :]))
                        by_head = coef.rearrange("p (g b j) -> p g j b", g=2, b=2)
                        if what in ("sel", "win"):
                            br = 1 if what == "sel" else 2
                            gate = gate_sig.rearrange("p (t h b) -> p t h b", t=NT, b=3)[:, t, :, br]
                            seq(dve.tensor_tensor(coef_h.rearrange("p (g j b) -> p g j b", g=2, b=2), by_head,
                                                  gate.rearrange("p (g j b) -> p g j b", g=2, b=2), ALU.mult))
                        else:
                            seq(dve.tensor_copy(coef_h.rearrange("p (g j b) -> p g j b", g=2, b=2), by_head))
                        o_ps = ps[:, 6 + grp % 2, :].rearrange("p (h d) -> p h d", h=8)
                        cb = coef_h.unsqueeze(2).to_broadcast([P, 8, HD])
                        if what in ("sel", "win"):
                            o = o_tok[:, t, 512:1024]
                            seq_ins = dve.tensor_tensor(tmp_o.rearrange("p (h d) -> p h d", h=8), o_ps, cb, ALU.mult)
                            seq_ins.then_inc(sem(f"pv_out{L}"), 1)
                            dve.wait_ge(sem(f"pv_out{L}"), grp + 1)
                            seq(dve.tensor_tensor(o, o, tmp_o, ALU.add))
                        else:
                            c0 = 0 if what == "dsa" else 512 * (g // 2)
                            dve.tensor_tensor(o_tok[:, t, c0:c0 + 512].rearrange("p (h d) -> p h d", h=8), o_ps, cb, ALU.mult)\
                               .then_inc(sem(f"pv_out{L}"), 1)
                            last = (what == "dsa") or g >= 2
                            if last:
                                dve.wait_ge(sem(f"pv_out{L}"), grp + 1)
                                dve.engine_nop().then_inc(sem(f"o_ready{L}"), 1)

            def rsqrt(v, scale, eps):
                rs_count[0] += 1
                dve.tensor_scalar(var_eps, v, scale, eps, ALU.mult, ALU.add).then_inc(sem("var_ready"), 1)
                dve.wait_ge(sem("rstd_guess"), rs_count[0])
                seq(dve.tensor_scalar(newton, rstd, rstd, var_eps, ALU.mult, ALU.mult))
                seq(dve.tensor_scalar(newton, newton, -0.5, 1.5, ALU.mult, ALU.add))
                seq(dve.tensor_tensor(rstd, rstd, newton, ALU.mult))

            def layer_norm(L, which, other):
                j = 3 * L + which - 1
                for t in range(NT):
                    for half in range(2):
                        xs = x_tok[:, t, half * PIECE:(half + 1) * PIECE]
                        if which == 1:
                            dve.wait_ge(sem(f"wo_mm{L}"), NT * half + t + 1)
                        seq(dve.scalar_tensor_tensor(xs, xs, ALPHA, other(t, half), ALU.mult, ALU.add))
                        seq(dve.bn_stats(stats[:, t, half, :], xs))
                    seq(dve.bn_aggr(mean_var, stats[:, t, :, :]))
                    rsqrt(mean_var[:, 1:2], 1.0, LN_EPS)
                    seq(dve.tensor_scalar(x_tok[:, t, :], x_tok[:, t, :], mean_var[:, 0:1], rstd, ALU.subtract, ALU.mult))
                    dve.wait_ge(sem("gb_loaded"), 32 * (j + 1))
                    seq(dve.tensor_tensor(x_tok[:, t, :], x_tok[:, t, :], gb_row[:, 0, :], ALU.mult))
                    seq(dve.tensor_tensor(x_tok[:, t, :], x_tok[:, t, :], gb_row[:, 1, :], ALU.add))
                    dve.engine_nop().then_inc(sem(f"ln{which}_out{L}"), 1)
                    dve.engine_nop().then_inc(sem("gb_used"), 1)

            tp = 0
            dve.wait_ge(sem("const_loaded"), 16)
            for L in range(DEPTH):
                copy_T("xT_dve", tp)
                tp += NT
                if L % 2 == 0:
                    for j, (c0, c1) in enumerate(proj_pieces[0]):
                        dve.wait_ge(sem(f"proj_mm{L}"), 2 * j + 2)
                        dve.tensor_copy(proj[:, 1, c0:c1], ps[:, 4 + (2 * j + 1) % 4, 0:c1 - c0])\
                           .then_inc(sem(f"proj_t1_{L}"), 1)
                    dve.wait_ge(sem(f"proj_t0_{L}"), 5)
                    dve.wait_ge(sem(f"proj_t1_{L}"), 5)
                    for groups in (((QA, 8, 0),), ((KA, 1, 8),), ((QI, 9, 10),), ((QB, 8, 20),), ((KS, 1, 28), (KW, 1, 30))):
                        for src, n, dst in groups:
                            for t in range(NT):
                                ins = rope(t, proj[:, t, src:src + n * HD].rearrange("p (n h k) -> p n h k", n=n, h=2), n,
                                           roped[:, t, dst * HD:(dst + n) * HD].rearrange("p (n h k) -> p n h k", n=n, h=2),
                                           const[:, C_COS + 32 * t:C_COS + 32 * t + 32],
                                           const[:, C_SIN + 32 * t:C_SIN + 32 * t + 32])
                                if t == NT - 1 and (src, n, dst) == groups[-1]:
                                    ins.then_inc(sem(f"roped{L}"), 1)
                                else:
                                    seq(ins)
                        dve.wait_ge(sem(f"roped{L}"), 1) if groups[0][0] == QA else None
                    dve.wait_ge(sem(f"roped{L}"), 5)
                    dve.wait_ge(sem("cmp_tp"), 1)
                    seq(dve.tensor_copy(kvT, ps[:, 4, 0:SEQ]))
                    seq(dve.tensor_copy(peT, ps[:, 5, 0:CMP_LEN]))
                    for c in range(N_CMP):
                        ins = dve.tensor_tensor(cmp_blk[:, :, c], kvT[:, c * CMP_STRIDE:c * CMP_STRIDE + CMP_LEN], peT, ALU.add)
                    ins.then_inc(sem("cmp_blk"), 1)
                    dve.wait_ge(sem("cmp_exp"), 1)
                    seq(dve.tensor_scalar(small[0:HD, 160:192], small[0:HD, 160:192], 1.0, None, ALU.add))
                    seq(dve.reciprocal(small[0:HD, 160:192], small[0:HD, 160:192]))
                    dve.tensor_tensor(small[0:HD, 128:128 + N_CMP], ps[0:HD, 6, 0:N_CMP], small[0:HD, 160:160 + N_CMP], ALU.mult)
                    dve.tensor_tensor(small[0:HD, 144:144 + N_CMP], ps[0:HD, 7, 0:N_CMP], small[0:HD, 176:176 + N_CMP], ALU.mult)\
                       .then_inc(sem("cmp_hs"), 1)
                    dve.wait_ge(sem("cmp_kv"), 1)
                    seq(dve.tensor_copy(small[0:N_CMP, 384:448], ps[0:N_CMP, 4, HD:P]))
                    seq(rope(0, ps[0:N_CMP, 4, 0:HD].rearrange("p (n h k) -> p n h k", n=1, h=2), 1,
                             small[0:N_CMP, 256:320].rearrange("p (n h k) -> p n h k", n=1, h=2),
                             const[0:N_CMP, C_CCOS:C_CCOS + 32], const[0:N_CMP, C_CSIN:C_CSIN + 32], rows_=N_CMP,
                             tmp=small[0:N_CMP, 192:224].rearrange("p (n k) -> p n k", n=1)))
                    dve.tensor_copy(small[0:N_CMP, 320:384], small[0:N_CMP, 256:320]).then_inc(sem("cmp_roped"), 1)
                    dve.wait_ge(sem("bias_loaded"), 32)
                    dve.tensor_tensor(gate_sig.rearrange("p (t n) -> p t n", t=NT), proj[:, :, GB:GB + 24],
                                      bgate[:, :].unsqueeze(1).to_broadcast([P, NT, 24]), ALU.add).then_inc(sem("gate_z"), 1)
                    dve.wait_ge(sem("cmp_rep"), 1)
                    dve.tensor_copy(small[:, 448:448 + CMP_PAD], ps[:, 5, 0:CMP_PAD]).then_inc(sem("cmp_kT"), 1)
                    for h in range(HEADS):
                        ins = dve.tensor_scalar(v_bd[:, h * HD:(h + 1) * HD], ps[:, 6, 0:HD],
                                                const[:, C_BD + h:C_BD + h + 1], None, ALU.mult)
                    ins.then_inc(sem("v_bd_dve"), 1)
                    dve.wait_ge(sem("cmp_sc"), 1)
                    for b in range(2):
                        for t in range(NT):
                            sc = cmp_s[:, t, b * 64:(b + 1) * 64].rearrange("p (s c) -> p s c", s=4)
                            ins = dve.scalar_tensor_tensor(
                                sc, ps[:, 4 + b, t * 64:(t + 1) * 64].rearrange("p (s c) -> p s c", s=4), SCALE,
                                const[:, C_CBIAS + t * CMP_PAD:C_CBIAS + (t + 1) * CMP_PAD].unsqueeze(1).to_broadcast([P, 4, CMP_PAD]),
                                ALU.mult, ALU.add)
                    seq(ins)
                    sall = cmp_s.rearrange("p t (s c) -> p (t s) c", s=8)
                    seq(dve.tensor_reduce(cmp_m, sall, AX_X, ALU.max, negate=True))
                    dve.tensor_tensor(sall, sall, cmp_m.unsqueeze(2).to_broadcast([P, 16, CMP_PAD]), ALU.add)\
                       .then_inc(sem("cmp_sub"), 1)
                    dve.wait_ge(sem("cmp_e"), 1)
                    seq(dve.tensor_reduce(cmp_m, sall, AX_X, ALU.add))
                    for t in range(NT):
                        sc = cmp_s[:, t, :].rearrange("p (s c) -> p s c", s=8)
                        dve.tensor_tensor(sc, sc, const[:, C_CVALID + t * CMP_PAD:C_CVALID + (t + 1) * CMP_PAD]
                                          .unsqueeze(1).to_broadcast([P, 8, CMP_PAD]), ALU.mult).then_inc(sem("cmp_p"), 1)
                    dve.wait_ge(sem("gate_e"), 1)
                    seq(dve.tensor_scalar(gate_sig, gate_sig, 1.0, None, ALU.add))
                    seq(dve.reciprocal(gate_sig, gate_sig))
                    seq(dve.reciprocal(cmp_m, cmp_m))
                    for t in range(NT):
                        gate = gate_sig.rearrange("p (t h b) -> p t h b", t=NT, b=3)[:, t, :, 0]
                        seq(dve.tensor_tensor(coef_h.rearrange("p (j b) -> p j b", b=2),
                                              cmp_m[:, 8 * t:8 * t + 8].rearrange("p (b j) -> p j b", b=2),
                                              gate.rearrange("p (j b) -> p j b", b=2), ALU.mult))
                        dve.wait_ge(sem("cmp_o"), 1)
                        dve.tensor_tensor(o_tok[:, t, 512:1024].rearrange("p (h d) -> p h d", h=8),
                                          ps[:, 6 + t, :].rearrange("p (h d) -> p h d", h=8),
                                          coef_h.unsqueeze(2).to_broadcast([P, 8, HD]), ALU.mult).then_inc(sem("cmp_out"), 1)
                        dve.wait_ge(sem("cmp_out"), t + 1)
                    for n in range(NT * HEADS):
                        t, h = n // HEADS, n % HEADS
                        K = n_keys(t)
                        dve.wait_ge(sem("idx_relu"), n + 1)
                        w = proj[:, t, WI + h:WI + h + 1]
                        if h == 0:
                            ins = dve.tensor_scalar(selbias[:, t, 0:K], relu_buf[:, n % 2, 0:K], w, None, ALU.mult)
                        else:
                            ins = dve.scalar_tensor_tensor(selbias[:, t, 0:K], relu_buf[:, n % 2, 0:K], w,
                                                           selbias[:, t, 0:K], ALU.mult, ALU.add)
                        ins.then_inc(sem("idx_acc"), 1)
                        dve.wait_ge(sem("idx_acc"), n + 1)
                    for t in range(NT):
                        K = n_keys(t)
                        s = selbias[:, t, 0:K]
                        causal = const[:, C_CAUSAL + SEQ - K:C_CAUSAL + SEQ]
                        seq(dve.scalar_tensor_tensor(s, s, IDX_SCALE, causal, ALU.mult, ALU.add))
                        for _ in range(TOPK_KEYS // 8):
                            seq(dve.max(best8, s))
                            seq(dve.match_replace(s, best8, s, TAKEN))
                        seq(dve.tensor_scalar(s, s, TAKEN, 1.0, ALU.is_equal, ALU.subtract))
                        seq(dve.scalar_tensor_tensor(s, s, -NEG, causal, ALU.mult, ALU.add))
                else:
                    for t in range(NT):
                        dve.wait_ge(sem(f"proj_mm{L}"), t + 1)
                    z = fox_zb
                    dve.tensor_tensor(z.rearrange("p (t n) -> p t n", t=NT), ps[:, 6, 0:NT * FOX_HEADS].rearrange("p (t n) -> p t n", t=NT),
                                          fox_b[:, :].unsqueeze(1).to_broadcast([P, NT, FOX_HEADS]), ALU.add)\
                       .then_inc(sem("fox_z"), 1)
                    dve.wait_ge(sem("fox_abs"), 1)
                    seq(dve.tensor_scalar(z, z, 0.0, None, ALU.min))
                    dve.wait_ge(sem("fox_ln"), 1)
                    dve.tensor_tensor(logf.rearrange("p t n -> p (t n)"), z, fox_t, ALU.subtract).then_inc(sem("logf"), 1)
                    for j in range(4):
                        dve.wait_ge(sem(f"proj_mm{L}"), NT + 2 * j + 2)
                        dve.tensor_copy(qkT[:, 4 * j + 2:4 * j + 4, :], ps[:, (2 * j + 1) % 4, :].rearrange("p (b n) -> p b n", b=2))\
                           .then_inc(sem(f"proj_t1_{L}"), 1)
                    dve.memset(aug_d, 1.0)
                    seq(dve.memset(aug_k, 1.0))
                    dve.wait_ge(sem("dcum"), 1)
                    for r0, dst in ((0, aug_d), (64, aug_d), (32, aug_k), (96, aug_k)):
                        ins = dve.tensor_scalar(dst[r0:r0 + FOX_HEADS], ps[0:FOX_HEADS, 7, 0:SEQ], 1.0 / SCALE, None, ALU.mult)
                    seq(ins)
                    dve.tensor_tensor(aug_q, aug_d.unsqueeze(1).to_broadcast([P, 8, SEQ]),
                                      const[:, C_DELTA:C_DELTA + 8].unsqueeze(2).to_broadcast([P, 8, SEQ]), ALU.mult)\
                       .then_inc(sem("aug"), 1)
                    for j in range(2):
                        dve.wait_ge(sem(f"proj_mm{L}"), NT + 8 + 2 * j + 2)
                        dve.tensor_copy(v_fox[:, 1, j * PIECE:(j + 1) * PIECE], ps[:, 2 * j + 1, :])\
                           .then_inc(sem(f"proj_t1_{L}"), 1)
                attention(L)
                copy_T("oT_dve", tp)
                tp += NT
                layer_norm(L, 1, lambda t, half: ps[:, 4 + 2 * t + half, :])
                copy_T("xT_dve", tp)
                tp += NT

                dve.wait_ge(sem("layer_loaded"), 48 * (L + 1))
                for t in range(NT):
                    s = sig[:, t, :]
                    dve.wait_ge(sem("router_e"), NT * L + t + 1)
                    seq(dve.tensor_scalar(s, s, 1.0, None, ALU.add))
                    seq(dve.reciprocal(s, s))
                    seq(dve.tensor_tensor(sb_, s, router_b[:, :], ALU.add))
                    for g in range(N_GROUPS):
                        ins = dve.max(gmax[:, g, :], sb_[:, g * 8:(g + 1) * 8])
                    seq(ins)
                    seq(dve.tensor_tensor(gscore, gmax[:, :, 0], gmax[:, :, 1], ALU.add))
                    seq(dve.max(best8, gscore))
                    seq(dve.memset(best8[:, TOP_GROUPS:8], -TAKEN))
                    seq(dve.match_replace(gscore, best8, gscore, TAKEN))
                    seq(dve.tensor_scalar(gscore, gscore, TAKEN, 1.0, ALU.is_equal, ALU.subtract))
                    gm = gscore.unsqueeze(2).to_broadcast([P, 8, 8])
                    seq(dve.tensor_scalar(gmask0, gscore, 1.0, None, ALU.add))
                    g0 = gmask0.unsqueeze(2).to_broadcast([P, 8, 8])
                    sb3 = sb_.rearrange("p (g e) -> p g e", g=8)
                    seq(dve.tensor_tensor(sb3, sb3, g0, ALU.mult))
                    seq(dve.scalar_tensor_tensor(sb3, gm, -NEG, sb3, ALU.mult, ALU.add))
                    seq(dve.max(best8, sb_))
                    seq(dve.match_replace(sb_, best8, sb_, TAKEN))
                    seq(dve.tensor_scalar(sb_, sb_, TAKEN, None, ALU.is_equal))
                    g1 = gates[:, t, :]
                    seq(dve.tensor_copy(chosen[:, t, :], sb_))
                    seq(dve.tensor_tensor(g1, s, sb_, ALU.mult))
                    seq(dve.tensor_reduce(rstd, g1, AX_X, ALU.add))
                    seq(dve.reciprocal(rstd, rstd))
                    dve.tensor_scalar(g1, g1, rstd, ROUTED_SCALE, ALU.mult, ALU.mult).then_inc(sem(f"router_dve{L}"), 1)
                    dve.wait_ge(sem(f"router_dve{L}"), t + 1)

                dve.wait_ge(sem("place_mm"), L + 1)
                for t in range(NT):
                    ins = dve.tensor_tensor(place[:, t, :], ps[:, 6 + t, 0:NE], chosen[:, t, :], ALU.mult)
                seq(ins)
                seq(dve.tensor_scalar(place, place, 1.0, None, ALU.subtract))
                dve.tensor_reduce(over_row, place, mybir.AxisListType.XY, ALU.max).then_inc(sem("place_max"), 1)
                seq(dve.scalar_tensor_tensor(gates_over, place, float(SLOTS), gates[:, :, :], ALU.is_ge, ALU.mult))
                dve.wait_ge(sem("shared_silu"), L + 1)
                dve.tensor_tensor(h_all, h_silu_all, ps[:, 5, :], ALU.mult).then_inc(sem("shared_h"), 1)

                M0 = L * PAIRS

                def later(m, n):
                    return M0 > 0 or not isinstance(m, int) or m >= n

                def sel_build(m, par):
                    if later(m, 2):
                        dve.wait_ge(sem("gathered"), m + (M0 - 1))
                        dve.wait_ge(sem("selT_tp"), m + (M0 - 1))
                    cols = slice(2 * m, 2 * m + 2) if isinstance(m, int) else bass.ds(2 * m, 2)
                    for t in range(NT):
                        ins = dve.tensor_tensor(sel[:, par, t, :].rearrange("p (e s) -> p e s", e=2),
                                                place[:, t, cols].unsqueeze(2).to_broadcast([P, 2, SLOTS]),
                                                const[:, C_IOTA:C_IOTA + SLOTS].unsqueeze(1).to_broadcast([P, 2, SLOTS]),
                                                ALU.is_equal)
                    ins.then_inc(sem("sel_built"), 1)

                def gate_h(m, par):
                    dve.wait_ge(sem("exp_silu"), m + (M0 + 1))
                    dve.wait_ge(sem("selT_copied"), m + (M0 + 1))
                    if later(m, 1):
                        dve.wait_ge(sem("hT_tp"), m + M0)
                    dve.scalar_tensor_tensor(h_exp, h_silu, slot_gate[:, par:par + 1], ps[:, 2, FE:2 * FE], ALU.mult, ALU.mult)\
                       .then_inc(sem("exp_h"), 1)

                def add_y(m, t):
                    dve.wait_ge(sem("scattered"), 2 * m + (2 * M0 + t + 1))
                    if later(m, 1):
                        dve.wait_ge(sem("y_added"), 2 * m + (2 * M0 + t - 1))
                    dve.tensor_tensor(y_acc[:, t, :], ps[:, 6:8, :].rearrange("p b n -> p (b n)"), y_acc[:, t, :], ALU.add)\
                       .then_inc(sem("y_added"), 1)

                def dve_step(m, u, build=True, add=True):
                    gate_h(m, u)
                    if build:
                        sel_build(m + 2, u)
                    if add:
                        add_y(m - 1, 0)
                        add_y(m - 1, 1)

                sel_build(0, 0)
                sel_build(1, 1)
                dve.wait_ge(sem("place_all"), L + 1)
                dve.tensor_scalar(over_int, over_all, float(SLOTS), None, ALU.is_ge).then_inc(sem("over_flag"), 1)
                dve.wait_ge(sem("shared_down"), L + 1)
                for t in range(NT):
                    ins = dve.tensor_copy(y_acc[:, t, :], ps[:, 2 * t:2 * t + 2, :].rearrange("p b n -> p (b n)"))
                ins.then_inc(sem("shared_added"), 1)
                dve.wait_ge(sem("shared_added"), L + 1)
                dve_step(0, 0, add=False)
                dve_step(1, 1)
                with dve.Fori(1, PAIRS // 2 - 1) as i:
                    for u in range(2):
                        dve_step(2 * i + u, u)
                dve_step(PAIRS - 2, 0, build=False)
                dve_step(PAIRS - 1, 1, build=False)
                add_y(PAIRS - 1, 0)
                add_y(PAIRS - 1, 1)
                dve.wait_ge(sem("y_added"), 2 * (M0 + PAIRS))

                flag = dve.value_load(over_int[0:1, 0:1], min_val=0, max_val=1)
                with dve.If(flag > 0):
                    with dve.Fori(0, NE) as e:
                        dve.wait_ge(sem(f"over_silu{L}"), e + 1)
                        dve.tensor_tensor(h_all, h_silu_all, ps[:, 5, :], ALU.mult).then_inc(sem(f"over_h{L}"), 1)
                        dve.wait_ge(sem(f"over_down{L}"), e + 1)
                        for t in range(NT):
                            ins = dve.scalar_tensor_tensor(y_acc[:, t, :], ps[:, 2 * t:2 * t + 2, :].rearrange("p b n -> p (b n)"),
                                                           gates_over[:, t, bass.ds(e, 1)], y_acc[:, t, :], ALU.mult, ALU.add)
                        ins.then_inc(sem(f"over_added{L}"), 1)
                    dve.wait_ge(sem(f"over_added{L}"), NE)

                layer_norm(L, 2, lambda t, half: y_acc[:, t, half * PIECE:(half + 1) * PIECE])
                copy_T("xT_dve", tp)
                tp += NT

                for t in range(NT):
                    dve.wait_ge(sem(f"ple_sq{L}"), t + 1)
                    rsqrt(ple_ss[:, t:t + 1], 1.0 / D, RMS_EPS)
                    dve.wait_ge(sem("gb_loaded"), 32 * (3 * L + 3))
                    seq(dve.scalar_tensor_tensor(y_acc[:, t, :], ps[:, 4 + 2 * t:6 + 2 * t, :].rearrange("p b n -> p (b n)"),
                                                 rstd, gb_row[:, 0, :], ALU.mult, ALU.mult))
                    dve.engine_nop().then_inc(sem("gb_used"), 1)
                for t in range(NT):
                    dve.wait_ge(sem(f"ple_sig{L}"), t + 1)
                    seq(dve.tensor_tensor(y_acc[:, t, :], y_acc[:, t, :], roped[:, t, 0:D], ALU.mult))
                    seq(dve.tensor_tensor(x_tok[:, t, :], x_tok[:, t, :], y_acc[:, t, :], ALU.add))
                    dve.engine_nop().then_inc(sem(f"ple_out{L}"), 1)


_INS = ['x', 'p', 'ev_w_in', 'ev_b_gate', 'ev_cmp_pos_k', 'ev_cmp_w1_k', 'ev_cmp_w2_k', 'ev_cmp_pos_v',
        'ev_cmp_w1_v', 'ev_cmp_w2_v', 'ev_w_o', 'od_w_in', 'od_b_f', 'od_w_o', 'ln1_g', 'ln1_b', 'ln2_g', 'ln2_b',
        'router_w', 'router_bias', 'exp_w1', 'exp_w3', 'exp_w2', 'sh_w1', 'sh_w3', 'sh_w2', 'ple_w_gate',
        'ple_w_proj', 'ple_norm_g']


def kernel(**inputs):
    import numpy as _np
    import concourse.bacc as _bacc
    from concourse import mybir as _mybir
    from concourse.bass_utils import run_bass_kernel_spmd as _run

    nc = _bacc.Bacc("TRN2", target_bir_lowering=False, num_devices=1)
    arrays, aps = {}, {}
    for name in _INS + ["const"]:
        v = constant_table() if name == "const" else _np.ascontiguousarray(inputs[name])
        arrays[f"in_{name}_dram"] = v
        aps[name] = nc.dram_tensor(f"in_{name}_dram", v.shape, _mybir.dt.from_np(v.dtype), kind="ExternalInput").ap()
    out = nc.dram_tensor("out_0_dram", (1, SEQ, D), _mybir.dt.float32, kind="ExternalOutput").ap()
    build_trunk(nc, aps, out)
    r = _run(nc, [arrays], core_ids=[0])
    return r.results[0]["out_0_dram"]
```

```python
from contextlib import ExitStack

import numpy as np
import concourse.bass as bass
from concourse import mybir

ALU = mybir.AluOpType
ACT = mybir.ActivationFunctionType
F32 = mybir.dt.float32
F32R = mybir.dt.float32r
BF16 = mybir.dt.bfloat16
AX_X = mybir.AxisListType.X

P = 128
D = 1024
DC = D // P
SEQ = 256
NT = SEQ // P
DEPTH = 2
HD = 64
PLE = 256
LN_EPS = 1e-5
RMS_EPS = 1e-6
NEG = -1e30
TAKEN = -3e38
ALPHA = (2.0 * DEPTH) ** 0.25
SCALE = HD ** -0.5

HEADS = 8
FOX_HEADS = 16
IDX_SCALE = (8 * 64) ** -0.5
TOPK_KEYS = 64
CMP_LEN = 32
CMP_STRIDE = 16
N_CMP = (SEQ - CMP_LEN) // CMP_STRIDE + 1
CMP_PAD = 16

NE = 64
TOP_E = 8
N_GROUPS = 8
TOP_GROUPS = 4
FE = 256
ROUTED_SCALE = 2.5

QA, KA, VA, QI, KI, WI, QB, KC, VC, KS, VS, KW, VW, GB = (
    0, 512, 576, 640, 1152, 1216, 1224, 1736, 1800, 1864, 1928, 1992, 2056, 2120)
EVEN_COLS = 2144
ODD_COLS = 3 * D + FOX_HEADS

SLOTS = 64
PAIRS = NE // 2
RING = 4
SLOT = 6144
PIECE = 512
UNROLL = 4
EARLY_ROUNDS = 5

C_ID = 0
C_CAUSAL = C_ID + P
C_TRI = C_CAUSAL + SEQ
C_COS = C_TRI + 2 * SEQ
C_SIN = C_COS + NT * 32
C_CCOS = C_SIN + NT * 32
C_CSIN = C_CCOS + 32
C_CBIAS = C_CSIN + 32
C_CVALID = C_CBIAS + NT * CMP_PAD
C_REP = C_CVALID + NT * CMP_PAD
C_BD = C_REP + P
C_DELTA = C_BD + HEADS
C_IOTA = C_DELTA + FOX_HEADS // 2
C_END = C_IOTA + SLOTS


def constant_table():
    t = np.zeros((P, C_END), np.float32)
    r = np.arange(P)
    t[:, C_ID:C_ID + P] = np.eye(P)
    t[:, C_CAUSAL + P:C_CAUSAL + SEQ] = np.where(r[None, :] > r[:, None], NEG, 0.0)
    for c in range(NT):
        tok, pos = c * P + r, np.arange(SEQ)
        t[:, C_TRI + c * SEQ:C_TRI + (c + 1) * SEQ] = tok[:, None] <= pos[None, :]
    inv = 1.0 / (10000.0 ** (np.arange(0, HD, 2, dtype=np.float32) / HD))
    ang = np.arange(SEQ, dtype=np.float32)[:, None] * inv.astype(np.float32)[None, :]
    cos, sin = np.cos(ang), np.sin(ang)
    last = np.arange(N_CMP) * CMP_STRIDE + CMP_LEN - 1
    for c in range(NT):
        t[:, C_COS + 32 * c:C_COS + 32 * c + 32] = cos[c * P:(c + 1) * P]
        t[:, C_SIN + 32 * c:C_SIN + 32 * c + 32] = sin[c * P:(c + 1) * P]
        ok = np.zeros((P, CMP_PAD), bool)
        ok[:, :N_CMP] = last[None, :] <= (c * P + r)[:, None]
        t[:, C_CBIAS + CMP_PAD * c:C_CBIAS + CMP_PAD * (c + 1)] = np.where(ok, 0.0, NEG)
        t[:, C_CVALID + CMP_PAD * c:C_CVALID + CMP_PAD * (c + 1)] = ok
    t[:N_CMP, C_CCOS:C_CCOS + 32] = cos[last]
    t[:N_CMP, C_CSIN:C_CSIN + 32] = sin[last]
    for c in range(CMP_PAD):
        t[c, C_REP + c:C_REP + P:CMP_PAD] = 1.0
    for s in range(HEADS):
        t[s * CMP_PAD:(s + 1) * CMP_PAD, C_BD + s] = 1.0
    for h in range(FOX_HEADS):
        t[64 * (h % 2) + h, C_DELTA + h // 2] = 1.0
        t[64 * (h % 2) + 32 + h, C_DELTA + h // 2] = -1.0
    t[:, C_IOTA:C_IOTA + SLOTS] = np.arange(SLOTS)
    return t


def build_trunk(nc, a, out):
    with ExitStack() as ctx:
        def sb(name, *shape):
            return ctx.enter_context(nc.sbuf_tensor(name, [P, *shape], F32))

        sems = {}

        def sem(name):
            if name not in sems:
                sems[name] = ctx.enter_context(nc.semaphore(name))
            return sems[name]

        ps = ctx.enter_context(nc.psum_tensor("ps", [P, 8, 512], F32))

        ring = sb("ring", RING, SLOT)
        const = sb("const", C_END)
        x_tok = sb("x_tok", NT, D)
        xT = sb("xT", DC, SEQ)
        proj = sb("proj", NT, EVEN_COLS)
        qkT = sb("qkT", 17, SEQ)
        qkT_at = nc.sbuf_base - 17 * SEQ * 4
        y_hi = nc.alloc_sbuf_tensor_at("y_hi", [P, D], F32R, offset=qkT_at)
        y_lo = nc.alloc_sbuf_tensor_at("y_lo", [P, D], F32R, offset=qkT_at + 4 * D)
        selT = nc.alloc_sbuf_tensor_at("selT", [P, 2, SEQ], F32R, offset=qkT_at + 8 * D)
        x_part3 = nc.alloc_sbuf_tensor_at("x_part3", [P, NT, D], BF16, offset=qkT_at + 10 * D)
        sel_bf = nc.alloc_sbuf_tensor_at("sel_bf", [P, 2, NT, P], BF16, offset=qkT_at + 14 * D)
        roped = sb("roped", NT, 2048)
        pT = sb("pT", 2, 1024)
        pT_at = nc.sbuf_base - 2 * 1024 * 4
        x_part1 = nc.alloc_sbuf_tensor_at("x_part1", [P, NT, D], BF16, offset=pT_at)
        x_part2 = nc.alloc_sbuf_tensor_at("x_part2", [P, NT, D], BF16, offset=pT_at + 4 * D)
        x_parts = (x_part1, x_part2, x_part3)
        o_tok = sb("o_tok", NT, D)
        gb_row = sb("gb_row", 2, D)
        router_w = sb("router_w", DC, NE)
        router_b = sb("router_b", NE)
        p_tok = sb("p_tok", NT, PLE)
        bgate = sb("bgate", 24)
        fox_b = sb("fox_b", FOX_HEADS)
        small = sb("small", 1024)
        stats = sb("stats", NT, 2, 6)
        selbias = sb("selbias", NT, SEQ)
        gates = sb("gates", NT, NE)

        rows = sb("rows", 512)
        over_int = ctx.enter_context(nc.sbuf_tensor("over_int", [P, 1], mybir.dt.int32))[:, :]

        scores = roped[:, :, :].rearrange("p t n -> p (t n)").rearrange("p (u n) -> p u n", u=4)
        cmp_w1 = o_tok[:, :, :].rearrange("p t n -> p (t n)").rearrange("p (l f) -> p l f", l=CMP_LEN)
        h_silu_all = roped[:, 0, 0:512]
        h_all = roped[:, 0, 512:1024]
        y_acc = o_tok

        tmp_o = sb("tmp_o", 512)[:, :]
        cmp_blk = tmp_o[:, 0:CMP_LEN * N_CMP].rearrange("p (l n) -> p l n", l=CMP_LEN)
        rope_tmp = sb("rope_tmp", SEQ)
        cmp_s = small[:, 512:768].rearrange("p (t n) -> p t n", t=NT)
        cmp_all = cmp_s.rearrange("p t (s c) -> p (t s) c", s=8)
        small_pT = small[:, 768:1024].rearrange("p (t n) -> p t n", t=NT)
        v_bd = pT[:, 1, 0:512]
        v_fox = proj[:, :, :].rearrange("p t n -> p (t n)")[:, 0:NT * D].rearrange("p (t n) -> p t n", t=NT)
        logf = small[:, 64:64 + NT * FOX_HEADS].rearrange("p (t n) -> p t n", t=NT)
        aug_k = small[:, 256:512]
        proj_flat = proj[:, :, :].rearrange("p t n -> p (t n)")
        aug_q = proj_flat[:, NT * D:NT * D + 8 * SEQ].rearrange("p (h n) -> p h n", h=8)
        aug_d = small[:, 512:768]
        x_rest = proj_flat[:, 0:D]
        xe = proj_flat[:, 1024:3072].rearrange("p (b c n) -> p b c n", b=2, c=DC)
        sel = proj_flat[:, 3072:3584].rearrange("p (b t n) -> p b t n", b=2, t=NT)
        hT = proj_flat[:, 3584:3840].rearrange("p (f n) -> p f n", f=2)
        h_silu = roped[:, 0, 1536:1792]
        h_exp = roped[:, 0, 1792:2048]
        slot_gate = rows[:, 492:494]
        chosen = roped[:, 1, 0:128].rearrange("p (t n) -> p t n", t=NT)
        place = roped[:, 1, 128:256].rearrange("p (t n) -> p t n", t=NT)
        gates_over = roped[:, 1, 256:384].rearrange("p (t n) -> p t n", t=NT)
        over_row = rows[:, 490:491]
        over_all = rows[:, 491:492]
        ple_pT = pT[:, 0, 0:512].rearrange("p (c n) -> p c n", c=2)

        relu_buf = pT[:, :, :].rearrange("p a n -> p (a n)").rearrange("p (b n) -> p b n", b=8)
        neg_max = rows[:, 0:8].rearrange("p (u s) -> p u s", u=2)
        denom = gates[:, 0, 0:32].rearrange("p (g s) -> p g s", g=4)
        coef = rows[:, 24:32]
        coef_h = rows[:, 32:40]
        mean_var = rows[:, 40:42]
        rstd = rows[:, 42:43]
        ple_ss = rows[:, 43:45]
        best8 = rows[:, 48:56]
        gscore = rows[:, 56:64]
        gmask0 = rows[:, 64:72]
        gmax = rows[:, 72:136].rearrange("p (g e) -> p g e", g=8)
        gate_sig = rows[:, 136:184]
        cmp_m = rows[:, 184:200]
        fox_t = rows[:, 200:232]
        fox_zb = rows[:, 232:264]
        sb_ = rows[:, 264:328]
        sig = rows[:, 328:456].rearrange("p (t n) -> p t n", t=NT)
        peT = rows[:, 456:488]
        var_eps = rows[:, 488:489]
        newton = rows[:, 489:490]
        kvT = small[:, 512:768]

        ident = const[:, C_ID:C_ID + P]
        block = ctx.enter_context(nc.Block())

        items = []

        def static_item(parts, release):
            items.append((parts, release))

        def piece(w, c0, c1):
            n = c1 - c0
            return ((0, DC * n), (DC, n), w.rearrange("(p c) n -> p c n", c=DC)[:, :, c0:c1])

        proj_pieces = {
            0: [(512, 1024), (1024, 1536), (0, 512), (1536, 2048), (2048, EVEN_COLS)],
            1: [(3 * D, ODD_COLS)] + [(c, c + PIECE) for c in range(0, 3 * D, PIECE)],
        }
        first_item = {}
        shared_item = {}
        for L in range(DEPTH):
            w_in = a["ev_w_in"][0] if L % 2 == 0 else a["od_w_in"][0]
            w_o = a["ev_w_o"][0] if L % 2 == 0 else a["od_w_o"][0]
            first_item[L] = len(items)
            for n, (c0, c1) in enumerate(proj_pieces[L % 2]):
                static_item([piece(w_in, c0, c1)], ("proj_mm", L, n))
            for n in range(2):
                static_item([piece(w_o, n * PIECE, (n + 1) * PIECE)], ("wo_mm", L, n))
            shared_item[L] = len(items)
            items.append(("shared", ("shared_down", L, 0)))
            for e in range(NE):
                items.append(("expert", ("exp_down", L, e)))
            static_item([((0, 2 * D), (2, D), a["ple_w_proj"][L].rearrange("(p c) n -> p c n", c=2))], ("ple_mm", L, 0))
            for n in range(2):
                static_item([piece(a["ple_w_gate"][L], n * PIECE, (n + 1) * PIECE)], ("ple_mm", L, 1 + n))

        def release_value(rel):
            what, L, n = rel
            if what == "proj_mm":
                return sem(f"proj_mm{L}"), NT * (n + 1)
            if what == "wo_mm":
                return sem(f"wo_mm{L}"), 2 * (NT - 1) + n + 1
            if what == "shared_down":
                return sem("shared_down"), NT * (L + 1)
            if what == "exp_down":
                return sem("exp_down"), L * PAIRS + n // 2 + 1
            return sem(f"ple_mm{L}"), NT * 2 + n if n else NT

        loaded, down_loaded_at = [], []
        total, down_total = [0] * RING, [0] * RING
        for k, (parts, _) in enumerate(items):
            ffn = parts in ("shared", "expert")
            total[k % RING] += 16 * (2 if ffn else len(parts))
            down_total[k % RING] += 16 if ffn else 0
            loaded.append(total[k % RING])
            down_loaded_at.append(down_total[k % RING])
        w_loaded = [sem(f"w_loaded{s}") for s in range(RING)]
        down_loaded = [sem(f"down_loaded{s}") for s in range(RING)]

        def slot_view(k, n, c):
            return ring[:, k % RING, 0:c * n].rearrange("p (c n) -> p c n", c=c)

        def wait_item(eng, k):
            eng.wait_ge(w_loaded[k % RING], loaded[k])
            if items[k][0] == "shared":
                eng.wait_ge(down_loaded[k % RING], down_loaded_at[k])

        UP_N = DC * FE
        DOWN0 = 2 * UP_N

        def ffn_views(slot):
            w1 = ring[:, slot, 0:UP_N].rearrange("p (c f) -> p c f", c=DC)
            w3 = ring[:, slot, UP_N:2 * UP_N].rearrange("p (c f) -> p c f", c=DC)
            w2 = ring[:, slot, DOWN0:DOWN0 + 2 * D].rearrange("p (c n) -> p c n", c=2)
            return w1, w3, w2

        def by_f(h, t):
            return h.rearrange("p (f n) -> p f n", f=2)[:, :, t * P:(t + 1) * P]

        QKT_BATCHES = [((5, 6, 7, 8), 0), ((9,), 2), ((0, 1, 2, 3), 0), ((4,), 2), ((10, 11, 12, 13), 0), ((14, 15), 2)]

        def rope_views(t, src, n, dst):
            return (proj[:, t, src:src + n * HD].rearrange("p (n h k) -> p n h k", n=n, h=2),
                    roped[:, t, dst * HD:(dst + n) * HD].rearrange("p (n h k) -> p n h k", n=n, h=2),
                    const[:, C_COS + 32 * t:C_COS + 32 * t + 32], const[:, C_SIN + 32 * t:C_SIN + 32 * t + 32])

        def rope(eng, step, src, dst, cs, sn, tmp, rows_=P):
            n = src.shape[1]
            c = cs.unsqueeze(1).unsqueeze(1)
            s = sn.unsqueeze(1).to_broadcast([rows_, n, 32])
            tmp = tmp[0:rows_, 0:n * 32].rearrange("p (n k) -> p n k", n=n)
            step(eng.tensor_tensor(tmp, src[:, :, 1, :], s, ALU.mult))
            step(eng.tensor_tensor(dst, src, c.to_broadcast([rows_, n, 2, 32]), ALU.mult))
            step(eng.tensor_tensor(dst[:, :, 0, :], dst[:, :, 0, :], tmp, ALU.subtract))
            step(eng.tensor_tensor(tmp, src[:, :, 0, :], s, ALU.mult))
            return eng.tensor_tensor(dst[:, :, 1, :], dst[:, :, 1, :], tmp, ALU.add)

        @block.sync
        def _(sp):
            rows_of = "(p c) f -> p (c f)"

            def up_load(slot, w1, w3):
                sp.dma_start(ring[:, slot, 0:UP_N], w1.rearrange(rows_of, c=DC)).then_inc(w_loaded[slot], 16)
                sp.dma_start(ring[:, slot, UP_N:2 * UP_N], w3.rearrange(rows_of, c=DC)).then_inc(w_loaded[slot], 16)

            def down_load(slot, w2):
                sp.dma_start(ring[:, slot, DOWN0:DOWN0 + 2 * D], w2.rearrange(rows_of, c=2)).then_inc(down_loaded[slot], 16)

            def ffn_load(slot, w1, w3, w2):
                up_load(slot, w1, w3)
                down_load(slot, w2)

            def over_load(L, e):
                up = rows_of
                done = sem(f"over_loaded{L}")
                sp.dma_start(ring[:, 0, 0:UP_N], a["exp_w1"][L, e].rearrange(up, c=DC)).then_inc(done, 16)
                sp.dma_start(ring[:, 0, UP_N:2 * UP_N], a["exp_w3"][L, e].rearrange(up, c=DC)).then_inc(done, 16)
                sp.dma_start(ring[:, 0, DOWN0:DOWN0 + 2 * D], a["exp_w2"][L, e].rearrange(up, c=2)).then_inc(done, 16)

            sp.dma_start(x_tok[:, 0, :], a["x"][0, 0:P, :]).then_inc(sem("x_loaded0"), 16)
            sp.dma_start(ident, a["const"][:, C_ID:C_ID + P]).then_inc(sem("ident_loaded"), 16)
            sp.dma_start(x_tok[:, 1, :], a["x"][0, P:SEQ, :]).then_inc(sem("x_loaded1"), 16)
            for L in range(DEPTH):
                k = first_item[L]
                e0 = shared_item[L] + 1
                end = e0 + NE + 3
                while k < end:
                    if k == e0 + UNROLL:
                        with sp.Fori(1, NE // UNROLL) as i:
                            for u in range(0, UNROLL, 2):
                                sp.wait_ge(sem("exp_up"), i * 2 + (L * PAIRS + u // 2 - 1))
                                for v in (u, u + 1):
                                    up_load((e0 + v) % RING, a["exp_w1"][L, i * UNROLL + v], a["exp_w3"][L, i * UNROLL + v])
                                sp.wait_ge(sem("exp_down"), i * 2 + (L * PAIRS + u // 2 - 1))
                                for v in (u, u + 1):
                                    down_load((e0 + v) % RING, a["exp_w2"][L, i * UNROLL + v])
                        k = e0 + NE
                        sp.wait_ge(sem("over_flag"), L + 1)
                        flag = sp.value_load(over_int[0:1, 0:1], min_val=0, max_val=1)
                        with sp.If(flag > 0):
                            sp.wait_ge(sem("exp_down"), (L + 1) * PAIRS)
                            over_load(L, 0)
                            with sp.Fori(1, NE) as e:
                                sp.wait_ge(sem(f"over_added{L}"), e)
                                over_load(L, e)
                            sp.wait_ge(sem(f"over_added{L}"), NE)
                        continue
                    if k >= RING:
                        sp.wait_ge(*release_value(items[k - RING][1]))
                    parts = items[k][0]
                    if parts == "shared":
                        ffn_load(k % RING, a["sh_w1"][L], a["sh_w3"][L], a["sh_w2"][L])
                    elif parts == "expert":
                        e = k - e0
                        ffn_load(k % RING, a["exp_w1"][L, e], a["exp_w3"][L, e], a["exp_w2"][L, e])
                    else:
                        for (lo, hi), (c, n), src in parts:
                            sp.dma_start(slot_view(k, n, c), src).then_inc(w_loaded[k % RING], 16)
                    if k == 0:
                        sp.dma_start(const[:, P:C_END], a["const"][:, P:C_END]).then_inc(sem("const_loaded"), 16)
                    k += 1
            for t in range(NT):
                sp.wait_ge(sem(f"ple_out{DEPTH - 1}"), t + 1)
                sp.dma_start(out[0, t * P:(t + 1) * P, :], x_tok[:, t, :]).then_inc(sem("out_stored"), 16)
            sp.wait_ge(sem("out_stored"), 16 * NT)

        @block.gpsimd
        def _(pool):
            pool.memset(small[:, 0:1024], 0.0).then_inc(sem("small_zero"), 1)
            pool.dma_start(bgate[:, :], a["ev_b_gate"][0].partition_broadcast(P)).then_inc(sem("bias_loaded"), 16)
            pool.dma_start(fox_b[:, :], a["od_b_f"][0].partition_broadcast(P)).then_inc(sem("bias_loaded"), 16)
            pe_t = qkT[:, 16, 0:2 * HD]
            pool.dma_start(pe_t[0:CMP_LEN, 0:HD], a["ev_cmp_pos_k"][0]).then_inc(sem("cmp_loaded"), 16)
            pool.dma_start(pe_t[0:CMP_LEN, HD:2 * HD], a["ev_cmp_pos_v"][0]).then_inc(sem("cmp_loaded"), 16)
            pool.dma_start(cmp_w1[0:HD], a["ev_cmp_w1_k"][0].rearrange("(l d) f -> d l f", d=HD)).then_inc(sem("cmp_loaded"), 16)
            pool.dma_start(cmp_w1[HD:P], a["ev_cmp_w1_v"][0].rearrange("(l d) f -> d l f", d=HD)).then_inc(sem("cmp_loaded"), 16)
            pool.wait_ge(sem("small_zero"), 1)
            pool.dma_start(small[0:HD, 0:HD], a["ev_cmp_w2_k"][0]).then_inc(sem("cmp_loaded"), 16)
            pool.dma_start(small[0:HD, HD:2 * HD], a["ev_cmp_w2_v"][0]).then_inc(sem("cmp_loaded"), 16)
            def load_layer(L):
                if L:
                    pool.wait_ge(sem(f"router_mm{L - 1}"), NT)
                    pool.wait_ge(sem(f"router_dve{L - 1}"), NT)
                    pool.wait_ge(sem(f"pT_tp{L - 1}"), NT)
                pool.dma_start(router_w[:, :, :], a["router_w"][L].rearrange("(p c) n -> p c n", c=DC)).then_inc(sem("layer_loaded"), 16)
                pool.dma_start(router_b[:, :], a["router_bias"][L].partition_broadcast(P)).then_inc(sem("layer_loaded"), 16)
                pool.dma_start(p_tok[:, :, :], a["p"][L, 0].rearrange("(t p) n -> p t n", p=P)).then_inc(sem("layer_loaded"), 16)
                load_rows(L, 0)

            def load_rows(L, n):
                g, b = (("ln1_g", "ln1_b"), ("ln2_g", "ln2_b"), ("ple_norm_g", "ple_norm_g"))[n]
                if 3 * L + n:
                    pool.wait_ge(sem("gb_used"), NT * (3 * L + n))
                pool.dma_start(gb_row[:, 0, :], a[g][L].partition_broadcast(P)).then_inc(sem("gb_loaded"), 16)
                pool.dma_start(gb_row[:, 1, :], a[b][L].partition_broadcast(P)).then_inc(sem("gb_loaded"), 16)

            load_layer(0)
            steps = [0]

            def step(ins):
                steps[0] += 1
                ins.then_inc(sem("pool_step"), 1)
                pool.wait_ge(sem("pool_step"), steps[0])

            pool.wait_ge(sem("const_loaded"), 16)
            for n, (src, heads, dst) in enumerate(((QB, 8, 20), (KS, 1, 28), (KW, 1, 30))):
                for t in range(NT):
                    pool.wait_ge(sem(f"proj_t{t}_0"), (4, 4, 5)[n])
                    ins = rope(pool, step, *rope_views(t, src, heads, dst), rope_tmp[:, :])
                    if t < NT - 1:
                        step(ins)
                ins.then_inc(sem("roped_nsa"), 1)
                pool.wait_ge(sem("roped_nsa"), n + 1)
            for L in range(DEPTH):
                if L:
                    load_layer(L)
                for t in range(NT):
                    pool.wait_ge(sem(f"ln1_out{L}"), t + 1)
                    rest = x_tok[:, t, :]
                    for part in (x_part1, x_part2):
                        step(pool.tensor_copy(part[:, t, :], rest))
                        step(pool.tensor_tensor(x_rest, rest, part[:, t, :], ALU.subtract))
                        rest = x_rest
                    pool.tensor_copy(x_part3[:, t, :], rest).then_inc(sem("x_split"), 1)
                    pool.wait_ge(sem("x_split"), NT * L + t + 1)
                pool.wait_ge(sem("place_max"), L + 1)
                pool.partition_all_reduce(over_all, over_row, P, bass.bass_isa.ReduceOp.max).then_inc(sem("place_all"), 1)
                load_rows(L, 1)
                load_rows(L, 2)

        UNITS = {0: [("sel", t, g) for t in range(NT) for g in range(2)]
                 + [("win", t, g) for t in range(NT) for g in range(2)]
                 + [("dsa", t, g) for t in range(NT) for g in range(2)],
                 1: [("fox", t, g) for t in range(NT) for g in range(4)]}
        BRANCH = {"sel": (20, 28, VS), "win": (20, 30, VW), "dsa": (0, 8, VA)}

        def n_keys(t):
            return (t + 1) * P

        def unit_slots(g):
            return [4 * g + 2 * j + parity for parity in range(2) for j in range(2)]

        @block.tensor
        def _(pe):
            def transpose_tile(src, t):
                for c in range(DC):
                    ins = pe.transpose(ps[:, 2 * t + c // 4, (c % 4) * P:(c % 4 + 1) * P],
                                       src[:, t, c::DC], ident)
                ins.then_inc(sem("xT_tp"), 1)

            def wait_tile(name, j, t):
                pe.wait_ge(sem(name + "_act"), NT * j + t + 1)
                if t > 0:
                    pe.wait_ge(sem(name + "_dve"), (NT - 1) * j + t)

            def attention(L):
                units = UNITS[L % 2]
                for u in range(len(units) + 3):
                    if u < len(units):
                        what, t, g = units[u]
                        K = n_keys(t)
                        if u >= 2:
                            pe.wait_ge(sem(f"sc_biased{L}"), u - 1)
                        for s, h in enumerate(unit_slots(g)):
                            o = ps[:, 2 * (u % 2) + s // 2, (s % 2) * K:(s % 2 + 1) * K]
                            r = slice(HD * (h % 2), HD * (h % 2) + HD)
                            if what == "fox":
                                ra = r
                                ins = pe.matmul(o, qkT[r, h // 2, t * P:(t + 1) * P], qkT[r, 8 + h // 2, 0:K],
                                                start=True, stop=False)
                                ins = pe.matmul(o, aug_q[ra, h // 2, t * P:(t + 1) * P], aug_k[ra, 0:K],
                                                start=False, stop=True)
                            else:
                                q0, k0, _ = BRANCH[what]
                                ins = pe.matmul(o, qkT[r, (q0 + h) // 2, t * P:(t + 1) * P],
                                                qkT[r, k0 // 2, 0:K], start=True, stop=True)
                        ins.then_inc(sem(f"sc_mm{L}"), 1)
                    if L == 0 and u == 1:
                        pe.wait_ge(sem("cmp_p"), NT)
                        for tt in range(NT):
                            ins = pe.transpose(ps[:, 6, tt * P:(tt + 1) * P], cmp_s[:, tt, :], ident)
                        ins.then_inc(sem("cmp_pT"), 1)
                    if L == 0 and u == 2:
                        pe.wait_ge(sem("cmp_pT_copied"), 1)
                        for tt in range(NT):
                            ins = pe.matmul(ps[:, 6 + tt, :], small_pT[:, tt, :], v_bd, start=True, stop=True)
                        ins.then_inc(sem("cmp_o"), 1)
                    if 2 <= u < len(units) + 2:
                        v = u - 2
                        what, t, g = units[v]
                        pe.wait_ge(sem(f"sc_exp{L}"), v + 1)
                        if v:
                            pe.wait_ge(sem(f"pT_copied{L}"), v)
                        for s in range(4):
                            for c in range(t + 1):
                                b = s * (t + 1) + c
                                ins = pe.transpose(ps[:, 4 + b // 4, (b % 4) * P:(b % 4 + 1) * P],
                                                   scores[:, v % 4, s * n_keys(t) + c * P:s * n_keys(t) + (c + 1) * P],
                                                   ident)
                        ins.then_inc(sem(f"pT_tp{L}u"), 1)
                    if u >= 3:
                        v = u - 3
                        what, t, g = units[v]
                        if L == 0 and v == 0:
                            pe.wait_ge(sem("cmp_out"), NT)
                        pe.wait_ge(sem(f"pT_copied{L}"), v + 1)
                        grp = v // 2
                        if v % 2 == 0 and grp >= 2:
                            pe.wait_ge(sem(f"pv_out{L}"), grp - 1)
                        for h, s in sorted((h, s) for s, h in enumerate(unit_slots(g))):
                            hh = h % 8
                            v0, v_end = (h * HD, D) if what == "fox" else (BRANCH[what][2], EVEN_COLS)
                            wide = min(2 * HD, v_end - v0, PIECE - hh * HD)
                            for c in range(t + 1):
                                vals = (v_fox if what == "fox" else proj)[:, c, v0:v0 + wide]
                                ins = pe.matmul(ps[:, 6 + grp % 2, hh * HD:hh * HD + wide],
                                                pT[:, v % 2, (s * (t + 1) + c) * P:(s * (t + 1) + c + 1) * P],
                                                vals, start=(c == 0), stop=(c == t))
                        ins.then_inc(sem(f"pv_mm{L}"), 1)

            pe.wait_ge(sem("ident_loaded"), 16)
            for L in range(DEPTH):
                if L % 2 == 0:
                    for t in range(NT):
                        if L == 0:
                            pe.wait_ge(sem(f"x_loaded{t}"), 16)
                        else:
                            pe.wait_ge(sem(f"ple_out{L - 1}"), t + 1)
                        transpose_tile(x_tok, t)
                    for t in range(NT):
                        wait_tile("xT", 3 * L, t)
                if L % 2 == 0:
                    def project(j):
                        c0, c1 = proj_pieces[0][j]
                        k = first_item[L] + j
                        wait_item(pe, k)
                        w = slot_view(k, c1 - c0, DC)
                        for t in range(NT):
                            if j >= 2:
                                pe.wait_ge(sem(f"proj_t{t}_{L}"), j - 1)
                            for c in range(DC):
                                ins = pe.matmul(ps[:, 4 + (2 * j + t) % 4, 0:c1 - c0], xT[:, c, t * P:(t + 1) * P],
                                                w[:, c, :], start=(c == 0), stop=(c == DC - 1))
                            ins.then_inc(sem(f"proj_mm{L}"), 1)

                    def transpose_pairs(m):
                        blocks, bank = QKT_BATCHES[m]
                        for n, b in enumerate(blocks):
                            for t in range(NT):
                                ins = pe.transpose(ps[:, bank + n // 2, (n % 2) * SEQ + t * P:(n % 2) * SEQ + (t + 1) * P],
                                                   roped[:, t, b * P:(b + 1) * P], ident)
                        ins.then_inc(sem("qkT_tp"), 1)

                    for j in range(3):
                        project(j)
                    pe.wait_ge(sem("const_loaded"), 16)
                    pe.wait_ge(sem("roped_dsa"), 1)
                    pe.wait_ge(sem("dup"), 1)
                    transpose_pairs(0)
                    transpose_pairs(1)
                    project(3)
                    for t in range(NT):
                        pe.wait_ge(sem(f"proj_t{t}_0"), 4)
                    for t in range(NT):
                        pe.transpose(ps[:, 6, t * P:(t + 1) * P], proj[:, t, KC:KC + P], ident)
                    pe.wait_ge(sem("cmp_loaded"), 96)
                    pe.transpose(ps[:, 7, 0:CMP_LEN], qkT[0:CMP_LEN, 16, 0:P], ident[0:CMP_LEN, 0:CMP_LEN])\
                        .then_inc(sem("cmp_tp"), 1)
                    pe.wait_ge(sem("qkT_copied"), 2)
                    for n in range(NT * HEADS):
                        t, h = n // HEADS, n % HEADS
                        r = slice(HD * (h % 2), HD * (h % 2) + HD)
                        if n >= 4:
                            pe.wait_ge(sem("idx_relu"), n - 3)
                        pe.matmul(ps[:, n % 4, 0:n_keys(t)], qkT[r, (10 + h) // 2, t * P:(t + 1) * P],
                                  qkT[r, 9, 0:n_keys(t)], start=True, stop=True).then_inc(sem("idx_mm"), 1)
                    pe.wait_ge(sem("cmp_blk"), 1)
                    for l in range(CMP_LEN):
                        for half in range(2):
                            r = slice(HD * half, HD * half + HD)
                            ins = pe.matmul(ps[0:HD, 6 + half, 0:N_CMP], cmp_w1[r, l, :],
                                            cmp_blk[r, l, :], start=(l == 0), stop=(l == CMP_LEN - 1))
                    ins.then_inc(sem("cmp_h"), 1)
                    project(4)
                    pe.wait_ge(sem("cmp_hs"), 1)
                    for half in range(2):
                        ins = pe.matmul(ps[0:N_CMP, 6, half * HD:(half + 1) * HD],
                                        small[0:HD, 128 + 16 * half:128 + 16 * half + N_CMP],
                                        small[0:HD, half * HD:(half + 1) * HD], start=True, stop=True)
                    ins.then_inc(sem("cmp_kv"), 1)
                    pe.wait_ge(sem("roped_dsa"), 3)
                    pe.wait_ge(sem("dup"), 2)
                    pe.wait_ge(sem("idx_relu"), NT * HEADS)
                    transpose_pairs(2)
                    transpose_pairs(3)
                    pe.wait_ge(sem("cmp_roped"), 1)
                    pe.transpose(ps[:, 7, 0:CMP_PAD], small[0:CMP_PAD, 256:384], ident[0:CMP_PAD, 0:CMP_PAD])
                    pe.matmul(ps[:, 6, 0:HD], const[0:CMP_PAD, C_REP:C_REP + P], small[0:CMP_PAD, 384:448],
                              start=True, stop=True).then_inc(sem("cmp_rep"), 1)
                    pe.wait_ge(sem("roped_nsa"), 3)
                    pe.wait_ge(sem("dup"), 4)
                    pe.wait_ge(sem("qkT_copied"), 4)
                    transpose_pairs(4)
                    transpose_pairs(5)
                    pe.wait_ge(sem("cmp_kT"), 1)
                    pe.wait_ge(sem("qkT_copied"), 6)
                    for t in range(NT):
                        for j in range(HEADS // 2):
                            c0 = t * P + 2 * j * CMP_PAD
                            ins = pe.matmul(ps[:, 7, c0:c0 + 2 * CMP_PAD], qkT[:, 10 + j, t * P:(t + 1) * P],
                                            small[:, 448:448 + 2 * CMP_PAD], start=True, stop=True)
                    ins.then_inc(sem("cmp_sc"), 1)
                else:
                    kf, kq = first_item[L], first_item[L] + 1
                    pe.wait_ge(sem(f"ple_out{L - 1}"), 1)
                    transpose_tile(x_tok, 0)
                    for t in range(NT):
                        wait_tile("xT", 3 * L, t)
                        if t == 0:
                            wait_item(pe, kf)
                            wait_item(pe, kq)
                        w = slot_view(kf, FOX_HEADS, DC)
                        for c in range(DC):
                            ins = pe.matmul(ps[:, 6, t * FOX_HEADS:(t + 1) * FOX_HEADS], xT[:, c, t * P:(t + 1) * P],
                                            w[:, c, :], start=(c == 0), stop=(c == DC - 1))
                        ins.then_inc(sem(f"proj_mm{L}"), 1)
                        w = slot_view(kq, PIECE, DC)
                        for b in range(4):
                            if b == 2 and t == 0:
                                pe.wait_ge(sem(f"ple_out{L - 1}"), 2)
                                transpose_tile(x_tok, 1)
                            for c in range(DC):
                                ins = pe.matmul(ps[:, b // 2, (b % 2) * SEQ + t * P:(b % 2) * SEQ + (t + 1) * P],
                                                w[:, c, b * P:(b + 1) * P], xT[:, c, t * P:(t + 1) * P],
                                                start=(c == 0), stop=(c == DC - 1))
                            if t == NT - 1 and b % 2 == 1:
                                ins.then_inc(sem(f"proj_mm{L}"), 1)
                    for j in range(1, 4):
                        k = first_item[L] + 1 + j
                        wait_item(pe, k)
                        w = slot_view(k, PIECE, DC)
                        for half in range(2):
                            if j >= 2:
                                pe.wait_ge(sem(f"proj_t{half}_{L}"), j - 1)
                            for b in range(2):
                                for c in range(DC):
                                    ins = pe.matmul(ps[:, (2 * j + half) % 4, b * SEQ:(b + 1) * SEQ],
                                                    w[:, c, (2 * half + b) * P:(2 * half + b + 1) * P], xT[:, c, :],
                                                    start=(c == 0), stop=(c == DC - 1))
                            ins.then_inc(sem(f"proj_mm{L}"), 1)
                    pe.wait_ge(sem("logf"), 1)
                    for c in range(NT):
                        ins = pe.matmul(ps[0:FOX_HEADS, 7, 0:SEQ], logf[:, c, :],
                                        const[:, C_TRI + c * SEQ:C_TRI + (c + 1) * SEQ], start=(c == 0), stop=(c == NT - 1))
                    ins.then_inc(sem("dcum"), 1)
                    for j in range(2):
                        k = first_item[L] + 5 + j
                        wait_item(pe, k)
                        w = slot_view(k, PIECE, DC)
                        for t in range(NT):
                            pe.wait_ge(sem(f"proj_t{t}_{L}"), j + 3)
                            for c in range(DC):
                                ins = pe.matmul(ps[:, (2 * j + t) % 4, :], xT[:, c, t * P:(t + 1) * P],
                                                w[:, c, :], start=(c == 0), stop=(c == DC - 1))
                            ins.then_inc(sem(f"proj_mm{L}"), 1)
                    pe.wait_ge(sem(f"proj_t0_{L}"), 6)
                    pe.wait_ge(sem(f"proj_t1_{L}"), 6)
                    pe.wait_ge(sem("aug"), 1)
                attention(L)

                if L % 2 == 0:
                    pe.wait_ge(sem(f"proj_t0_{L}"), 5)
                pe.wait_ge(sem(f"o_ready{L}"), 1)
                transpose_tile(o_tok, 0)
                for t in range(NT):
                    wait_tile("oT", L, t)
                    for n in range(2):
                        if n == 1 and t == 0:
                            pe.wait_ge(sem(f"o_ready{L}"), 2)
                            transpose_tile(o_tok, 1)
                        if n == 1 and t == 1:
                            pe.wait_ge(sem(f"ln1_out{L}"), 1)
                            transpose_tile(x_tok, 0)
                        k = shared_item[L] - 2 + n
                        if t == 0:
                            wait_item(pe, k)
                        w = slot_view(k, PIECE, DC)
                        for c in range(DC):
                            ins = pe.matmul(ps[:, 4 + 2 * t + n, :], xT[:, c, t * P:(t + 1) * P], w[:, c, :],
                                            start=(c == 0), stop=(c == DC - 1))
                        ins.then_inc(sem(f"wo_mm{L}"), 1)

                ks = shared_item[L]

                def up_all(slot):
                    w1, w3, _ = ffn_views(slot)
                    for b, w in enumerate((w1, w3)):
                        for f in range(2):
                            for c in range(DC):
                                ins = pe.matmul(ps[:, 4 + b, f * SEQ:(f + 1) * SEQ], w[:, c, f::2],
                                                xT[:, c, :], start=(c == 0), stop=(c == DC - 1))
                    return ins

                def up_tile(slot, t, between):
                    w1, w3, _ = ffn_views(slot)
                    for b, w in enumerate((w1, w3)):
                        if b == 1 and t == 0:
                            between()
                        for f in range(2):
                            for c in range(DC):
                                ins = pe.matmul(ps[:, 4 + t, (2 * b + f) * P:(2 * b + f + 1) * P], w[:, c, f::2],
                                                xT[:, c, t * P:(t + 1) * P], start=(c == 0), stop=(c == DC - 1))
                    return ins

                def down_all(slot, tiles=range(NT)):
                    _, _, w2 = ffn_views(slot)
                    for t in tiles:
                        for half in range(2):
                            for f in range(2):
                                ins = pe.matmul(ps[:, 2 * t + half, :], h_all[:, f * SEQ + t * P:f * SEQ + (t + 1) * P],
                                                w2[:, f, half * PIECE:(half + 1) * PIECE], start=(f == 0), stop=(f == 1))
                    return ins

                def router(t, L=L):
                    if t == 0:
                        pe.wait_ge(sem("layer_loaded"), 48 * (L + 1))
                        pe.wait_ge(sem("var_ready"), 3 * NT * L + NT)
                    for c in range(DC):
                        ins = pe.matmul(ps[:, 6 + t, 0:NE], xT[:, c, t * P:(t + 1) * P], router_w[:, c, :],
                                        start=(c == 0), stop=(c == DC - 1))
                    ins.then_inc(sem(f"router_mm{L}"), 1)

                def between(L=L):
                    router(0)
                    pe.wait_ge(sem(f"ln1_out{L}"), 2)
                    transpose_tile(x_tok, 1)

                wait_item(pe, ks)
                wait_tile("xT", 3 * L + 1, 0)
                up_tile(ks % RING, 0, between).then_inc(sem("shared_up"), 1)
                wait_tile("xT", 3 * L + 1, 1)
                router(1)
                up_tile(ks % RING, 1, None).then_inc(sem("shared_up"), 1)
                pe.wait_ge(sem("shared_h"), NT * L + 1)
                down_all(ks % RING, [0]).then_inc(sem("shared_down"), 1)
                pe.wait_ge(sem(f"router_dve{L}"), NT)
                for t in range(NT):
                    for c in range(t + 1):
                        ins = pe.matmul(ps[:, 6 + t, 0:NE], const[:, C_TRI + c * SEQ + t * P:C_TRI + c * SEQ + (t + 1) * P],
                                        chosen[:, c, :], start=(c == 0), stop=(c == t))
                ins.then_inc(sem("place_mm"), 1)
                pe.wait_ge(sem("shared_h"), NT * L + 2)
                down_all(ks % RING, [1]).then_inc(sem("shared_down"), 1)

                M0 = L * PAIRS

                def gather(m, par, half):
                    if half == 0:
                        pe.wait_ge(sem("sel_built"), m + (M0 + 1))
                        if M0 or not isinstance(m, int) or m > 0:
                            pe.wait_ge(sem("xe_copied"), m + M0)
                    for c in range(4 * half, 4 * half + 4):
                        for t in range(NT):
                            for part in x_parts:
                                ins = pe.matmul(ps[:, c // 4, (c % 4) * P:(c % 4 + 1) * P], part[:, t, c::DC],
                                                sel_bf[:, par, t, :], start=(t == 0 and part is x_part1),
                                                stop=(t == NT - 1 and part is x_part3))
                    if half == 1:
                        ins.then_inc(sem("gathered"), 1)

                def sel_transpose(m, par, first=False):
                    pe.wait_ge(sem("sel_built"), m + (M0 + 1))
                    if not first:
                        pe.wait_ge(sem("hT_copied"), m + M0)
                    for t in range(NT):
                        pe.transpose(ps[:, 3, t * P:(t + 1) * P], sel[:, par, t, :], ident)
                    for t in range(NT):
                        cols = slice(2 * m, 2 * m + 2) if isinstance(m, int) else bass.ds(2 * m, 2)
                        ins = pe.matmul(ps[:, 3, SEQ:SEQ + 2], sel[:, par, t, :], gates[:, t, cols],
                                        start=(t == 0), stop=(t == NT - 1))
                    ins.then_inc(sem("selT_tp"), 1)

                def exp_up(m, par, first):
                    pe.wait_ge(sem("xe_copied"), m + (M0 + 1))
                    if not first:
                        pe.wait_ge(sem("exp_h"), m + M0)
                    views = [ffn_views((ks + 1 + 2 * par + b) % RING) for b in range(2)]
                    for w in range(2):
                        for c in range(DC):
                            for b in range(2):
                                ins = pe.matmul(ps[b * SLOTS:(b + 1) * SLOTS, 2, w * FE:(w + 1) * FE],
                                                xe[:, par, c, b * SLOTS:(b + 1) * SLOTS], views[b][w][:, c, :],
                                                start=(c == 0), stop=(c == DC - 1))
                    ins.then_inc(sem("exp_up"), 1)

                def h_transpose(m):
                    pe.wait_ge(sem("exp_h"), m + (M0 + 1))
                    pe.wait_ge(sem("selT_copied"), m + (M0 + 1))
                    for f in range(2):
                        ins = pe.transpose(ps[:, 3, f * P:(f + 1) * P], h_exp[:, f::2], ident)
                    ins.then_inc(sem("hT_tp"), 1)

                def exp_down(m, par, first):
                    for b in range(2):
                        k = ks + 1 + 2 * par + b
                        if isinstance(m, int):
                            pe.wait_ge(down_loaded[k % RING], 16 * (m // 2) + down_loaded_at[k])
                        else:
                            pe.wait_ge(down_loaded[k % RING], 8 * (m - par) + down_loaded_at[k])
                    pe.wait_ge(sem("hT_copied"), m + (M0 + 1))
                    if not first:
                        pe.wait_ge(sem("y_split"), m + M0)
                    views = [ffn_views((ks + 1 + 2 * par + b) % RING)[2] for b in range(2)]
                    for half in range(2):
                        for f in range(2):
                            for b in range(2):
                                ins = pe.matmul(ps[b * SLOTS:(b + 1) * SLOTS, 4 + half, :],
                                                hT[:, f, b * SLOTS:(b + 1) * SLOTS],
                                                views[b][:, f, half * PIECE:(half + 1) * PIECE], start=(f == 0), stop=(f == 1))
                    ins.then_inc(sem("exp_down"), 1)

                def scatter(m, t, par, first, bank=6):
                    if t == 0:
                        pe.wait_ge(sem("y_split"), m + (M0 + 1))
                    if bank == 6 and not (first and t == 0):
                        pe.wait_ge(sem("y_added"), 2 * m + (2 * M0 + t))
                    for half in range(2):
                        for part in (y_hi, y_lo):
                            ins = pe.matmul(ps[:, bank + half, :], selT[:, par, t * P:(t + 1) * P],
                                            part[:, half * PIECE:(half + 1) * PIECE],
                                            start=(part is y_hi), stop=(part is y_lo))
                    ins.then_inc(sem("scattered"), 1)

                def pe_step(m, u, gather_next=True, scatter_last=True, first=False):
                    for b in range(2):
                        k = ks + 1 + 2 * u + b
                        if isinstance(m, int):
                            pe.wait_ge(w_loaded[k % RING], 32 * (m // 2) + loaded[k])
                        else:
                            pe.wait_ge(w_loaded[k % RING], 16 * (m - u) + loaded[k])
                    exp_up(m, u, first and M0 == 0)
                    if gather_next:
                        gather(m + 1, 1 - u, 0)
                    h_transpose(m)
                    if scatter_last:
                        scatter(m - 1, 0, 1 - u, M0 == 0 and isinstance(m, int) and m == 1)
                    if gather_next:
                        gather(m + 1, 1 - u, 1)
                    exp_down(m, u, first and M0 == 0)
                    if gather_next:
                        sel_transpose(m + 1, 1 - u)
                    if scatter_last:
                        scatter(m - 1, 1, 1 - u, False)

                pe.wait_ge(sem("shared_added"), NT * L + 1)
                pe.wait_ge(sem("x_split"), NT * (L + 1))
                gather(0, 0, 0)
                gather(0, 0, 1)
                pe.wait_ge(sem("shared_added"), NT * L + 2)
                sel_transpose(0, 0, first=True)
                pe_step(0, 0, scatter_last=False, first=True)
                pe_step(1, 1)
                with pe.Fori(1, PAIRS // 2 - 1) as i:
                    for u in range(2):
                        pe_step(2 * i + u, u)
                pe_step(PAIRS - 2, 0)
                pe_step(PAIRS - 1, 1, gather_next=False)
                pe.wait_ge(sem("over_flag"), L + 1)
                flag = pe.value_load(over_int[0:1, 0:1], min_val=0, max_val=1)
                for t in range(NT):
                    for c in range(2):
                        ins = pe.transpose(ps[:, 0, c * SEQ + t * P:c * SEQ + (t + 1) * P], p_tok[:, t, c::2], ident)
                    ins.then_inc(sem(f"pT_tp{L}"), 1)
                scatter(PAIRS - 1, 0, 1, False)
                scatter(PAIRS - 1, 1, 1, False, bank=2)

                with pe.If(flag > 0):
                    pe.wait_ge(sem("y_added"), 2 * (M0 + PAIRS))
                    pe.wait_ge(sem(f"pT_done{L}"), 1)
                    with pe.Fori(0, NE) as e:
                        pe.wait_ge(sem(f"over_loaded{L}"), 48 * e + 48)
                        up_all(0).then_inc(sem(f"over_up{L}"), 1)
                        pe.wait_ge(sem(f"over_h{L}"), e + 1)
                        down_all(0).then_inc(sem(f"over_down{L}"), 1)
                    pe.wait_ge(sem(f"over_added{L}"), NE)

                kp = ks + 1 + NE
                pe.wait_ge(sem(f"pT_done{L}"), 1)
                wait_item(pe, kp)
                w = slot_view(kp, D, 2)
                for t in range(NT):
                    if t == 1:
                        pe.wait_ge(sem("y_added"), 2 * (M0 + PAIRS) - 1)
                    for half in range(2):
                        for c in range(2):
                            ins = pe.matmul(ps[:, 4 + 2 * t + half, :], ple_pT[:, c, t * P:(t + 1) * P],
                                            w[:, c, half * PIECE:(half + 1) * PIECE], start=(c == 0), stop=(c == 1))
                    ins.then_inc(sem(f"ple_mm{L}"), 1)
                pe.wait_ge(sem(f"ln2_out{L}"), 1)
                transpose_tile(x_tok, 0)
                for t in range(NT):
                    wait_tile("xT", 3 * L + 2, t)
                    for n in range(2):
                        if n == 1 and t == 0:
                            pe.wait_ge(sem(f"ln2_out{L}"), 2)
                            transpose_tile(x_tok, 1)
                        if t == 0:
                            wait_item(pe, kp + 1 + n)
                        w = slot_view(kp + 1 + n, PIECE, DC)
                        for c in range(DC):
                            ins = pe.matmul(ps[:, 2 * t + n, :], xT[:, c, t * P:(t + 1) * P], w[:, c, :],
                                            start=(c == 0), stop=(c == DC - 1))
                        ins.then_inc(sem(f"ple_mm{L}"), 1)

        @block.scalar
        def _(act):
            def copy_T(name, count, t):
                banks = 2 if t == 0 else 1
                act.wait_ge(sem("xT_tp"), count + t + 1)
                act.activation(xT[:, 0:4 * banks, t * P:(t + 1) * P],
                               ps[:, 2 * t:2 * t + banks, :].rearrange("p b (c n) -> p (b c) n", c=4),
                               ACT.Copy).then_inc(sem(name), 1)

            def attention(L):
                units = UNITS[L % 2]
                for u in range(len(units) + 2):
                    if u < len(units):
                        what, t, g = units[u]
                        K = n_keys(t)
                        act.wait_ge(sem(f"sc_max{L}"), u + 1)
                        for s, h in enumerate(unit_slots(g)):
                            ins = act.activation(scores[:, u % 4, s * K:(s + 1) * K], scores[:, u % 4, s * K:(s + 1) * K],
                                                 ACT.Exp, bias=neg_max[:, u % 2, s:s + 1],
                                                 accum_out=denom[:, (u // 2) % 4, 4 * (u % 2) + s:4 * (u % 2) + s + 1])
                        ins.then_inc(sem(f"sc_exp{L}"), 1)
                        if L == 0 and u == 1:
                            act.wait_ge(sem("cmp_pT"), 1)
                            act.activation(small_pT, ps[:, 6, 0:SEQ], ACT.Copy).then_inc(sem("cmp_pT_copied"), 1)
                    if u >= 2:
                        v = u - 2
                        t = units[v][1]
                        act.wait_ge(sem(f"pT_tp{L}u"), v + 1)
                        if v >= 2:
                            act.wait_ge(sem(f"pv_mm{L}"), v - 1)
                        n = 4 * (t + 1) * P
                        act.activation(pT[:, v % 2, 0:n], ps[:, 4:6, :].rearrange("p b n -> p (b n)")[:, 0:n],
                                       ACT.Copy).then_inc(sem(f"pT_copied{L}"), 1)

            rs_count = [0]

            def rsqrt_guess():
                rs_count[0] += 1
                act.wait_ge(sem("var_ready"), rs_count[0])
                act.activation(rstd, var_eps, ACT.Sqrt).then_inc(sem("rstd_guess"), 1)

            tp = 0
            for L in range(DEPTH):
                for t in range(NT):
                    copy_T("xT_act", tp, t)
                tp += NT
                if L % 2 == 0:
                    def copy_piece(j):
                        c0, c1 = proj_pieces[0][j]
                        for t in range(NT):
                            act.wait_ge(sem(f"proj_mm{L}"), 2 * j + t + 1)
                            act.activation(proj[:, t, c0:c1], ps[:, 4 + (2 * j + t) % 4, 0:c1 - c0], ACT.Copy)\
                               .then_inc(sem(f"proj_t{t}_{L}"), 1)

                    def duplicate(name, need, src):
                        act.wait_ge(sem(name), need)
                        act.activation(roped[:, :, (src + 1) * HD:(src + 2) * HD], roped[:, :, src * HD:(src + 1) * HD],
                                       ACT.Copy).then_inc(sem("dup"), 1)

                    def copy_pairs(m):
                        blocks, bank = QKT_BATCHES[m]
                        n = len(blocks)
                        act.wait_ge(sem("qkT_tp"), m + 1)
                        act.activation(qkT[:, blocks[0]:blocks[0] + n, :],
                                       ps[:, bank:bank + 2, :].rearrange("p b (c n) -> p (b c) n", c=2)[:, 0:n, :],
                                       ACT.Copy).then_inc(sem("qkT_copied"), 1)

                    for j in range(3):
                        copy_piece(j)
                    duplicate("roped_dsa", 1, 18)
                    copy_pairs(0)
                    copy_pairs(1)
                    copy_piece(3)
                    for n in range(NT * HEADS):
                        t = n // HEADS
                        act.wait_ge(sem("idx_mm"), n + 1)
                        if n >= 8:
                            act.wait_ge(sem("idx_acc"), n - 7)
                        act.activation(relu_buf[:, n % 8, 0:n_keys(t)], ps[:, n % 4, 0:n_keys(t)], ACT.Relu)\
                           .then_inc(sem("idx_relu"), 1)
                    act.wait_ge(sem("cmp_h"), 1)
                    act.activation(small[0:HD, 160:160 + N_CMP], ps[0:HD, 6, 0:N_CMP], ACT.Exp, scale=-1.0)
                    act.activation(small[0:HD, 176:176 + N_CMP], ps[0:HD, 7, 0:N_CMP], ACT.Exp, scale=-1.0)\
                       .then_inc(sem("cmp_exp"), 1)
                    copy_piece(4)
                    duplicate("roped_dsa", 3, 8)
                    copy_pairs(2)
                    copy_pairs(3)
                    duplicate("roped_nsa", 2, 28)
                    duplicate("roped_nsa", 3, 30)
                    copy_pairs(4)
                    copy_pairs(5)
                    act.wait_ge(sem("gate_z"), 1)
                    act.activation(gate_sig, gate_sig, ACT.Exp, scale=-1.0).then_inc(sem("gate_e"), 1)
                    act.wait_ge(sem("cmp_sub"), 1)
                    act.activation(cmp_s, cmp_s, ACT.Exp).then_inc(sem("cmp_e"), 1)
                else:
                    act.wait_ge(sem("fox_z"), 1)
                    act.activation(fox_t, fox_zb, ACT.Abs).then_inc(sem("fox_abs"), 1)
                    act.wait_ge(sem("fox_abs"), 1)
                    act.activation(fox_t, fox_t, ACT.Exp, scale=-1.0).then_inc(sem("fox_e"), 1)
                    act.wait_ge(sem("fox_e"), 1)
                    act.activation(fox_t, fox_t, ACT.Ln, bias=1.0).then_inc(sem("fox_ln"), 1)
                    for j in range(4):
                        act.wait_ge(sem(f"proj_mm{L}"), NT + 2 * j + 1)
                        act.activation(qkT[:, 4 * j:4 * j + 2, :], ps[:, 2 * j % 4, :], ACT.Copy)\
                           .then_inc(sem(f"proj_t0_{L}"), 1)
                    for j in range(2):
                        act.wait_ge(sem(f"proj_mm{L}"), NT + 8 + 2 * j + 1)
                        act.activation(v_fox[:, 0, j * PIECE:(j + 1) * PIECE], ps[:, 2 * j, :], ACT.Copy)\
                           .then_inc(sem(f"proj_t0_{L}"), 1)
                attention(L)
                def shared_silu(t):
                    act.wait_ge(sem("shared_up"), NT * L + t + 1)
                    act.activation(by_f(h_silu_all, t), ps[:, 4 + t, 0:SEQ].rearrange("p (f n) -> p f n", f=2), ACT.Silu)\
                       .then_inc(sem("shared_silu"), 1)

                for t in range(NT):
                    copy_T("oT_act", tp, t)
                tp += NT
                rsqrt_guess()
                copy_T("xT_act", tp, 0)
                rsqrt_guess()
                for t in range(NT):
                    if t == NT - 1:
                        copy_T("xT_act", tp, t)
                    act.wait_ge(sem(f"router_mm{L}"), t + 1)
                    act.activation(sig[:, t, :], ps[:, 6 + t, 0:NE], ACT.Exp, scale=-1.0).then_inc(sem("router_e"), 1)
                    if t == 0:
                        shared_silu(0)
                shared_silu(1)
                tp += NT

                for t in range(NT):
                    act.wait_ge(sem("shared_down"), NT * L + t + 1)
                    act.activation(y_acc[:, t, :], ps[:, 2 * t:2 * t + 2, :], ACT.Copy).then_inc(sem("shared_added"), 1)

                M0 = L * PAIRS

                def later(m, n):
                    return M0 > 0 or not isinstance(m, int) or m >= n

                def xe_copy(m, par):
                    act.wait_ge(sem("gathered"), m + (M0 + 1))
                    if later(m, 2):
                        act.wait_ge(sem("exp_up"), m + (M0 - 1))
                    act.activation(xe[:, par, :, :], ps[:, 0:2, :].rearrange("p b (c n) -> p (b c) n", c=4), ACT.Copy)\
                       .then_inc(sem("xe_copied"), 1)

                def silu(m):
                    act.wait_ge(sem("exp_up"), m + (M0 + 1))
                    if later(m, 1):
                        act.wait_ge(sem("exp_h"), m + M0)
                    act.activation(h_silu, ps[:, 2, 0:FE], ACT.Silu).then_inc(sem("exp_silu"), 1)

                def hT_copy(m):
                    act.wait_ge(sem("hT_tp"), m + (M0 + 1))
                    if later(m, 1):
                        act.wait_ge(sem("exp_down"), m + M0)
                    act.activation(hT, ps[:, 3, 0:2 * P].rearrange("p (f n) -> p f n", f=2), ACT.Copy).then_inc(sem("hT_copied"), 1)

                def selT_copy(m, par):
                    act.wait_ge(sem("selT_tp"), m + (M0 + 1))
                    if later(m, 2):
                        act.wait_ge(sem("scattered"), 2 * m + (2 * M0 - 2))
                    if later(m, 2):
                        act.wait_ge(sem("exp_h"), m + (M0 - 1))
                    act.activation(selT[:, par, :], ps[:, 3, 0:SEQ], ACT.Copy)
                    for b in range(2):
                        ins = act.activation(slot_gate[b * SLOTS:(b + 1) * SLOTS, par:par + 1],
                                             ps[b * SLOTS:(b + 1) * SLOTS, 3, SEQ + b:SEQ + b + 1], ACT.Copy)
                    ins.then_inc(sem("selT_copied"), 1)

                def y_high(m):
                    act.wait_ge(sem("exp_down"), m + (M0 + 1))
                    if later(m, 1):
                        act.wait_ge(sem("scattered"), 2 * m + 2 * M0)
                    act.activation(y_hi[:, :], ps[:, 4:6, :], ACT.Copy).then_inc(sem("y_high"), 1)

                def act_step(m, u, more=True):
                    silu(m)
                    hT_copy(m)
                    if more:
                        xe_copy(m + 1, 1 - u)
                    y_high(m)
                    if more:
                        selT_copy(m + 1, 1 - u)

                xe_copy(0, 0)
                selT_copy(0, 0)
                act_step(0, 0)
                act_step(1, 1)
                with act.Fori(1, PAIRS // 2 - 1) as i:
                    for u in range(2):
                        act_step(2 * i + u, u)
                act_step(PAIRS - 2, 0)
                act.wait_ge(sem("over_flag"), L + 1)
                flag = act.value_load(over_int[0:1, 0:1], min_val=0, max_val=1)
                act_step(PAIRS - 1, 1, more=False)
                act.wait_ge(sem(f"pT_tp{L}"), NT)
                act.activation(ple_pT, ps[:, 0, :], ACT.Copy).then_inc(sem(f"pT_done{L}"), 1)

                with act.If(flag > 0):
                    with act.Fori(0, NE) as e:
                        act.wait_ge(sem(f"over_up{L}"), e + 1)
                        act.activation(h_silu_all, ps[:, 4, :], ACT.Silu).then_inc(sem(f"over_silu{L}"), 1)

                rsqrt_guess()
                copy_T("xT_act", tp, 0)
                rsqrt_guess()
                for t in range(NT):
                    act.wait_ge(sem(f"ple_mm{L}"), t + 1)
                    act.activation(roped[:, t, 0:D], ps[:, 4 + 2 * t:6 + 2 * t, :], ACT.Square,
                                   accum_out=ple_ss[:, t:t + 1]).then_inc(sem(f"ple_sq{L}"), 1)
                copy_T("xT_act", tp, 1)
                tp += NT
                rsqrt_guess()
                rsqrt_guess()
                for t in range(NT):
                    act.wait_ge(sem(f"ple_mm{L}"), NT + 2 * t + 2)
                    act.wait_ge(sem(f"ple_sq{L}"), NT)
                    act.activation(roped[:, t, 0:D], ps[:, 2 * t:2 * t + 2, :], ACT.Sigmoid)\
                       .then_inc(sem(f"ple_sig{L}"), 1)

        @block.vector
        def _(dve):
            step = [0]
            rs_count = [0]
            chain = sem("dve_step")

            def seq(ins):
                step[0] += 1
                ins.then_inc(chain, 1)
                dve.wait_ge(chain, step[0])

            def copy_T(name, count):
                for t in range(1, NT):
                    dve.wait_ge(sem("xT_tp"), count + t + 1)
                    dve.tensor_copy(xT[:, 4:8, t * P:(t + 1) * P],
                                    ps[:, 2 * t + 1, :].rearrange("p (c n) -> p c n", c=4))\
                       .then_inc(sem(name), 1)

            def topk_round(n):
                t = n // 8
                K = n_keys(t)
                s = selbias[:, t, 0:K]
                causal = const[:, C_CAUSAL + SEQ - K:C_CAUSAL + SEQ]
                if n % 8 == 0:
                    seq(dve.scalar_tensor_tensor(s, s, IDX_SCALE, causal, ALU.mult, ALU.add))
                seq(dve.max(best8, s))
                seq(dve.match_replace(s, best8, s, TAKEN))
                if n % 8 == 7:
                    seq(dve.tensor_scalar(s, s, TAKEN, 1.0, ALU.is_equal, ALU.subtract))
                    seq(dve.scalar_tensor_tensor(s, s, -NEG, causal, ALU.mult, ALU.add))

            def cmp_probs():
                dve.wait_ge(sem("cmp_e"), 1)
                seq(dve.tensor_reduce(cmp_m, cmp_all, AX_X, ALU.add))
                for t in range(NT):
                    sc = cmp_s[:, t, :].rearrange("p (s c) -> p s c", s=8)
                    dve.tensor_tensor(sc, sc, const[:, C_CVALID + t * CMP_PAD:C_CVALID + (t + 1) * CMP_PAD]
                                      .unsqueeze(1).to_broadcast([P, 8, CMP_PAD]), ALU.mult).then_inc(sem("cmp_p"), 1)
                dve.wait_ge(sem("gate_e"), 1)
                seq(dve.tensor_scalar(gate_sig, gate_sig, 1.0, None, ALU.add))
                seq(dve.reciprocal(gate_sig, gate_sig))
                seq(dve.reciprocal(cmp_m, cmp_m))

            def cmp_outputs():
                for t in range(NT):
                    gate = gate_sig.rearrange("p (t h b) -> p t h b", t=NT, b=3)[:, t, :, 0]
                    seq(dve.tensor_tensor(coef_h, cmp_m[:, 8 * t:8 * t + 8], gate, ALU.mult))
                    dve.wait_ge(sem("cmp_o"), 1)
                    dve.tensor_tensor(o_tok[:, t, 512:1024].rearrange("p (h d) -> p h d", h=8),
                                      ps[:, 6 + t, :].rearrange("p (h d) -> p h d", h=8),
                                      coef_h.unsqueeze(2).to_broadcast([P, 8, HD]), ALU.mult).then_inc(sem("cmp_out"), 1)
                    dve.wait_ge(sem("cmp_out"), t + 1)

            def attention(L):
                units = UNITS[L % 2]
                for u in range(len(units) + 4):
                    if L == 0 and u == 1:
                        cmp_probs()
                    if u < len(units):
                        what, t, g = units[u]
                        K = n_keys(t)
                        dve.wait_ge(sem(f"sc_mm{L}"), u + 1)
                        if u >= 4:
                            dve.wait_ge(sem(f"pT_tp{L}u"), u - 3)
                        bias = selbias[:, t, 0:K] if what == "dsa" else const[:, C_CAUSAL + SEQ - K:C_CAUSAL + SEQ]
                        s_out = scores[:, u % 4, 0:4 * K].rearrange("p (s k) -> p s k", s=4)
                        for b in range(2):
                            ins = dve.scalar_tensor_tensor(
                                s_out[:, 2 * b:2 * b + 2, :], ps[:, 2 * (u % 2) + b, 0:2 * K].rearrange("p (s k) -> p s k", s=2),
                                SCALE, bias.unsqueeze(1).to_broadcast([P, 2, K]), ALU.mult, ALU.add)
                        ins.then_inc(sem(f"sc_biased{L}"), 1)
                        dve.wait_ge(sem(f"sc_biased{L}"), u + 1)
                        if u >= 2:
                            dve.wait_ge(sem(f"sc_exp{L}"), u - 1)
                        dve.tensor_reduce(neg_max[:, u % 2, 0:4], s_out, AX_X, ALU.max, negate=True)\
                           .then_inc(sem(f"sc_max{L}"), 1)
                    if L == 0 and u == 2:
                        cmp_outputs()
                    if L == 0 and 10 + EARLY_ROUNDS + u < 16:
                        topk_round(10 + EARLY_ROUNDS + u)
                    if u >= 5 and u % 2 == 1:
                        v = u - 4
                        what, t, g = units[v]
                        grp = v // 2
                        dve.wait_ge(sem(f"pv_mm{L}"), v + 1)
                        seq(dve.reciprocal(coef, denom[:, grp % 4, :]))
                        by_head = coef.rearrange("p (g b j) -> p g j b", g=2, b=2)
                        if what in ("sel", "win"):
                            br = 1 if what == "sel" else 2
                            gate = gate_sig.rearrange("p (t h b) -> p t h b", t=NT, b=3)[:, t, :, br]
                            seq(dve.tensor_tensor(coef_h.rearrange("p (g j b) -> p g j b", g=2, b=2), by_head,
                                                  gate.rearrange("p (g j b) -> p g j b", g=2, b=2), ALU.mult))
                        else:
                            seq(dve.tensor_copy(coef_h.rearrange("p (g j b) -> p g j b", g=2, b=2), by_head))
                        o_ps = ps[:, 6 + grp % 2, :].rearrange("p (h d) -> p h d", h=8)
                        cb = coef_h.unsqueeze(2).to_broadcast([P, 8, HD])
                        if what in ("sel", "win"):
                            o = o_tok[:, t, 512:1024]
                            seq_ins = dve.tensor_tensor(tmp_o.rearrange("p (h d) -> p h d", h=8), o_ps, cb, ALU.mult)
                            seq_ins.then_inc(sem(f"pv_out{L}"), 1)
                            dve.wait_ge(sem(f"pv_out{L}"), grp + 1)
                            seq(dve.tensor_tensor(o, o, tmp_o, ALU.add))
                        else:
                            c0 = 0 if what == "dsa" else 512 * (g // 2)
                            dve.tensor_tensor(o_tok[:, t, c0:c0 + 512].rearrange("p (h d) -> p h d", h=8), o_ps, cb, ALU.mult)\
                               .then_inc(sem(f"pv_out{L}"), 1)
                            last = (what == "dsa") or g >= 2
                            if last:
                                dve.wait_ge(sem(f"pv_out{L}"), grp + 1)
                                dve.engine_nop().then_inc(sem(f"o_ready{L}"), 1)

            def rsqrt(v, scale, eps):
                rs_count[0] += 1
                dve.tensor_scalar(var_eps, v, scale, eps, ALU.mult, ALU.add).then_inc(sem("var_ready"), 1)
                dve.wait_ge(sem("rstd_guess"), rs_count[0])
                seq(dve.reciprocal(rstd, rstd))
                seq(dve.tensor_scalar(newton, rstd, rstd, var_eps, ALU.mult, ALU.mult))
                seq(dve.tensor_scalar(newton, newton, -0.5, 1.5, ALU.mult, ALU.add))
                seq(dve.tensor_tensor(rstd, rstd, newton, ALU.mult))

            def layer_norm(L, which, other):
                j = 3 * L + which - 1
                for t in range(NT):
                    for half in range(2):
                        xs = x_tok[:, t, half * PIECE:(half + 1) * PIECE]
                        if which == 1:
                            dve.wait_ge(sem(f"wo_mm{L}"), 2 * t + half + 1)
                        seq(dve.scalar_tensor_tensor(xs, xs, ALPHA, other(t, half), ALU.mult, ALU.add))
                        seq(dve.bn_stats(stats[:, t, half, :], xs))
                    seq(dve.bn_aggr(mean_var, stats[:, t, :, :]))
                    rsqrt(mean_var[:, 1:2], 1.0, LN_EPS)
                    dve.wait_ge(sem("gb_loaded"), 32 * (j + 1))
                    seq(dve.scalar_tensor_tensor(x_tok[:, t, :], x_tok[:, t, :], mean_var[:, 0:1], gb_row[:, 0, :], ALU.subtract, ALU.mult))
                    seq(dve.scalar_tensor_tensor(x_tok[:, t, :], x_tok[:, t, :], rstd, gb_row[:, 1, :], ALU.mult, ALU.add))
                    dve.engine_nop().then_inc(sem(f"ln{which}_out{L}"), 1)
                    dve.engine_nop().then_inc(sem("gb_used"), 1)

            tp = 0
            for L in range(DEPTH):
                copy_T("xT_dve", tp)
                tp += NT
                if L == 0:
                    dve.wait_ge(sem("const_loaded"), 16)
                if L % 2 == 0:
                    for n, (src, heads, dst) in enumerate(((QI, 9, 10), (QA, 8, 0), (KA, 1, 8))):
                        for t in range(NT):
                            dve.wait_ge(sem(f"proj_t{t}_{L}"), (2, 3, 3)[n])
                            ins = rope(dve, seq, *rope_views(t, src, heads, dst), tmp_o)
                            if t < NT - 1:
                                seq(ins)
                        ins.then_inc(sem("roped_dsa"), 1)
                        dve.wait_ge(sem("roped_dsa"), n + 1)
                    dve.wait_ge(sem("cmp_tp"), 1)
                    seq(dve.tensor_copy(kvT, ps[:, 6, 0:SEQ]))
                    seq(dve.tensor_copy(peT, ps[:, 7, 0:CMP_LEN]))
                    strides = kvT.rearrange("p (g r) -> p r g", r=CMP_STRIDE)
                    for half in range(2):
                        rows_l = slice(half * CMP_STRIDE, (half + 1) * CMP_STRIDE)
                        ins = dve.tensor_tensor(cmp_blk[:, rows_l, :], strides[:, :, half:half + N_CMP],
                                                peT[:, rows_l].unsqueeze(2).to_broadcast([P, CMP_STRIDE, N_CMP]), ALU.add)
                    ins.then_inc(sem("cmp_blk"), 1)
                    for n in range(NT * HEADS):
                        t, h = n // HEADS, n % HEADS
                        K = n_keys(t)
                        dve.wait_ge(sem("idx_relu"), n + 1)
                        w = proj[:, t, WI + h:WI + h + 1]
                        if h == 0:
                            ins = dve.tensor_scalar(selbias[:, t, 0:K], relu_buf[:, n % 8, 0:K], w, None, ALU.mult)
                        else:
                            ins = dve.scalar_tensor_tensor(selbias[:, t, 0:K], relu_buf[:, n % 8, 0:K], w,
                                                           selbias[:, t, 0:K], ALU.mult, ALU.add)
                        ins.then_inc(sem("idx_acc"), 1)
                        dve.wait_ge(sem("idx_acc"), n + 1)
                    for n in range(8):
                        topk_round(n)
                    dve.wait_ge(sem("cmp_exp"), 1)
                    seq(dve.tensor_scalar(small[0:HD, 160:192], small[0:HD, 160:192], 1.0, None, ALU.add))
                    seq(dve.reciprocal(small[0:HD, 160:192], small[0:HD, 160:192]))
                    dve.tensor_tensor(small[0:HD, 128:128 + N_CMP], ps[0:HD, 6, 0:N_CMP], small[0:HD, 160:160 + N_CMP], ALU.mult)
                    dve.tensor_tensor(small[0:HD, 144:144 + N_CMP], ps[0:HD, 7, 0:N_CMP], small[0:HD, 176:176 + N_CMP], ALU.mult)\
                       .then_inc(sem("cmp_hs"), 1)
                    topk_round(8)
                    topk_round(9)
                    dve.wait_ge(sem("cmp_kv"), 1)
                    seq(dve.tensor_copy(small[0:N_CMP, 384:448], ps[0:N_CMP, 6, HD:P]))
                    seq(rope(dve, seq, ps[0:N_CMP, 6, 0:HD].rearrange("p (n h k) -> p n h k", n=1, h=2),
                             small[0:N_CMP, 256:320].rearrange("p (n h k) -> p n h k", n=1, h=2),
                             const[0:N_CMP, C_CCOS:C_CCOS + 32], const[0:N_CMP, C_CSIN:C_CSIN + 32],
                             small[:, 192:224], rows_=N_CMP))
                    dve.tensor_copy(small[0:N_CMP, 320:384], small[0:N_CMP, 256:320]).then_inc(sem("cmp_roped"), 1)
                    dve.wait_ge(sem("cmp_rep"), 1)
                    dve.tensor_copy(small[0:HD, 448:448 + CMP_PAD], ps[0:HD, 7, 0:CMP_PAD])
                    dve.tensor_copy(small[HD:P, 448 + CMP_PAD:448 + 2 * CMP_PAD], ps[HD:P, 7, 0:CMP_PAD])\
                       .then_inc(sem("cmp_kT"), 1)
                    ins = dve.tensor_tensor(v_bd.rearrange("p (h d) -> p h d", h=8),
                                            ps[:, 6, 0:HD].unsqueeze(1).to_broadcast([P, 8, HD]),
                                            const[:, C_BD:C_BD + HEADS].unsqueeze(2).to_broadcast([P, 8, HD]), ALU.mult)
                    ins.then_inc(sem("v_bd"), 1)
                    dve.wait_ge(sem("bias_loaded"), 32)
                    for t in range(NT):
                        dve.wait_ge(sem(f"proj_t{t}_{L}"), 5)
                    dve.tensor_tensor(gate_sig.rearrange("p (t n) -> p t n", t=NT), proj[:, :, GB:GB + 24],
                                      bgate[:, :].unsqueeze(1).to_broadcast([P, NT, 24]), ALU.add).then_inc(sem("gate_z"), 1)
                    for n in range(10, 10 + EARLY_ROUNDS):
                        topk_round(n)
                    dve.wait_ge(sem("cmp_sc"), 1)
                    for t in range(NT):
                        ins = dve.scalar_tensor_tensor(
                            cmp_s[:, t, :].rearrange("p (s c) -> p s c", s=8),
                            ps[:, 7, t * P:(t + 1) * P].rearrange("p (s c) -> p s c", s=8), SCALE,
                            const[:, C_CBIAS + t * CMP_PAD:C_CBIAS + (t + 1) * CMP_PAD].unsqueeze(1).to_broadcast([P, 8, CMP_PAD]),
                            ALU.mult, ALU.add)
                    seq(ins)
                    seq(dve.tensor_reduce(cmp_m, cmp_all, AX_X, ALU.max, negate=True))
                    dve.tensor_tensor(cmp_all, cmp_all, cmp_m.unsqueeze(2).to_broadcast([P, 16, CMP_PAD]), ALU.add)\
                       .then_inc(sem("cmp_sub"), 1)
                else:
                    for t in range(NT):
                        dve.wait_ge(sem(f"proj_mm{L}"), t + 1)
                    z = fox_zb
                    dve.tensor_tensor(z.rearrange("p (t n) -> p t n", t=NT), ps[:, 6, 0:NT * FOX_HEADS].rearrange("p (t n) -> p t n", t=NT),
                                          fox_b[:, :].unsqueeze(1).to_broadcast([P, NT, FOX_HEADS]), ALU.add)\
                       .then_inc(sem("fox_z"), 1)
                    dve.wait_ge(sem("fox_abs"), 1)
                    seq(dve.tensor_scalar(z, z, 0.0, None, ALU.min))
                    dve.wait_ge(sem("fox_ln"), 1)
                    dve.tensor_tensor(logf.rearrange("p t n -> p (t n)"), z, fox_t, ALU.subtract).then_inc(sem("logf"), 1)
                    for j in range(4):
                        dve.wait_ge(sem(f"proj_mm{L}"), NT + 2 * j + 2)
                        dve.tensor_copy(qkT[:, 4 * j + 2:4 * j + 4, :], ps[:, (2 * j + 1) % 4, :].rearrange("p (b n) -> p b n", b=2))\
                           .then_inc(sem(f"proj_t1_{L}"), 1)
                    dve.memset(aug_d, 1.0)
                    seq(dve.memset(aug_k, 1.0))
                    dve.wait_ge(sem("dcum"), 1)
                    for r0, dst in ((0, aug_d), (64, aug_d), (32, aug_k), (96, aug_k)):
                        ins = dve.tensor_scalar(dst[r0:r0 + FOX_HEADS], ps[0:FOX_HEADS, 7, 0:SEQ], 1.0 / SCALE, None, ALU.mult)
                    seq(ins)
                    dve.tensor_tensor(aug_q, aug_d.unsqueeze(1).to_broadcast([P, 8, SEQ]),
                                      const[:, C_DELTA:C_DELTA + 8].unsqueeze(2).to_broadcast([P, 8, SEQ]), ALU.mult)\
                       .then_inc(sem("aug"), 1)
                    for j in range(2):
                        dve.wait_ge(sem(f"proj_mm{L}"), NT + 8 + 2 * j + 2)
                        dve.tensor_copy(v_fox[:, 1, j * PIECE:(j + 1) * PIECE], ps[:, 2 * j + 1, :])\
                           .then_inc(sem(f"proj_t1_{L}"), 1)
                attention(L)
                copy_T("oT_dve", tp)
                tp += NT
                layer_norm(L, 1, lambda t, half: ps[:, 4 + 2 * t + half, :])
                copy_T("xT_dve", tp)
                tp += NT

                dve.wait_ge(sem("layer_loaded"), 48 * (L + 1))
                for t in range(NT):
                    s = sig[:, t, :]
                    dve.wait_ge(sem("router_e"), NT * L + t + 1)
                    seq(dve.tensor_scalar(s, s, 1.0, None, ALU.add))
                    seq(dve.reciprocal(s, s))
                    seq(dve.tensor_tensor(sb_, s, router_b[:, :], ALU.add))
                    for g in range(N_GROUPS):
                        ins = dve.max(gmax[:, g, :], sb_[:, g * 8:(g + 1) * 8])
                    seq(ins)
                    seq(dve.tensor_tensor(gscore, gmax[:, :, 0], gmax[:, :, 1], ALU.add))
                    seq(dve.max(best8, gscore))
                    seq(dve.memset(best8[:, TOP_GROUPS:8], -TAKEN))
                    seq(dve.match_replace(gscore, best8, gscore, TAKEN))
                    seq(dve.tensor_scalar(gscore, gscore, TAKEN, 1.0, ALU.is_equal, ALU.subtract))
                    gm = gscore.unsqueeze(2).to_broadcast([P, 8, 8])
                    seq(dve.tensor_scalar(gmask0, gscore, 1.0, None, ALU.add))
                    g0 = gmask0.unsqueeze(2).to_broadcast([P, 8, 8])
                    sb3 = sb_.rearrange("p (g e) -> p g e", g=8)
                    seq(dve.tensor_tensor(sb3, sb3, g0, ALU.mult))
                    seq(dve.scalar_tensor_tensor(sb3, gm, -NEG, sb3, ALU.mult, ALU.add))
                    seq(dve.max(best8, sb_))
                    seq(dve.match_replace(sb_, best8, sb_, TAKEN))
                    seq(dve.tensor_scalar(sb_, sb_, TAKEN, None, ALU.is_equal))
                    g1 = gates[:, t, :]
                    seq(dve.tensor_copy(chosen[:, t, :], sb_))
                    seq(dve.tensor_tensor(g1, s, sb_, ALU.mult))
                    seq(dve.tensor_reduce(rstd, g1, AX_X, ALU.add))
                    seq(dve.reciprocal(rstd, rstd))
                    dve.tensor_scalar(g1, g1, rstd, ROUTED_SCALE, ALU.mult, ALU.mult).then_inc(sem(f"router_dve{L}"), 1)
                    dve.wait_ge(sem(f"router_dve{L}"), t + 1)
                    dve.wait_ge(sem("shared_silu"), NT * L + t + 1)
                    dve.tensor_tensor(by_f(h_all, t), by_f(h_silu_all, t), ps[:, 4 + t, SEQ:2 * SEQ].rearrange("p (f n) -> p f n", f=2),
                                      ALU.mult).then_inc(sem("shared_h"), 1)

                dve.wait_ge(sem("place_mm"), L + 1)
                for t in range(NT):
                    ins = dve.tensor_tensor(place[:, t, :], ps[:, 6 + t, 0:NE], chosen[:, t, :], ALU.mult)
                seq(ins)
                seq(dve.tensor_scalar(place, place, 1.0, None, ALU.subtract))
                dve.tensor_reduce(over_row, place, mybir.AxisListType.XY, ALU.max).then_inc(sem("place_max"), 1)
                seq(dve.scalar_tensor_tensor(gates_over, place, float(SLOTS), gates[:, :, :], ALU.is_ge, ALU.mult))
                M0 = L * PAIRS

                def later(m, n):
                    return M0 > 0 or not isinstance(m, int) or m >= n

                def sel_build(m, par):
                    if later(m, 2):
                        dve.wait_ge(sem("gathered"), m + (M0 - 1))
                        dve.wait_ge(sem("selT_tp"), m + (M0 - 1))
                    cols = slice(2 * m, 2 * m + 2) if isinstance(m, int) else bass.ds(2 * m, 2)
                    for dst, t in ((d, t) for d in (sel, sel_bf) for t in range(NT)):
                        ins = dve.tensor_tensor(dst[:, par, t, :].rearrange("p (e s) -> p e s", e=2),
                                                place[:, t, cols].unsqueeze(2).to_broadcast([P, 2, SLOTS]),
                                                const[:, C_IOTA:C_IOTA + SLOTS].unsqueeze(1).to_broadcast([P, 2, SLOTS]),
                                                ALU.is_equal)
                    ins.then_inc(sem("sel_built"), 1)

                def gate_h(m, par):
                    dve.wait_ge(sem("exp_silu"), m + (M0 + 1))
                    dve.wait_ge(sem("selT_copied"), m + (M0 + 1))
                    if later(m, 1):
                        dve.wait_ge(sem("hT_tp"), m + M0)
                    dve.scalar_tensor_tensor(h_exp, h_silu, slot_gate[:, par:par + 1], ps[:, 2, FE:2 * FE], ALU.mult, ALU.mult)\
                       .then_inc(sem("exp_h"), 1)

                def add_y(m, t, bank=6):
                    dve.wait_ge(sem("scattered"), 2 * m + (2 * M0 + t + 1))
                    if later(m, 1):
                        dve.wait_ge(sem("y_added"), 2 * m + (2 * M0 + t - 1))
                    dve.tensor_tensor(y_acc[:, t, :], ps[:, bank:bank + 2, :].rearrange("p b n -> p (b n)"), y_acc[:, t, :], ALU.add)\
                       .then_inc(sem("y_added"), 1)

                def y_low(m):
                    dve.wait_ge(sem("y_high"), m + (M0 + 1))
                    dve.tensor_tensor(y_lo[:, :], ps[:, 4:6, :].rearrange("p b n -> p (b n)"), y_hi[:, :], ALU.subtract)\
                       .then_inc(sem("y_split"), 1)

                def dve_step(m, u, build=True, add=True):
                    gate_h(m, u)
                    if build:
                        sel_build(m + 2, u)
                    if add:
                        add_y(m - 1, 0)
                        add_y(m - 1, 1)
                    y_low(m)

                sel_build(0, 0)
                sel_build(1, 1)
                dve.wait_ge(sem("place_all"), L + 1)
                dve.tensor_scalar(over_int, over_all, float(SLOTS), None, ALU.is_ge).then_inc(sem("over_flag"), 1)
                dve.wait_ge(sem("shared_added"), NT * (L + 1))
                dve_step(0, 0, add=False)
                dve_step(1, 1)
                with dve.Fori(1, PAIRS // 2 - 1) as i:
                    for u in range(2):
                        dve_step(2 * i + u, u)
                dve_step(PAIRS - 2, 0, build=False)
                dve.wait_ge(sem("over_flag"), L + 1)
                flag = dve.value_load(over_int[0:1, 0:1], min_val=0, max_val=1)
                dve_step(PAIRS - 1, 1, build=False)
                add_y(PAIRS - 1, 0)
                add_y(PAIRS - 1, 1, bank=2)
                dve.wait_ge(sem("y_added"), 2 * (M0 + PAIRS))

                with dve.If(flag > 0):
                    with dve.Fori(0, NE) as e:
                        dve.wait_ge(sem(f"over_silu{L}"), e + 1)
                        dve.tensor_tensor(h_all, h_silu_all, ps[:, 5, :], ALU.mult).then_inc(sem(f"over_h{L}"), 1)
                        dve.wait_ge(sem(f"over_down{L}"), e + 1)
                        for t in range(NT):
                            ins = dve.scalar_tensor_tensor(y_acc[:, t, :], ps[:, 2 * t:2 * t + 2, :].rearrange("p b n -> p (b n)"),
                                                           gates_over[:, t, bass.ds(e, 1)], y_acc[:, t, :], ALU.mult, ALU.add)
                        ins.then_inc(sem(f"over_added{L}"), 1)
                    dve.wait_ge(sem(f"over_added{L}"), NE)

                layer_norm(L, 2, lambda t, half: y_acc[:, t, half * PIECE:(half + 1) * PIECE])
                copy_T("xT_dve", tp)
                tp += NT

                for t in range(NT):
                    dve.wait_ge(sem(f"ple_sq{L}"), t + 1)
                    rsqrt(ple_ss[:, t:t + 1], 1.0 / D, RMS_EPS)
                    dve.wait_ge(sem("gb_loaded"), 32 * (3 * L + 3))
                    seq(dve.scalar_tensor_tensor(y_acc[:, t, :], ps[:, 4 + 2 * t:6 + 2 * t, :].rearrange("p b n -> p (b n)"),
                                                 rstd, gb_row[:, 0, :], ALU.mult, ALU.mult))
                    dve.engine_nop().then_inc(sem("gb_used"), 1)
                for t in range(NT):
                    dve.wait_ge(sem(f"ple_sig{L}"), t + 1)
                    seq(dve.tensor_tensor(y_acc[:, t, :], y_acc[:, t, :], roped[:, t, 0:D], ALU.mult))
                    seq(dve.tensor_tensor(x_tok[:, t, :], x_tok[:, t, :], y_acc[:, t, :], ALU.add))
                    dve.engine_nop().then_inc(sem(f"ple_out{L}"), 1)


_INS = ['x', 'p', 'ev_w_in', 'ev_b_gate', 'ev_cmp_pos_k', 'ev_cmp_w1_k', 'ev_cmp_w2_k', 'ev_cmp_pos_v',
        'ev_cmp_w1_v', 'ev_cmp_w2_v', 'ev_w_o', 'od_w_in', 'od_b_f', 'od_w_o', 'ln1_g', 'ln1_b', 'ln2_g', 'ln2_b',
        'router_w', 'router_bias', 'exp_w1', 'exp_w3', 'exp_w2', 'sh_w1', 'sh_w3', 'sh_w2', 'ple_w_gate',
        'ple_w_proj', 'ple_norm_g']


def kernel(**inputs):
    import numpy as _np
    import concourse.bacc as _bacc
    from concourse import mybir as _mybir
    from concourse.bass_utils import run_bass_kernel_spmd as _run

    nc = _bacc.Bacc("TRN2", target_bir_lowering=False, num_devices=1)
    arrays, aps = {}, {}
    for name in _INS + ["const"]:
        v = constant_table() if name == "const" else _np.ascontiguousarray(inputs[name])
        arrays[f"in_{name}_dram"] = v
        aps[name] = nc.dram_tensor(f"in_{name}_dram", v.shape, _mybir.dt.from_np(v.dtype), kind="ExternalInput").ap()
    out = nc.dram_tensor("out_0_dram", (1, SEQ, D), _mybir.dt.float32, kind="ExternalOutput").ap()
    build_trunk(nc, aps, out)
    r = _run(nc, [arrays], core_ids=[0])
    return r.results[0]["out_0_dram"]
```
